# Optimizing a Trainium2 kernel written in Bass

```python
import math
import jax, jax.numpy as jnp
from jax import lax
import numpy as np

D_MODEL = 1024
BATCH = 1
SEQ = 1024
DEPTH = 1

CHUNK = 64
Q_BLOCK = 128
HEAD_DIM = 64
NORM_EPS = 1e-6

DA_HEADS = 4
DA_QK_WIDTH = DA_HEADS * 2 * HEAD_DIM
DA_V_WIDTH = DA_HEADS * 2 * HEAD_DIM

SW_HEADS = 8
SW_KV_HEADS = 2
SW_WINDOW = 128
SW_PREV_CHUNKS = SW_WINDOW // CHUNK - 1
SW_Q_WIDTH = SW_HEADS * HEAD_DIM
SW_KV_WIDTH = SW_KV_HEADS * HEAD_DIM

SSM_INNER = D_MODEL
SSM_HEAD_DIM = 64
SSM_HEADS = SSM_INNER // SSM_HEAD_DIM
SSM_GROUPS = 2
SSM_STATE = 128
SSM_CONV = 4
SSM_CONV_DIM = SSM_INNER + 2 * SSM_GROUPS * SSM_STATE

MLP_HIDDEN = 4 * D_MODEL
N_BRANCHES = 3

IN_SPLITS = (DA_QK_WIDTH, DA_QK_WIDTH, DA_V_WIDTH,
             SW_Q_WIDTH, SW_KV_WIDTH, SW_KV_WIDTH,
             SSM_INNER, SSM_CONV_DIM, SSM_HEADS,
             N_BRANCHES * D_MODEL)
D_IN_PROJ = sum(IN_SPLITS)
BRANCH_WIDTHS = (DA_V_WIDTH, SW_Q_WIDTH, SSM_INNER)
BRANCH_IN = sum(BRANCH_WIDTHS)

N_ALIBI_HEADS = SW_HEADS + DA_HEADS
ALIBI_SLOPES = np.exp2(-8.0 * np.arange(1, N_ALIBI_HEADS + 1) / N_ALIBI_HEADS).astype(np.float32)
SW_SLOPES = ALIBI_SLOPES[:SW_HEADS]
DA_SLOPES = ALIBI_SLOPES[SW_HEADS:]

kernel_name = "hybrid_chunk_causal_encoder_block"

def _split(x, sizes):
    return jnp.split(x, [int(s) for s in np.cumsum(sizes)[:-1]], axis=-1)

def _rms_normalize(x):
    xf = x.astype(jnp.float32)
    return xf * lax.rsqrt(jnp.mean(xf * xf, axis=-1, keepdims=True) + NORM_EPS)

def rms_norm(x, g):
    return (_rms_normalize(x) * g.astype(jnp.float32)).astype(x.dtype)

def differential_attention(q, k, v, lam, subln_g, lam_init):
    b, L, _ = q.shape
    q = q.reshape(b, L, DA_HEADS, 2, HEAD_DIM)
    k = k.reshape(b, L, DA_HEADS, 2, HEAD_DIM)
    v = v.reshape(b, L, DA_HEADS, 2 * HEAD_DIM)
    scale = HEAD_DIM ** -0.5
    kpos = jnp.arange(L)
    kchunk = kpos // CHUNK
    slopes = jnp.asarray(DA_SLOPES)[:, None, None]

    def block(qi):
        start = qi * Q_BLOCK
        qb = lax.dynamic_slice_in_dim(q, start, Q_BLOCK, axis=1)
        qpos = start + jnp.arange(Q_BLOCK)
        s = jnp.einsum("bqhmd,bkhmd->bmhqk", qb, k).astype(jnp.float32) * scale
        dist = jnp.abs(qpos[:, None] - kpos[None, :]).astype(jnp.float32)
        allowed = kchunk[None, :] <= (qpos // CHUNK)[:, None]
        s = jnp.where(allowed, s - slopes * dist, -jnp.inf)
        p = jax.nn.softmax(s, axis=-1)
        w = p[:, 0] - lam * p[:, 1]
        return jnp.einsum("bhqk,bkhe->bqhe", w.astype(v.dtype), v)

    out = lax.map(block, jnp.arange(L // Q_BLOCK))
    out = out.transpose(1, 0, 2, 3, 4).reshape(b, L, DA_HEADS, 2 * HEAD_DIM)
    out = rms_norm(out, subln_g) * (1.0 - lam_init)
    return out.reshape(b, L, DA_V_WIDTH)

def sliding_window_attention(q, k, v, sinks):
    b, L, _ = q.shape
    nC = L // CHUNK
    g, r, P = SW_KV_HEADS, SW_HEADS // SW_KV_HEADS, SW_PREV_CHUNKS
    S = (P + 1) * CHUNK
    q = q.reshape(b, nC, CHUNK, g, r, HEAD_DIM)
    k = k.reshape(b, nC, CHUNK, g, HEAD_DIM)
    v = v.reshape(b, nC, CHUNK, g, HEAD_DIM)
    pad = ((0, 0), (P, 0), (0, 0), (0, 0), (0, 0))
    kp, vp = jnp.pad(k, pad), jnp.pad(v, pad)
    kb = jnp.concatenate([kp[:, o:o + nC] for o in range(P + 1)], axis=2)
    vb = jnp.concatenate([vp[:, o:o + nC] for o in range(P + 1)], axis=2)
    s = jnp.einsum("bcqgrd,bcsgd->bcgrqs", q, kb).astype(jnp.float32) * (HEAD_DIM ** -0.5)
    i = jnp.arange(CHUNK)
    j = jnp.arange(S)
    rel = (i[:, None] + P * CHUNK - j[None, :]).astype(jnp.float32)
    bias = -jnp.asarray(SW_SLOPES).reshape(g, r)[:, :, None, None] * jnp.abs(rel)
    key_chunk = jnp.arange(nC)[:, None] - P + (j // CHUNK)[None, :]
    valid = (key_chunk >= 0)[None, :, None, None, None, :]
    s = jnp.where(valid, s + bias, -jnp.inf)
    sink = jnp.broadcast_to(sinks.astype(jnp.float32).reshape(1, 1, g, r, 1, 1), s.shape[:-1] + (1,))
    p = jax.nn.softmax(jnp.concatenate([s, sink], axis=-1), axis=-1)[..., :-1]
    o = jnp.einsum("bcgrqs,bcsgd->bcqgrd", p.astype(vb.dtype), vb)
    return o.reshape(b, L, SW_Q_WIDTH)

def _segsum(a):
    T = a.shape[-1]
    cs = jnp.cumsum(a, axis=-1)
    d = cs[..., :, None] - cs[..., None, :]
    return jnp.where(jnp.tril(jnp.ones((T, T), dtype=bool)), d, -jnp.inf)

def ssd_scan(x, dt, A, Bm, Cm, D):
    b, L, H, P = x.shape
    nC = L // CHUNK
    G, R, N = SSM_GROUPS, SSM_HEADS // SSM_GROUPS, SSM_STATE
    xd = (x * dt[..., None]).reshape(b, nC, CHUNK, G, R, P)
    a = (dt * A).reshape(b, nC, CHUNK, G, R).transpose(0, 3, 4, 1, 2)
    Bc = Bm.reshape(b, nC, CHUNK, G, N)
    Cc = Cm.reshape(b, nC, CHUNK, G, N)
    a_cs = jnp.cumsum(a, axis=-1)
    Lmat = jnp.exp(_segsum(a))
    y_diag = jnp.einsum("bclgn,bcsgn,bgrcls,bcsgrp->bclgrp", Cc, Bc, Lmat, xd)
    decay_states = jnp.exp(a_cs[..., -1:] - a_cs)
    states = jnp.einsum("bclgn,bgrcl,bclgrp->bcgrpn", Bc, decay_states, xd)
    chunk_decay = jnp.exp(a_cs[..., -1])

    def step(h, inp):
        st, dec = inp
        return h * dec[..., None, None] + st, h

    h0 = jnp.zeros_like(states[:, 0])
    _, prev = lax.scan(step, h0, (jnp.moveaxis(states, 1, 0), jnp.moveaxis(chunk_decay, -1, 0)))
    prev = jnp.moveaxis(prev, 0, 1)
    y_off = jnp.einsum("bclgn,bcgrpn,bgrcl->bclgrp", Cc, prev, jnp.exp(a_cs))
    y = (y_diag + y_off).reshape(b, L, H, P)
    return y + x * D.astype(jnp.float32)[:, None]

def mamba2_ssd(z, xbc, dt_raw, conv_w, conv_b, dt_bias, A_log, D, norm_g):
    b, L, _ = z.shape
    xbc = lax.conv_general_dilated(
        xbc, conv_w.astype(xbc.dtype)[:, None, :], window_strides=(1,),
        padding=[(SSM_CONV - 1, 0)], dimension_numbers=("NWC", "WIO", "NWC"),
        feature_group_count=SSM_CONV_DIM) + conv_b
    xbc = jax.nn.silu(xbc)
    xs, Bm, Cm = _split(xbc, (SSM_INNER, SSM_GROUPS * SSM_STATE, SSM_GROUPS * SSM_STATE))
    dt = jax.nn.softplus(dt_raw.astype(jnp.float32) + dt_bias.astype(jnp.float32))
    A = -jnp.exp(A_log.astype(jnp.float32))
    y = ssd_scan(xs.reshape(b, L, SSM_HEADS, SSM_HEAD_DIM), dt, A,
                 Bm.reshape(b, L, SSM_GROUPS, SSM_STATE), Cm.reshape(b, L, SSM_GROUPS, SSM_STATE), D)
    y = y.reshape(b, L, SSM_INNER) * jax.nn.silu(z.astype(jnp.float32))
    y = _rms_normalize(y.reshape(b, L, SSM_GROUPS, SSM_INNER // SSM_GROUPS)).reshape(b, L, SSM_INNER)
    return (y * norm_g.astype(jnp.float32)).astype(z.dtype)

def setup_inputs(seed: int = 0) -> dict:
    key = jax.random.key(seed)
    ks = jax.random.split(key, 24)

    def nrm(k, shape, scale):
        return jax.random.normal(k, shape, jnp.float32) * scale

    u = jax.random.uniform(ks[14], (DEPTH, SSM_HEADS), jnp.float32)
    dt0 = jnp.exp(u * (math.log(0.1) - math.log(0.001)) + math.log(0.001))
    branch_scale = jnp.asarray(np.concatenate(
        [np.full((w,), w ** -0.5, np.float32) for w in BRANCH_WIDTHS]))[:, None]
    return {
        "x": nrm(ks[0], (BATCH, SEQ, D_MODEL), 1.0),
        "c": nrm(ks[1], (BATCH, D_MODEL), 1.0),
        "ada_w": nrm(ks[2], (DEPTH, D_MODEL, 6 * D_MODEL), 0.5 * D_MODEL ** -0.5),
        "ada_b": nrm(ks[3], (DEPTH, 6 * D_MODEL), 0.02),
        "norm_mix_g": 1.0 + nrm(ks[4], (DEPTH, D_MODEL), 0.02),
        "w_in": nrm(ks[5], (DEPTH, D_MODEL, D_IN_PROJ), D_MODEL ** -0.5),
        "da_lambda_q1": nrm(ks[6], (DEPTH, HEAD_DIM), 0.1),
        "da_lambda_k1": nrm(ks[7], (DEPTH, HEAD_DIM), 0.1),
        "da_lambda_q2": nrm(ks[8], (DEPTH, HEAD_DIM), 0.1),
        "da_lambda_k2": nrm(ks[9], (DEPTH, HEAD_DIM), 0.1),
        "da_subln_g": 1.0 + nrm(ks[10], (DEPTH, 2 * HEAD_DIM), 0.02),
        "sw_sinks": nrm(ks[11], (DEPTH, SW_HEADS), 1.0),
        "ssm_conv_w": nrm(ks[12], (DEPTH, SSM_CONV, SSM_CONV_DIM), SSM_CONV ** -0.5),
        "ssm_conv_b": nrm(ks[13], (DEPTH, SSM_CONV_DIM), 0.02),
        "ssm_dt_bias": dt0 + jnp.log(-jnp.expm1(-dt0)),
        "ssm_A_log": jnp.log(jax.random.uniform(ks[15], (DEPTH, SSM_HEADS), jnp.float32, 1.0, 16.0)),
        "ssm_D": 1.0 + nrm(ks[16], (DEPTH, SSM_HEADS), 0.1),
        "ssm_norm_g": 1.0 + nrm(ks[17], (DEPTH, SSM_INNER), 0.02),
        "w_branch": nrm(ks[18], (DEPTH, BRANCH_IN, D_MODEL), 1.0) * branch_scale,
        "w_out": nrm(ks[19], (DEPTH, D_MODEL, D_MODEL), D_MODEL ** -0.5),
        "norm_mlp_g": 1.0 + nrm(ks[20], (DEPTH, D_MODEL), 0.02),
        "w_mlp1": nrm(ks[21], (DEPTH, D_MODEL, MLP_HIDDEN), D_MODEL ** -0.5),
        "w_mlp2": nrm(ks[22], (DEPTH, MLP_HIDDEN, D_MODEL), MLP_HIDDEN ** -0.5),
        "final_norm_g": 1.0 + nrm(ks[23], (D_MODEL,), 0.02),
    }

def reference(x, c, ada_w, ada_b, norm_mix_g, w_in, da_lambda_q1, da_lambda_k1, da_lambda_q2,
              da_lambda_k2, da_subln_g, sw_sinks, ssm_conv_w, ssm_conv_b, ssm_dt_bias, ssm_A_log,
              ssm_D, ssm_norm_g, w_branch, w_out, norm_mlp_g, w_mlp1, w_mlp2, final_norm_g):
    for l in range(DEPTH):
        mod = (c @ ada_w[l] + ada_b[l])[:, None, :]
        shift_mix, scale_mix, gate_mix, shift_mlp, scale_mlp, gate_mlp = jnp.split(mod, 6, axis=-1)

        h = rms_norm(x, norm_mix_g[l]) * (1.0 + scale_mix) + shift_mix
        (da_q, da_k, da_v, sw_q, sw_k, sw_v,
         ssm_z, ssm_xbc, ssm_dt, gate_logits) = _split(h @ w_in[l], IN_SPLITS)

        lam_init = 0.8 - 0.6 * math.exp(-0.3 * l)
        lam = (jnp.exp(jnp.sum(da_lambda_q1[l].astype(jnp.float32) * da_lambda_k1[l].astype(jnp.float32)))
               - jnp.exp(jnp.sum(da_lambda_q2[l].astype(jnp.float32) * da_lambda_k2[l].astype(jnp.float32)))
               + lam_init)
        o_a = differential_attention(da_q, da_k, da_v, lam, da_subln_g[l], lam_init)
        o_b = sliding_window_attention(sw_q, sw_k, sw_v, sw_sinks[l])
        o_c = mamba2_ssd(ssm_z, ssm_xbc, ssm_dt, ssm_conv_w[l], ssm_conv_b[l], ssm_dt_bias[l],
                         ssm_A_log[l], ssm_D[l], ssm_norm_g[l])

        w_a, w_b, w_c = jnp.split(w_branch[l], [DA_V_WIDTH, DA_V_WIDTH + SW_Q_WIDTH], axis=0)
        g_a, g_b, g_c = jnp.split(jax.nn.sigmoid(gate_logits), N_BRANCHES, axis=-1)
        merged = g_a * (o_a @ w_a) + g_b * (o_b @ w_b) + g_c * (o_c @ w_c)
        x = x + gate_mix * (merged @ w_out[l])

        h = rms_norm(x, norm_mlp_g[l]) * (1.0 + scale_mlp) + shift_mlp
        x = x + gate_mlp * (jnp.square(jax.nn.relu(h @ w_mlp1[l])) @ w_mlp2[l])
    return rms_norm(x, final_norm_g)


_drawn_inputs = setup_inputs


def setup_inputs(seed=0):
    import zlib

    import numpy as np

    out = dict(_drawn_inputs(seed))
    spreads = {}
    factors = {'norm_mix_g': 6.144,
     'da_lambda_q1': 64.0,
     'da_lambda_k1': 53.232,
     'da_lambda_q2': 4.614,
     'da_lambda_k2': 200.0,
     'da_subln_g': 127.057,
     'sw_sinks': 3.877,
     'ssm_conv_b': 24.579,
     'ssm_D': 200.0,
     'ssm_norm_g': 123.057,
     'norm_mlp_g': 14.212,
     'final_norm_g': 23.271}
    for name, (base, spread) in spreads.items():
        noise = np.random.default_rng([zlib.crc32(name.encode()), seed]).standard_normal(out[name].shape)
        drawn = base * np.exp(spread * noise) if base else spread * noise
        out[name] = __import__('jax').numpy.asarray(drawn.astype(out[name].dtype))
    for name, factor in factors.items():
        out[name] = (out[name] * factor).astype(out[name].dtype)
    return out
```

```python
from contextlib import ExitStack, contextmanager

import numpy as np
import concourse.bass as bass
from concourse import mybir

F32 = mybir.dt.float32
F32R = mybir.dt.float32r
ALU = mybir.AluOpType
ACT = mybir.ActivationFunctionType

P = 128
T = 1024
D = 1024
KT = D // P
NT = T // P
HALF = 512
EPS = 1e-6
DA_HEADS = 4
SW_PAIRS = 4
GROUPS = 2
GH = 8
HD = 64
HEADS = GROUPS * GH
LAM_INIT = 0.8 - 0.6 * 1.0
DA_OUT = 1.0 - LAM_INIT
SCALE = HD ** -0.5
NEG = -1.0e30

N_DA = 0
N_SW = N_DA + 3 * DA_HEADS
N_AB = N_SW + 2 + SW_PAIRS
N_DT = N_AB + 3 * KT
N_SSM = N_DT + 1
N_C = N_SSM + 10 * GROUPS
N_OUT = N_C + 2 * KT
N_MLP = N_OUT + KT
QUARTERS = 4
N_ALL = N_MLP + 16 * QUARTERS

C_GMIX, C_GMLP, C_GFIN, C_GSSM = 0, 8, 16, 24
C_ADAB = 32
C_CONV = C_ADAB + 48
C_D = C_CONV + 60
C_SUBLN = C_D + 8
C_DTB = C_SUBLN + 1
C_ALOG = C_DTB + HEADS
C_SINK = C_ALOG + HEADS
C_ALL = C_SINK + 8
K_ID, K_TRI, K_ALL = 0, P, 2 * P

PIECES = [(i, half) for i in range(NT) for half in range(1 + i // 4)]
NP_ = len(PIECES)


class Steps:

    def __init__(self, eng, sem):
        self.eng, self.sem, self.base, self.k = eng, sem, 0, 0

    def mark(self, ins):
        ins.then_inc(self.sem, 1)
        self.k += 1

    def settle(self):
        self.eng.wait_ge(self.sem, self.base + self.k)

    @contextmanager
    def loop(self, i, per, trips):
        old, start = self.base, self.k
        self.base = old + i * per
        yield
        assert self.k - start == per, (self.k - start, per)
        self.base, self.k = old, start + per * trips


def flat(ap):
    return ap.rearrange("p a b -> p (a b)")


def build(nc, x_in, c_in, ada_in, w_in, par_in, con_in, da_tab, sw_tab, lam_v, out):
    with ExitStack() as ctx:
        def sb(name, shape, dt=F32):
            return ctx.enter_context(nc.sbuf_tensor(name, shape, dt))

        def sem(name):
            return ctx.enter_context(nc.semaphore(name))

        h_hi = sb("h_hi", [P, KT, T], F32R)
        h_lo = sb("h_lo", [P, KT, T], F32R)
        u_hi = sb("u_hi", [P, KT, T], F32R)
        u_lo = sb("u_lo", [P, KT, T], F32R)
        w_hi = [sb(f"w_hi{i}", [P, KT, P], F32R) for i in range(2)]
        w_lo = [sb(f"w_lo{i}", [P, KT, P], F32R) for i in range(2)]
        raw = sb("raw", [P, 2, KT * P])
        tile = sb("tile", [P, 13, T])
        con = sb("con", [P, K_ALL])
        par = sb("par", [P, C_ALL])
        c_sb = sb("c_sb", [P, KT])
        ones = sb("ones", [P, 1])
        eps = sb("eps", [P, 1])
        mod = sb("mod", [P, 48])
        a_mix = sb("a_mix", [P, KT])
        a_mlp = sb("a_mlp", [P, KT])
        a_da = sb("a_da", [P, 1])
        rms = sb("rms", [P, 6, KT])
        rstd = sb("rstd", [P, KT])
        lam = sb("lam", [P, 8])
        mx = sb("mx", [P, 4])
        mxp = sb("mxp", [P, 4])
        sm = sb("sm", [P, 4])
        rc = sb("rc", [P, 4])
        swm = sb("swm", [P, 16])
        swn = sb("swn", [P, 16])
        sws = sb("sws", [P, 16])
        swe = sb("swe", [P, 16])
        swd = sb("swd", [P, 16])
        swr = sb("swr", [P, 16])
        exp_a = sb("exp_a", [P, HEADS])
        gpar = sb("gpar", [P, 34])

        dtm = tile[:, 12, :].rearrange("p (n x) -> p n x", n=8)
        id_ = con[:, K_ID:K_ID + P]
        tri = con[:, K_TRI:K_TRI + P]

        acc = [ctx.enter_context(nc.psum_tensor(f"acc{i}", [P, T], F32)) for i in range(2)]
        wk = [ctx.enter_context(nc.psum_tensor(f"wk{i}", [P, T], F32)) for i in range(2)]
        bank = [wk[0][:, 0:HALF], wk[0][:, HALF:T], wk[1][:, 0:HALF], wk[1][:, HALF:T]]

        sw_bias = tile[:, 11, :]

        merged_d = nc.dram_tensor("merged_d", [KT, P, T], F32, kind="Internal").ap()
        cs_d = nc.dram_tensor("cs_d", [P, P], F32, kind="Internal").ap()

        S = {}
        for name in """par_in lam_in con_in c_in w_in0 w_in1 x_in0 x_in1 x_in2 x_in3 ada_in0 ada_in1
            split_hi split_ready block_done acc_free0 acc_free1
            mod_done sq_ready sq_used ms_ready root_ready rstd_ready bcast_ready h_scaled h_hi_ready h_ready
            dve_own gates_free relu_free da_tab_in
            qkv_ready v_turned v_tok scored biased negmax exped weighted turned turned_sb pv_done o_copied
            da_clipped da_sq da_ms da_root da_rstd da_bcast da_scaled da_hi u_ready lam_dots lam_exps
            sw_tab_in sw_qkv sw_vt sw_vtok sw_scored sw_biased sw_negmax sw_exped sw_weighted sw_turned sw_turned_sb
            sw_out sw_hi sw_used
            gate_ready ab_free ab_ready merged_out merged_saved
            dt_copied dt_turned dt_abs dt_exp dt_da cs_ready cs_copied cs_saved dt_diff dt_decays
            conv_first conv_done conv_silu csb_in diff_ready relu_ready l_ready e_ready x_turned g_ready btok_ready
            g_masked xd_ready m_ready s_ready y_ready y_taken state_ready
            z_silu z_used y_gated ssm_sq ssm_ms ssm_root ssm_rstd ssm_bcast ssm_scaled ssm_hi y_split
            c_gate c_free merged_in0 merged_in1 merged_all merged_hi merged_ready
            x2_in x1_ready x1_sq x1_sum n2_ms n2_root n2_rstd n2_bcast n2_scaled n2_hi n2_ready
            hid_relu hid_sq hid_hi hid_ready x2_ready f_sq f_sum f_ms f_root f_rstd f_bcast f_ready out_saved
            mod_rest ada_freed""".split():
            S[name] = sem(name)
        w_in_s = [S["w_in0"], S["w_in1"]]
        x_in_s = [S["x_in0"], S["x_in1"], S["x_in2"], S["x_in3"]]
        ada_s = [S["ada_in0"], S["ada_in1"]]
        acc_free = [S["acc_free0"], S["acc_free1"]]
        merged_s = [S["merged_in0"], S["merged_in1"]]

        xres = [tile[:, k, :] for k in range(KT)]
        block = ctx.enter_context(nc.Block())

        @block.sync
        def _(sp):
            sp.dma_start(par[:], par_in).then_inc(S["par_in"], 16)
            sp.dma_start(tile[:, 11, 0:4 * HD], lam_v).then_inc(S["lam_in"], 16)
            sp.dma_start(c_sb[:], c_in).then_inc(S["c_in"], 16)
            for q in range(4):
                sp.dma_start(tile[:, 2 * q:2 * q + 2, :],
                             x_in[2 * q:2 * q + 2].rearrange("k p t -> p k t")).then_inc(x_in_s[q], 16)
                if q == 0:
                    sp.dma_start(con[:], con_in).then_inc(S["con_in"], 16)
            for n in range(2):
                sp.dma_start(raw[:, n], w_in[n]).then_inc(w_in_s[n], 16)
            for b in range(16):
                if b >= 2:
                    sp.wait_ge(S["mod_done"], b - 1)
                sp.dma_start(tile[:, 8 + b % 2, :], ada_in[b]).then_inc(ada_s[b % 2], 16)
            with sp.Fori(0, (N_ALL - 3) // 2) as i:
                for b in range(2):
                    sp.wait_ge(S["split_ready"], i * 2 + b + 1)
                    sp.dma_start(raw[:, b], w_in[bass.ds(i * 2 + 2 + b, 1)].rearrange("a p c -> (a p) c")
                                 ).then_inc(w_in_s[b], 16)
            sp.wait_ge(S["split_ready"], N_ALL - 2)
            sp.dma_start(raw[:, 0], w_in[N_ALL - 1]).then_inc(w_in_s[0], 16)

        @block.gpsimd
        def _(pool):
            def split(b, n, trip, first):
                pool.wait_ge(w_in_s[b], trip * 16 + 16)
                if not first:
                    pool.wait_ge(S["block_done"], n - 1)
                pool.nop(nofuse=True)
                pool.tensor_scalar(flat(w_hi[b][:]), raw[:, b], 1.0, 1.0, ALU.mult, ALU.mult).then_inc(S["split_hi"], 1)
                pool.wait_ge(S["split_hi"], n + 1)
                pool.tensor_tensor(flat(w_lo[b][:]), raw[:, b], flat(w_hi[b][:].bitcast(F32)),
                                   ALU.subtract).then_inc(S["split_ready"], 1)

            split(0, 0, 0, True)
            split(1, 1, 0, True)
            with pool.Fori(0, (N_ALL - 3) // 2) as i:
                for b in range(2):
                    split(b, i * 2 + 2 + b, i + 1, False)
            split(0, N_ALL - 1, (N_ALL - 1) // 2, False)

        @block.tensor
        def _(pe):
            def terms(b, k, rhs_hi, rhs_lo, kr, psum, first, last):
                for t, (w, r) in enumerate(((w_hi, rhs_hi), (w_hi, rhs_lo), (w_lo, rhs_hi))):
                    for half in range(2):
                        cols = slice(half * HALF, (half + 1) * HALF)
                        mm = pe.matmul(psum[:, cols], w[b][:, k, :], r[:, kr, cols],
                                       start=first and t == 0, stop=last and t == 2)
                return mm

            def dense(b, pair, rhs_hi, rhs_lo, moving=None):
                pe.wait_ge(S["split_ready"], pair * 2 + b + 1)
                pe.wait_ge(acc_free[b], pair + 1)
                for k in range(KT):
                    if moving is not None:
                        pe.wait_ge(moving[0], moving[1] + k + 1)
                    mm = terms(b, k, rhs_hi, rhs_lo, k, acc[b], k == 0, k == KT - 1)
                mm.then_inc(S["block_done"], 1)

            def row_means(total, signal, at=0):
                for c in range(NT):
                    mm = pe.matmul(bank[3][:, at + c:at + c + 1], total[:, c * P:(c + 1) * P], ones[:, 0:1],
                                   start=True, stop=True)
                mm.then_inc(signal, 1)

            def broadcast(signal):
                for c in range(NT):
                    mm = pe.matmul(wk[0][:, c * P:(c + 1) * P], rstd[:, c:c + 1].to_broadcast([P, P]), id_,
                                   start=True, stop=True)
                mm.then_inc(signal, 1)

            def modulation(b, slot, trip):
                pe.wait_ge(ada_s[slot], trip * 16 + 16)
                for k in range(KT):
                    mm = pe.matmul(bank[2][:, b:b + 1], tile[:, 8 + slot, k * P:(k + 1) * P], c_sb[:, k:k + 1],
                                   start=k == 0, stop=k == KT - 1)
                mm.then_inc(S["mod_done"], 1)

            pe.wait_ge(S["c_in"], 16)
            for b in range(16):
                modulation(b, b % 2, b // 2)
            pe.wait_ge(S["sq_used"], KT)
            row_means(tile[:, 11, :], S["ms_ready"])
            pe.wait_ge(S["rstd_ready"], 1)
            pe.wait_ge(S["con_in"], 16)
            broadcast(S["bcast_ready"])

            def da_head(head):
                pe.wait_ge(S["qkv_ready"], head * 3 + 1)
                for j in range(NT):
                    mm = pe.transpose(wk[0][:, j * P:(j + 1) * P], tile[:, 2, j * P:(j + 1) * P], id_)
                mm.then_inc(S["v_turned"], 1)
                pe.wait_ge(S["v_tok"], head * 2 + 2)
                pe.wait_ge(S["qkv_ready"], head * 3 + 3)

                def scores(i, m):
                    if i or m:
                        pe.wait_ge(S["biased"], head * 16 + 2 * i + m)
                    rows = slice(m * HD, (m + 1) * HD)
                    for lo in range(0, (i + 1) * P, HALF):
                        hi = min(lo + HALF, (i + 1) * P)
                        mm = pe.matmul(wk[0][:, lo:hi], tile[rows, 1, i * P:(i + 1) * P], tile[rows, 0, lo:hi],
                                       start=True, stop=True)
                    mm.then_inc(S["scored"], 1)

                def turn(i, half):
                    n = PIECES.index((i, half))
                    pe.wait_ge(S["weighted"], head * 8 + i + 1)
                    if n:
                        pe.wait_ge(S["turned_sb"], head * NP_ + n)
                    for j in range(4 * half, min(4 * half + 4, i + 1)):
                        mm = pe.transpose(bank[2][:, (j % 4) * P:(j % 4 + 1) * P], tile[:, 12, j * P:(j + 1) * P], id_)
                    mm.then_inc(S["turned"], 1)

                def attend(i, half):
                    n = PIECES.index((i, half))
                    pe.wait_ge(S["turned_sb"], head * NP_ + n + 1)
                    if i == 4 and half == 0:
                        pe.wait_ge(S["o_copied"], head * 2 + 1)
                    for j in range(4 * half, min(4 * half + 4, i + 1)):
                        at = (n % 2) * HALF + (j % 4) * P
                        mm = pe.matmul(bank[3][:, (i % 4) * P:(i % 4 + 1) * P], tile[:, 3, j * P:(j + 1) * P],
                                       tile[:, 9, at:at + P], start=j == 0, stop=j == i)
                    mm.then_inc(S["pv_done"], 1)

                for i in range(NT):
                    scores(i, 0)
                    scores(i, 1)
                    if i:
                        for half in range(1 + (i - 1) // 4):
                            turn(i - 1, half)
                            attend(i - 1, half)
                for half in range(2):
                    turn(NT - 1, half)
                    attend(NT - 1, half)
                pe.wait_ge(S["o_copied"], head * 2 + 2)
                pe.wait_ge(S["da_sq"], head * 2 + 2)
                row_means(tile[:, 5, :], S["da_ms"])
                row_means(tile[:, 8, :], S["da_ms"], NT)
                pe.wait_ge(S["da_rstd"], head + 1)
                broadcast(S["da_bcast"])

            with pe.Fori(0, DA_HEADS // 2) as t:
                for s in range(2):
                    for q in range(3):
                        n = 3 * s + q
                        dense(n % 2, t * 3 + n // 2, h_hi, h_lo, (S["h_ready"], 0) if n == 0 else None)
                    da_head(t * 2 + s)

            pe.wait_ge(S["u_ready"], 4)
            dense(0, N_SW // 2, h_hi, h_lo)
            dense(1, N_SW // 2, h_hi, h_lo)
            pe.wait_ge(S["sw_qkv"], 1)
            for j in range(NT):
                mm = pe.transpose(wk[0][:, j * P:(j + 1) * P], tile[:, 2, j * P:(j + 1) * P], id_)
            mm.then_inc(S["sw_vt"], 1)
            pe.wait_ge(S["sw_vtok"], 1)

            def sw_pair(j):
                pe.wait_ge(S["sw_qkv"], j + 3)
                for i in range(NT):
                    if i >= 2:
                        pe.wait_ge(S["sw_biased"], j * NT + i - 1)
                    lo = max(i - 1, 0) * P
                    for g in range(2):
                        rows = slice(g * HD, (g + 1) * HD)
                        w = (i + 1) * P - lo
                        mm = pe.matmul(bank[2 * (i % 2) + g][:, 256 - w:256], tile[rows, 1, i * P:(i + 1) * P],
                                       tile[rows, 0, lo:lo + w], start=True, stop=True)
                    mm.then_inc(S["sw_scored"], 1)
                pe.wait_ge(S["sw_biased"], j * NT + NT)

                def attend(i):
                    pe.wait_ge(S["sw_turned_sb"], j * NT + i + 1)
                    for g in range(2):
                        rows = slice(g * HD, (g + 1) * HD)
                        for kb in range(0 if i else 1, 2):
                            jj = i - 1 + kb
                            at = (i % 2) * HALF + (g * 2 + kb) * P
                            mm = pe.matmul(wk[0][rows, i * P:(i + 1) * P], tile[:, 3, jj * P + g * HD:jj * P + (g + 1) * HD],
                                           tile[:, 9, at:at + P], start=kb == (0 if i else 1), stop=kb == 1)
                    mm.then_inc(S["sw_out"], 1)

                for i in range(NT):
                    pe.wait_ge(S["sw_weighted"], j * NT + i + 1)
                    if i >= 2:
                        pe.wait_ge(S["sw_turned_sb"], j * NT + i - 1)
                    for g in range(2):
                        for kb in range(0 if i else 1, 2):
                            at = (g * 2 + kb) * P
                            src = i * 256 + kb * P
                            mm = pe.transpose(bank[2 + i % 2][:, at:at + P],
                                              tile[:, 5 + 2 * g + src // T, src % T:src % T + P], id_)
                    mm.then_inc(S["sw_turned"], 1)
                    if i:
                        attend(i - 1)
                attend(NT - 1)

            with pe.Fori(0, SW_PAIRS // 2) as t:
                for s in range(2):
                    dense(s, t + (N_SW + 2) // 2, h_hi, h_lo)
                    sw_pair(t * 2 + s)
                    pe.wait_ge(S["u_ready"], t * 2 + s + 5)

            with pe.Fori(0, KT // 2) as t:
                for s in range(2):
                    for q in range(3):
                        n = 3 * s + q
                        pair = t * 3 + N_AB // 2 + n // 2
                        if q < 2:
                            dense(n % 2, pair, h_hi, h_lo)
                        else:
                            pe.wait_ge(S["split_ready"], pair * 2 + n % 2 + 1)
                            pe.wait_ge(S["ab_free"], t * 2 + s + 1)
                            for k in range(KT):
                                mm = terms(n % 2, k, u_hi, u_lo, k, wk[0] if k < 4 else acc[n % 2],
                                           k % 4 == 0, k % 4 == 3)
                                if k == 3:
                                    pe.wait_ge(acc_free[n % 2], pair + 1)
                            mm.then_inc(S["block_done"], 1)
                    for q in range(4):
                        pe.wait_ge(ada_s[q % 2], t * 64 + (8 + 2 * s + q // 2) * 16 + 16)
                        for k in range(KT):
                            mm = pe.matmul(bank[2][:, bass.ds(t * 8 + (16 + 4 * s + q), 1)],
                                           tile[:, 8 + q % 2, k * P:(k + 1) * P], c_sb[:, k:k + 1],
                                           start=k == 0, stop=k == KT - 1)
                        mm.then_inc(S["mod_done"], 1)

            dense(0, N_DT // 2, h_hi, h_lo)
            pe.wait_ge(S["dt_copied"], 1)
            pe.wait_ge(S["mod_rest"], 1)
            pe.wait_ge(S["merged_out"], KT)
            for c in range(NT):
                mm = pe.transpose(bank[0][:, c * HEADS:(c + 1) * HEADS], tile[0:HEADS, 0, c * P:(c + 1) * P], id_[0:HEADS, 0:HEADS])
            mm.then_inc(S["dt_turned"], 1)
            pe.wait_ge(S["dt_da"], 1)
            a_tok = dtm[:, 0, :]
            pe.matmul(bank[1][:, 0:P], a_tok, tri, start=True, stop=True)
            pe.matmul(bank[1][:, P:2 * P], tri, a_tok, start=True, stop=True)
            pe.matmul(bank[1][:, 2 * P:3 * P], ones[:].to_broadcast([P, P]), a_tok, start=True, stop=True).then_inc(S["cs_ready"], 1)
            pe.wait_ge(S["cs_copied"], 2)

            with pe.Fori(0, GROUPS) as g:
                for q in range(6):
                    dense((q + 1) % 2, g * 5 + (N_SSM + q) // 2, h_hi, h_lo)
                pe.wait_ge(S["conv_silu"], g * 6 + 6)
                for c in range(NT):
                    cols = slice(c * P, (c + 1) * P)
                    if c:
                        pe.wait_ge(S["xd_ready"], g * 16 + 2 * c)
                        pe.wait_ge(S["btok_ready"], g * NT + c)
                        pe.wait_ge(S["g_masked"], g * NT + c)
                    for j in range(4):
                        mm = pe.transpose(bank[0][:, j * P:(j + 1) * P], tile[:, j, cols], id_)
                    mm.then_inc(S["x_turned"], 1)
                    pe.transpose(bank[1][:, 0:P], tile[:, 4, cols], id_)
                    pe.matmul(bank[1][:, P:2 * P], tile[:, 4, cols], tile[:, 5, cols], start=True, stop=True
                              ).then_inc(S["g_ready"], 1)
                    pe.wait_ge(S["xd_ready"], g * 16 + 2 * c + 2)
                    pe.wait_ge(S["btok_ready"], g * NT + c + 1)
                    if c:
                        pe.wait_ge(S["state_ready"], g * (NT + 1) + c + 1)
                        pe.wait_ge(S["y_taken"], g * NT * 4 + 4 * c)
                    else:
                        pe.wait_ge(S["state_ready"], g * (NT + 1) + 1)
                    pe.matmul(bank[2][:, :], tile[:, 11, HALF:HALF + P], tile[:, 10, HALF:T], start=True, stop=True
                              ).then_inc(S["s_ready"], 1)
                    pe.wait_ge(S["m_ready"], g * 16 + 2 * c + 2)
                    for r in range(GH):
                        rows = slice((r % 2) * HD, (r % 2 + 1) * HD)
                        o = bank[3][rows, (r // 2) * P:(r // 2 + 1) * P]
                        pe.matmul(o, tile[:, 10, r * HD:(r + 1) * HD], tile[:, 8, r * P:(r + 1) * P],
                                  start=True, stop=False)
                        mm = pe.matmul(o, tile[:, 11, r * HD:(r + 1) * HD], tile[:, 9, r * P:(r + 1) * P],
                                       start=False, stop=True)
                    mm.then_inc(S["y_ready"], 1)
                for q in range(6, 10):
                    dense((q + 1) % 2, g * 5 + (N_SSM + q) // 2, h_hi, h_lo)
                pe.wait_ge(S["ssm_sq"], g * 4 + 4)
                row_means(tile[:, 7, :], S["ssm_ms"])
                pe.wait_ge(S["ssm_rstd"], g + 1)
                broadcast(S["ssm_bcast"])

            with pe.Fori(0, KT // 2) as t:
                for s in range(2):
                    dense(1, t * 2 + (N_C // 2 + s), h_hi, h_lo)
                    dense(0, t * 2 + (N_C // 2 + 1 + s), u_hi, u_lo, (S["y_split"], 0) if s == 0 else None)

            with pe.Fori(0, KT // 2) as t:
                for s in range(2):
                    n = N_OUT + s
                    dense(n % 2, t + n // 2, u_hi, u_lo, (S["merged_ready"], 0) if s == 0 else None)
            pe.wait_ge(S["x1_sum"], KT)
            row_means(tile[:, 11, :], S["n2_ms"])
            pe.wait_ge(S["n2_rstd"], 1)
            broadcast(S["n2_bcast"])

            with pe.Fori(0, QUARTERS) as q4:
                with pe.Fori(0, KT // 2) as t:
                    for s in range(2):
                        n = N_MLP + s
                        dense(n % 2, q4 * 8 + t + n // 2, h_hi, h_lo, (S["n2_ready"], 0) if s == 0 else None)
                with pe.Fori(0, KT // 2) as t:
                    for s in range(2):
                        n = N_MLP + 8 + s
                        dense(n % 2, q4 * 8 + t + n // 2, u_hi, u_lo, (S["hid_ready"], q4 * 8) if s == 0 else None)
            pe.wait_ge(S["f_sum"], KT)
            row_means(tile[:, 11, :], S["f_ms"])
            pe.wait_ge(S["f_rstd"], 1)
            broadcast(S["f_bcast"])

        @block.scalar
        def _(act):
            act.sem_inc(S["merged_saved"], 16)

            def root(width, signal):
                act.activation(rms[:, 1, 0:NT], rms[:, 0, 0:NT], ACT.Sqrt, bias=eps[:, 0:1], scale=1.0 / width
                               ).then_inc(signal, 1)

            for k in range(KT):
                act.wait_ge(x_in_s[k // 2], 16)
                if k >= 2:
                    act.wait_ge(S["sq_used"], k - 1)
                act.activation(tile[:, 10 + 2 * (k % 2), :], xres[k], ACT.Square).then_inc(S["sq_ready"], 1)
            act.wait_ge(S["lam_dots"], 2)
            act.activation(lam[:, 2:4], lam[:, 0:2], ACT.Exp).then_inc(S["lam_exps"], 1)
            act.wait_ge(S["root_ready"], 1)
            root(D, S["root_ready"])
            for k in range(KT):
                act.wait_ge(S["h_scaled"], k + 1)
                act.activation(h_hi[:, k, :], xres[k], ACT.Identity, bias=mod[:, k:k + 1]).then_inc(S["h_hi_ready"], 1)

            def da_evacuate(s, head):
                for q, dst in enumerate((2, 0, 1)):
                    n = 3 * s + q
                    act.wait_ge(S["block_done"], head * 3 + q + 1)
                    act.activation(tile[:, dst, :], acc[n % 2][:], ACT.Copy).then_inc(S["qkv_ready"], 1)
                    act.wait_ge(S["qkv_ready"], head * 3 + q + 1)
                    act.sem_inc(acc_free[n % 2], 1)
                    if q == 0:
                        act.wait_ge(S["v_turned"], head + 1)
                        for half in range(2):
                            act.activation(tile[:, 3, half * HALF:(half + 1) * HALF], bank[half], ACT.Copy
                                           ).then_inc(S["v_tok"], 1)

            def da_head(head):
                def exps(i):
                    for m in range(2):
                        act.wait_ge(S["negmax"], head * 16 + 2 * i + m + 1)
                        col = 2 * (i % 2) + m
                        src = tile[:, (5, 6, 7, 8)[col], 0:(i + 1) * P]
                        act.activation(src, src, ACT.Exp, bias=mx[:, col:col + 1], accum_out=sm[:, col:col + 1]
                                       ).then_inc(S["exped"], 1)

                def pieces(i):
                    for half in range(1 + i // 4):
                        n = PIECES.index((i, half))
                        act.wait_ge(S["turned"], head * NP_ + n + 1)
                        if n >= 2:
                            act.wait_ge(S["pv_done"], head * NP_ + n - 1)
                        w = (min(4 * half + 4, i + 1) - 4 * half) * P
                        act.activation(tile[:, 9, (n % 2) * HALF:(n % 2) * HALF + w], bank[2][:, 0:w], ACT.Copy
                                       ).then_inc(S["turned_sb"], 1)
                    if i % 4 == 3:
                        act.wait_ge(S["pv_done"], head * NP_ + n + 1)
                        act.activation(tile[:, 10, (i // 4) * HALF:(i // 4 + 1) * HALF], bank[3], ACT.Copy
                                       ).then_inc(S["o_copied"], 1)

                exps(0)
                for i in range(1, NT):
                    exps(i)
                    pieces(i - 1)
                pieces(NT - 1)
                act.wait_ge(S["da_clipped"], head * 2 + 2)
                act.activation(tile[:, 5, :], tile[:, 5, :], ACT.Square).then_inc(S["da_sq"], 1)
                act.activation(tile[:, 8, :], tile[:, 7, :], ACT.Square, scale=2.0 ** -30).then_inc(S["da_sq"], 1)
                act.wait_ge(S["da_root"], head * 2 + 1)
                root(P, S["da_root"])
                act.wait_ge(S["da_scaled"], head + 1)
                act.activation(u_hi[:, bass.ds(head, 1), :].rearrange("p a t -> p (a t)"), tile[:, 6, :], ACT.Copy
                               ).then_inc(S["da_hi"], 1)

            with act.Fori(0, DA_HEADS // 2) as t:
                for s in range(2):
                    head = t * 2 + s
                    act.dma_start(tile[:, 4, :], da_tab[bass.ds(head, 1)].rearrange("a p x -> (a p) x")
                                  ).then_inc(S["da_tab_in"], 16)
                    da_evacuate(s, head)
                    da_head(head)

            act.wait_ge(S["block_done"], N_SW + 1)
            act.activation(tile[:, 2, :], acc[0][:], ACT.Copy).then_inc(S["sw_qkv"], 1)
            act.wait_ge(S["sw_qkv"], 1)
            act.sem_inc(acc_free[0], 1)
            act.wait_ge(S["sw_vt"], 1)
            act.activation(tile[:, 3, :], wk[0][:], ACT.Copy).then_inc(S["sw_vtok"], 1)
            act.wait_ge(S["block_done"], N_SW + 2)
            act.activation(tile[:, 0, :], acc[1][:], ACT.Copy).then_inc(S["sw_qkv"], 1)
            act.wait_ge(S["sw_qkv"], 2)
            act.sem_inc(acc_free[1], 1)

            with act.Fori(0, SW_PAIRS // 2) as t:
                for s in range(2):
                    j = t * 2 + s
                    act.wait_ge(S["u_ready"], t * 2 + s + 3)
                    act.dma_start(sw_bias[:, s * 512:(s + 1) * 512], sw_tab[bass.ds(j, 1)].rearrange("a p x -> (a p) x")
                                  ).then_inc(S["sw_tab_in"], 16)
                    act.wait_ge(S["block_done"], j + N_SW + 3)
                    act.activation(tile[:, 1, :], acc[s][:], ACT.Copy).then_inc(S["sw_qkv"], 1)
                    act.wait_ge(S["sw_qkv"], j + 3)
                    act.sem_inc(acc_free[s], 1)
                    act.wait_ge(S["sw_negmax"], j * 2 + 2)
                    for g in range(2):
                        for i in range(NT):
                            lo = i * 256 + (0 if i else P)
                            src = tile[:, 5 + 2 * g + i // 4, lo % T:(i % 4 + 1) * 256]
                            col = g * NT + i
                            act.activation(src, src, ACT.Exp, bias=swn[:, col:col + 1], accum_out=sws[:, col:col + 1])
                    for g in range(2):
                        head = C_SINK + 4 * g + s
                        last = act.activation(swe[:, g * NT:(g + 1) * NT], swn[:, g * NT:(g + 1) * NT], ACT.Exp,
                                              bias=par[:, bass.ds(t * 2 + head, 1)])
                    last.then_inc(S["sw_exped"], 1)
                    for i in range(NT):
                        act.wait_ge(S["sw_turned"], j * NT + i + 1)
                        if i >= 2:
                            act.wait_ge(S["sw_out"], j * NT + i - 1)
                        lo = 0 if i else P
                        for g in range(2) if i == 0 else (0,):
                            a, z = (g * 256 + lo, g * 256 + 256) if i == 0 else (0, HALF)
                            last = act.activation(tile[:, 9, (i % 2) * HALF + a:(i % 2) * HALF + z],
                                                  bank[2 + i % 2][:, a:z], ACT.Copy)
                        last.then_inc(S["sw_turned_sb"], 1)
                    act.wait_ge(S["sw_out"], j * NT + NT)
                    act.activation(u_hi[:, bass.ds(j + 4, 1), :].rearrange("p a t -> p (a t)"), wk[0][:], ACT.Copy
                                   ).then_inc(S["sw_hi"], 1)

            with act.Fori(0, KT // 2) as t:
                for s in range(2):
                    m = t * 2 + s
                    for q in range(4):
                        b = 4 * s + q
                        act.wait_ge(S["mod_done"], t * 8 + (16 + b - 1))
                        act.dma_start(tile[:, 8 + q % 2, :], ada_in[bass.ds(t * 8 + (16 + b), 1)].rearrange("a p c -> (a p) c")
                                      ).then_inc(ada_s[q % 2], 16)
                        if q < 2:
                            n = 3 * s + q
                            act.wait_ge(S["block_done"], m * 3 + (N_AB + q + 1))
                            if q == 0:
                                act.wait_ge(S["gates_free"], m + 1)
                            act.activation(tile[:, q, :], acc[n % 2][:], ACT.Sigmoid).then_inc(S["gate_ready"], 1)
                            act.wait_ge(S["gate_ready"], m * 2 + q + 1)
                            act.sem_inc(acc_free[n % 2], 1)
                    act.wait_ge(S["merged_out"], m + 1)
                    act.dma_start(merged_d[bass.ds(m, 1)].rearrange("a p t -> (a p) t"), tile[:, 4 + s, :]
                                  ).then_inc(S["merged_saved"], 16)

            act.wait_ge(S["block_done"], N_DT + 1)
            act.activation(tile[0:HEADS, 0, :], acc[0][0:HEADS, :], ACT.Copy).then_inc(S["dt_copied"], 1)
            act.wait_ge(S["dt_copied"], 1)
            act.sem_inc(acc_free[0], 1)
            act.wait_ge(S["dt_abs"], 1)
            act.activation(dtm[:, 2, :], dtm[:, 1, :], ACT.Exp, scale=-1.0)
            act.activation(exp_a[:], par[:, C_ALOG:C_ALOG + HEADS], ACT.Exp).then_inc(S["dt_exp"], 1)
            act.wait_ge(S["cs_ready"], 1)
            act.activation(dtm[:, 5, :], bank[1][:, 2 * P:3 * P], ACT.Exp)
            act.activation(dtm[:, 1, :], bank[1][:, 0:P], ACT.Copy).then_inc(S["cs_copied"], 1)
            act.wait_ge(S["cs_copied"], 1)
            act.dma_start(cs_d, dtm[:, 1, :]).then_inc(S["cs_saved"], 16)
            act.wait_ge(S["dt_diff"], 1)
            act.activation(dtm[:, 6, :], dtm[:, 6, :], ACT.Exp).then_inc(S["dt_decays"], 1)
            act.wait_ge(S["cs_saved"], 16)

            with act.Fori(0, GROUPS) as g:
                def load_sums(c):
                    act.dma_start(tile[:, 6 + c % 2, :],
                                  cs_d[bass.ds(g * GH + c * HEADS, GH), :].rearrange("r l -> (r l)").partition_broadcast(P)
                                  ).then_inc(S["csb_in"], 16)

                for q in range(6):
                    dst = tile[:, (4, 5, 0, 1, 2, 3)[q], :]
                    act.wait_ge(S["block_done"], g * 10 + (N_SSM + q + 1))
                    if q == 0:
                        act.wait_ge(S["z_used"], g * 10 + 1)
                    act.activation(dst, acc[(q + 1) % 2][:], ACT.Identity, bias=gpar[:, 5 * q + 4:5 * q + 5],
                                   scale=gpar[:, 5 * q + 3:5 * q + 4]).then_inc(S["conv_first"], 1)
                    act.wait_ge(S["conv_done"], g * 6 + q + 1)
                    act.activation(dst, dst, ACT.Silu).then_inc(S["conv_silu"], 1)
                load_sums(0)
                for c in range(NT):
                    csb = tile[:, 6 + c % 2, :]
                    act.wait_ge(S["csb_in"], g * 128 + 16 * c + 16)
                    if c:
                        act.wait_ge(S["y_ready"], g * NT + c)
                    act.activation(tile[:, 9, :], csb, ACT.Exp).then_inc(S["e_ready"], 1)
                    act.wait_ge(S["g_ready"], g * NT + c + 1)
                    if c:
                        act.wait_ge(S["s_ready"], g * NT + c)
                    act.activation(tile[:, 11, HALF:HALF + P], bank[1][:, 0:P], ACT.Copy).then_inc(S["btok_ready"], 1)
                    act.wait_ge(S["diff_ready"], g * NT + c + 1)
                    if c + 1 < NT:
                        load_sums(c + 1)
                    act.activation(tile[:, 8, :], tile[:, 8, :], ACT.Relu, scale=-1.0).then_inc(S["relu_ready"], 1)
                    act.wait_ge(S["relu_ready"], g * NT + c + 1)
                    act.activation(tile[:, 8, :], tile[:, 8, :], ACT.Exp, scale=-1.0).then_inc(S["l_ready"], 1)
                for j in range(4):
                    act.wait_ge(S["block_done"], g * 10 + (N_SSM + 6 + j + 1))
                    if j:
                        act.wait_ge(S["z_used"], g * 10 + j + 1)
                    act.activation(tile[:, 9, :], acc[(j + 1) % 2][:], ACT.Silu).then_inc(S["z_silu"], 1)
                    act.wait_ge(S["z_silu"], g * 4 + j + 1)
                    act.sem_inc(acc_free[(j + 1) % 2], 1)
                    act.wait_ge(S["z_used"], g * 10 + j + 2)
                    if j:
                        act.wait_ge(S["ssm_sq"], g * 4 + j)
                    dst = tile[:, 8 if j else 7, :]
                    act.activation(dst, tile[:, j, :], ACT.Square).then_inc(S["y_gated"], 1)
                act.wait_ge(S["ssm_root"], g * 2 + 1)
                root(HALF, S["ssm_root"])
                for j in range(4):
                    act.wait_ge(S["ssm_scaled"], g * 4 + j + 1)
                    act.activation(u_hi[:, bass.ds(g * 4 + j, 1), :].rearrange("p a t -> p (a t)"), tile[:, j, :], ACT.Copy
                                   ).then_inc(S["ssm_hi"], 1)

            act.wait_ge(S["merged_saved"], 16 * KT + 16)
            act.wait_ge(S["z_used"], 21)
            with act.Fori(0, KT // 2) as t:
                for s in range(2):
                    m = t * 2 + s
                    act.wait_ge(S["c_free"], m + 1)
                    act.dma_start(tile[:, 10 + s, :], merged_d[bass.ds(m, 1)].rearrange("a p t -> (a p) t")
                                  ).then_inc(merged_s[s], 16)
                    act.wait_ge(S["block_done"], m * 2 + (N_C + 1))
                    act.activation(tile[:, 8 + s, :], acc[1][:], ACT.Sigmoid).then_inc(S["c_gate"], 1)
                    act.wait_ge(S["c_gate"], m + 1)
                    act.sem_inc(acc_free[1], 1)
            for k in range(KT):
                act.wait_ge(S["merged_all"], KT)
                act.activation(u_hi[:, k, :], tile[:, k, :], ACT.Copy).then_inc(S["merged_hi"], 1)
            for k in range(KT):
                act.wait_ge(S["merged_ready"], k + 1)
                act.dma_start(tile[:, k, :], x_in[k]).then_inc(S["x2_in"], 16)
            for k in range(KT):
                act.wait_ge(S["x1_ready"], k + 1)
                if k >= 2:
                    act.wait_ge(S["x1_sum"], k - 1)
                act.activation(tile[:, 10 + 2 * (k % 2), :], xres[k], ACT.Square).then_inc(S["x1_sq"], 1)
            act.wait_ge(S["n2_root"], 1)
            root(D, S["n2_root"])
            for k in range(KT):
                act.wait_ge(S["n2_scaled"], k + 1)
                act.activation(h_hi[:, k, :], tile[:, 8 + k % 2, :], ACT.Identity, bias=mod[:, 24 + k:25 + k]
                               ).then_inc(S["n2_hi"], 1)
            with act.Fori(0, QUARTERS) as q4:
                with act.Fori(0, KT // 2) as t:
                    for s in range(2):
                        b = (N_MLP + s) % 2
                        m = q4 * 8 + t * 2 + s
                        act.wait_ge(S["block_done"], q4 * 16 + t * 2 + (N_MLP + s + 1))
                        act.wait_ge(S["relu_free"], m + 1)
                        act.activation(tile[:, 8 + s, :], acc[b][:], ACT.Relu).then_inc(S["hid_relu"], 1)
                        act.wait_ge(S["hid_relu"], m + 1)
                        act.sem_inc(acc_free[b], 1)
                        act.wait_ge(S["hid_sq"], m + 1)
                        act.activation(u_hi[:, bass.ds(t * 2 + s, 1), :].rearrange("p a t -> p (a t)"), tile[:, 10 + s, :], ACT.Copy
                                       ).then_inc(S["hid_hi"], 1)
            for k in range(KT):
                act.wait_ge(S["x2_ready"], (QUARTERS - 1) * KT + k + 1)
                if k >= 2:
                    act.wait_ge(S["f_sum"], k - 1)
                act.activation(tile[:, 10 + 2 * (k % 2), :], xres[k], ACT.Square).then_inc(S["f_sq"], 1)
            act.wait_ge(S["f_root"], 1)
            root(D, S["f_root"])
            for k in range(KT):
                act.wait_ge(S["f_ready"], k + 1)
                act.dma_start(out[k], xres[k]).then_inc(S["out_saved"], 16)
            act.wait_ge(S["out_saved"], 16 * KT)

        @block.vector
        def _(dve):
            own = Steps(dve, S["dve_own"])
            dve.sem_inc(S["gates_free"], 1)
            dve.sem_inc(S["c_free"], 2)
            dve.sem_inc(S["relu_free"], 2)

            def squares_sum(first_wait, used, base=0):
                for k in range(KT):
                    dve.wait_ge(first_wait, base + k + 1)
                    src = tile[:, 10 + 2 * (k % 2), :]
                    if k == 0:
                        dve.tensor_copy(tile[:, 11, :], src).then_inc(used, 1)
                    else:
                        dve.wait_ge(used, base + k)
                        dve.tensor_tensor(tile[:, 11, :], tile[:, 11, :], src, ALU.add).then_inc(used, 1)

            def factor(ms, root, inverse, n):
                dve.wait_ge(ms, n + 1)
                dve.tensor_copy(rms[:, 0, :], bank[3][:, 0:NT]).then_inc(root, 1)
                dve.wait_ge(root, n * 2 + 2)
                dve.reciprocal(rstd[:], rms[:, 1, :]).then_inc(inverse, 1)

            dve.memset(ones[:], 1.0).then_inc(acc_free[0], 1)
            dve.memset(eps[:], EPS).then_inc(acc_free[1], 1)
            dve.memset(sm[:], 0.0).then_inc(S["ab_free"], 1)
            dve.wait_ge(S["par_in"], 16)
            dve.wait_ge(S["lam_in"], 16)
            for q in range(2):
                v = tile[:, 11, 2 * q * HD:2 * (q + 1) * HD]
                dve.tensor_tensor_reduce(tile[:, 11, (4 + q) * HD:(5 + q) * HD], v[:, 0:HD], v[:, HD:2 * HD], 1.0, 0.0, ALU.mult, ALU.add,
                                         lam[:, q:q + 1]).then_inc(S["lam_dots"], 1)
            own.mark(dve.tensor_scalar(a_da[:], par[:, C_SUBLN:C_SUBLN + 1], DA_OUT, None, ALU.mult))
            dve.wait_ge(S["lam_dots"], 2)
            squares_sum(S["sq_ready"], S["sq_used"])
            dve.wait_ge(S["lam_exps"], 1)
            own.mark(dve.tensor_tensor(lam[:, 4:5], lam[:, 3:4], lam[:, 2:3], ALU.subtract))
            own.settle()
            own.mark(dve.tensor_scalar(lam[:, 5:6], lam[:, 4:5], -LAM_INIT, None, ALU.add))
            dve.wait_ge(S["mod_done"], 16)
            own.mark(dve.tensor_tensor(mod[:, 0:16], bank[2][:, 0:16], par[:, C_ADAB:C_ADAB + 16], ALU.add))
            own.settle()
            own.mark(dve.scalar_tensor_tensor(out=a_mix[:], in0=mod[:, 8:16], scalar=1.0, in1=par[:, C_GMIX:C_GMIX + 8],
                                              op0=ALU.add, op1=ALU.mult))
            own.settle()

            factor(S["ms_ready"], S["root_ready"], S["rstd_ready"], 0)
            dve.wait_ge(S["bcast_ready"], 1)
            for k in range(KT):
                dve.scalar_tensor_tensor(out=xres[k], in0=xres[k], scalar=a_mix[:, k:k + 1], in1=wk[0][:],
                                         op0=ALU.mult, op1=ALU.mult).then_inc(S["h_scaled"], 1)
                if k:
                    dve.wait_ge(S["h_hi_ready"], k)
                    dve.scalar_tensor_tensor(out=h_lo[:, k - 1, :], in0=xres[k - 1], scalar=mod[:, k - 1:k],
                                             in1=h_hi[:, k - 1, :].bitcast(F32), op0=ALU.add, op1=ALU.subtract
                                             ).then_inc(S["h_ready"], 1)
            dve.wait_ge(S["h_hi_ready"], KT)
            dve.scalar_tensor_tensor(out=h_lo[:, KT - 1, :], in0=xres[KT - 1], scalar=mod[:, KT - 1:KT],
                                     in1=h_hi[:, KT - 1, :].bitcast(F32), op0=ALU.add, op1=ALU.subtract
                                     ).then_inc(S["h_ready"], 1)

            def da_head(head):
                def bias(i, m):
                    col = 2 * (i % 2) + m
                    w = (i + 1) * P
                    dve.wait_ge(S["scored"], head * 16 + 2 * i + m + 1)
                    dve.nop(nofuse=True)
                    dve.tensor_tensor_reduce(tile[:, (5, 6, 7, 8)[col], 0:w], wk[0][:, 0:w], tile[:, 4, T - w:T], SCALE, NEG,
                                             ALU.add, ALU.max, mxp[:, col:col + 1]).then_inc(S["biased"], 1)
                    dve.wait_ge(S["biased"], head * 16 + 2 * i + m + 1)
                    dve.tensor_scalar(mx[:, col:col + 1], mxp[:, col:col + 1], -1.0, None, ALU.mult).then_inc(S["negmax"], 1)

                def weigh(i):
                    col = 2 * (i % 2)
                    w = (i + 1) * P
                    p0, p1 = (tile[:, (5, 6, 7, 8)[col + m], 0:w] for m in range(2))
                    dve.wait_ge(S["exped"], head * 16 + 2 * i + 2)
                    own.mark(dve.reciprocal(rc[:, col:col + 2], sm[:, col:col + 2]))
                    own.settle()
                    own.mark(dve.tensor_scalar(p1, p1, rc[:, col + 1:col + 2], lam[:, 5:6], ALU.mult, ALU.mult))
                    own.settle()
                    if i:
                        dve.wait_ge(S["turned"], head * NP_ + PIECES.index((i - 1, (i - 1) // 4)) + 1)
                    dve.scalar_tensor_tensor(out=tile[:, 12, 0:w], in0=p0, scalar=rc[:, col:col + 1], in1=p1,
                                             op0=ALU.mult, op1=ALU.add).then_inc(S["weighted"], 1)

                dve.wait_ge(S["da_tab_in"], head * 16 + 16)
                for i in range(NT):
                    bias(i, 0)
                    bias(i, 1)
                    if i:
                        weigh(i - 1)
                        dve.wait_ge(S["weighted"], head * 8 + i)
                weigh(NT - 1)
                dve.wait_ge(S["o_copied"], head * 2 + 2)
                dve.tensor_scalar(tile[:, 5, :], tile[:, 10, :], 2.0 ** 60, -2.0 ** 60, ALU.min, ALU.max
                                  ).then_inc(S["da_clipped"], 1)
                dve.tensor_scalar(tile[:, 7, :], tile[:, 10, :], 2.0 ** 70, -2.0 ** 70, ALU.min, ALU.max
                                  ).then_inc(S["da_clipped"], 1)
                dve.wait_ge(S["da_ms"], head * 2 + 2)
                s1, s2 = bank[3][:, 0:NT], bank[3][:, NT:2 * NT]
                big, low, fac = rms[:, 2, :], rms[:, 3, :], rms[:, 4, :]
                own.mark(dve.tensor_scalar(big, s2, 2.0 ** 52, None, ALU.is_gt))
                own.mark(dve.tensor_scalar(rms[:, 5, :], s2, 2.0 ** 68, None, ALU.is_lt))
                own.settle()
                own.mark(dve.tensor_scalar(low, big, -1.0, 1.0, ALU.mult, ALU.add))
                own.mark(dve.tensor_tensor(rms[:, 1, :], s2, big, ALU.mult))
                own.settle()
                own.mark(dve.scalar_tensor_tensor(out=fac, in0=big, scalar=2.0 ** -30, in1=low, op0=ALU.mult, op1=ALU.add))
                own.settle()
                own.mark(dve.tensor_tensor(low, s1, low, ALU.mult))
                own.mark(dve.tensor_tensor(fac, fac, rms[:, 5, :], ALU.mult))
                own.settle()
                dve.tensor_tensor(rms[:, 0, :], low, rms[:, 1, :], ALU.add).then_inc(S["da_root"], 1)
                dve.wait_ge(S["da_root"], head * 2 + 2)
                own.mark(dve.reciprocal(rms[:, 2, :], rms[:, 1, :]))
                own.settle()
                dve.tensor_tensor(rstd[:], rms[:, 2, :], rms[:, 4, :], ALU.mult).then_inc(S["da_rstd"], 1)
                dve.wait_ge(S["da_bcast"], head + 1)
                dve.scalar_tensor_tensor(out=tile[:, 6, :], in0=tile[:, 7, :], scalar=a_da[:, 0:1], in1=wk[0][:],
                                         op0=ALU.mult, op1=ALU.mult).then_inc(S["da_scaled"], 1)
                dve.wait_ge(S["da_hi"], head + 1)
                dst = bass.ds(head, 1)
                dve.tensor_tensor(u_lo[:, dst, :].rearrange("p a t -> p (a t)"), tile[:, 6, :],
                                  u_hi[:, dst, :].rearrange("p a t -> p (a t)").bitcast(F32), ALU.subtract
                                  ).then_inc(S["u_ready"], 1)

            with dve.Fori(0, DA_HEADS) as head, own.loop(head, 24, DA_HEADS):
                da_head(head)

            def sw_pair(s, j):
                dve.wait_ge(S["sw_tab_in"], j * 16 + 16)
                for i in range(NT):
                    dve.wait_ge(S["sw_scored"], j * NT + i + 1)
                    dve.nop(nofuse=True)
                    w = 256 if i else P
                    for g in range(2):
                        last = dve.tensor_tensor_reduce(
                            tile[:, 5 + 2 * g + i // 4, (i % 4 + 1) * 256 - w:(i % 4 + 1) * 256],
                            bank[2 * (i % 2) + g][:, 256 - w:256],
                            sw_bias[:, s * 512 + (g + 1) * 256 - w:s * 512 + (g + 1) * 256], SCALE, NEG, ALU.add, ALU.max,
                            swm[:, g * NT + i:g * NT + i + 1])
                    last.then_inc(S["sw_biased"], 1)
                dve.wait_ge(S["sw_biased"], j * NT + NT)
                for g in range(2):
                    cols = slice(g * NT, (g + 1) * NT)
                    dve.tensor_scalar(swn[:, cols], swm[:, cols], par[:, bass.ds(j + (C_SINK + 4 * g), 1)], -1.0,
                                      ALU.max, ALU.mult).then_inc(S["sw_negmax"], 1)
                dve.wait_ge(S["sw_exped"], j + 1)
                own.mark(dve.tensor_tensor(swd[:], sws[:], swe[:], ALU.add))
                own.settle()
                own.mark(dve.reciprocal(swr[:], swd[:]))
                own.settle()
                for i in range(NT):
                    for g in range(2):
                        lo = i * 256 + (0 if i else P)
                        p = tile[:, 5 + 2 * g + i // 4, lo % T:(i % 4 + 1) * 256]
                        last = dve.tensor_scalar(p, p, swr[:, g * NT + i:g * NT + i + 1], None, ALU.mult)
                    last.then_inc(S["sw_weighted"], 1)
                dve.wait_ge(S["sw_hi"], j + 1)
                dst = bass.ds(j + 4, 1)
                dve.tensor_tensor(u_lo[:, dst, :].rearrange("p a t -> p (a t)"), wk[0][:],
                                  u_hi[:, dst, :].rearrange("p a t -> p (a t)").bitcast(F32), ALU.subtract
                                  ).then_inc(S["u_ready"], 1)

            with dve.Fori(0, SW_PAIRS // 2) as t, own.loop(t, 4, SW_PAIRS // 2):
                for s in range(2):
                    sw_pair(s, t * 2 + s)

            with dve.Fori(0, KT // 2) as t, own.loop(t, 4, KT // 2):
                for s in range(2):
                    m = t * 2 + s
                    b = (3 * s + 2) % 2
                    dve.wait_ge(S["gate_ready"], m * 2 + 2)
                    dve.wait_ge(S["block_done"], m * 3 + (N_AB + 3))
                    own.mark(dve.tensor_tensor(tile[:, 2, :], tile[:, 0, :], wk[0][:], ALU.mult))
                    own.mark(dve.tensor_tensor(tile[:, 3, :], tile[:, 1, :], acc[b][:], ALU.mult))
                    own.settle()
                    dve.sem_inc(acc_free[b], 1)
                    dve.sem_inc(S["ab_free"], 1)
                    dve.sem_inc(S["gates_free"], 1)
                    dve.wait_ge(S["merged_saved"], t * 32 + 16)
                    dve.tensor_tensor(tile[:, 4 + s, :], tile[:, 2, :], tile[:, 3, :], ALU.add).then_inc(S["merged_out"], 1)
                    dve.wait_ge(S["merged_out"], m + 1)
            dve.wait_ge(S["mod_done"], 48)
            dve.tensor_tensor(mod[:, 16:48], bank[2][:, 16:48], par[:, C_ADAB + 16:C_ADAB + 48], ALU.add
                              ).then_inc(S["mod_rest"], 1)
            dve.wait_ge(S["mod_rest"], 1)
            own.mark(dve.scalar_tensor_tensor(out=a_mlp[:], in0=mod[:, 32:40], scalar=1.0,
                                              in1=par[:, C_GMLP:C_GMLP + 8], op0=ALU.add, op1=ALU.mult))

            heads = lambda ap: ap.rearrange("p (c h) -> p c h", h=HEADS)
            dve.wait_ge(S["dt_turned"], 1)
            own.mark(dve.tensor_tensor(heads(dtm[:, 3, :]), heads(bank[0][:, 0:P]),
                                       par[:, C_DTB:C_DTB + HEADS].unsqueeze(1).to_broadcast([P, NT, HEADS]), ALU.add))
            own.settle()
            dve.scalar_tensor_tensor(out=dtm[:, 1, :], in0=dtm[:, 3, :], scalar=-1.0, in1=dtm[:, 3, :], op0=ALU.mult,
                                     op1=ALU.max).then_inc(S["dt_abs"], 1)
            dve.wait_ge(S["dt_exp"], 1)
            e_, s_, s2, q_ = (dtm[:, n, :] for n in (2, 4, 6, 7))
            own.mark(dve.tensor_scalar(q_, e_, 2.0, None, ALU.add))
            own.settle()
            own.mark(dve.reciprocal(s2, q_))
            own.settle()
            own.mark(dve.tensor_tensor(s_, e_, s2, ALU.mult))
            own.settle()
            own.mark(dve.tensor_tensor(s2, s_, s_, ALU.mult))
            own.settle()
            own.mark(dve.tensor_scalar(q_, s2, 1.0 / 15, None, ALU.mult))
            for odd in (13, 11, 9, 7, 5, 3):
                own.settle()
                own.mark(dve.scalar_tensor_tensor(out=q_, in0=q_, scalar=1.0 / odd, in1=s2, op0=ALU.add, op1=ALU.mult))
            own.settle()
            own.mark(dve.scalar_tensor_tensor(out=q_, in0=q_, scalar=1.0, in1=s_, op0=ALU.add, op1=ALU.mult))
            own.mark(dve.tensor_scalar(dtm[:, 3, :], dtm[:, 3, :], 0.0, None, ALU.max))
            own.settle()
            dt_ = dtm[:, 4, :]
            own.mark(dve.scalar_tensor_tensor(out=dt_, in0=q_, scalar=2.0, in1=dtm[:, 3, :], op0=ALU.mult, op1=ALU.add))
            own.settle()
            dve.scalar_tensor_tensor(out=heads(dtm[:, 0, :]), in0=heads(dt_), scalar=-1.0,
                                     in1=exp_a[:].unsqueeze(1).to_broadcast([P, NT, HEADS]),
                                     op0=ALU.mult, op1=ALU.mult).then_inc(S["dt_da"], 1)
            dve.wait_ge(S["dt_da"], 1)
            dve.wait_ge(S["cs_copied"], 1)
            own.mark(dve.tensor_copy(dtm[:, 7, :], bank[1][:, P:2 * P]))
            own.settle()
            dve.tensor_tensor(dtm[:, 6, :], bank[1][:, 2 * P:3 * P], dtm[:, 7, :], ALU.subtract).then_inc(S["dt_diff"], 1)
            dve.wait_ge(S["dt_decays"], 1)
            own.mark(dve.tensor_tensor(dtm[:, 6, :], dtm[:, 6, :], dt_, ALU.mult))
            own.settle()
            dve.sem_inc(S["cs_copied"], 1)

            with dve.Fori(0, GROUPS) as g, own.loop(g, 14 + NT + 4, GROUPS):
                own.mark(dve.tensor_copy(gpar[:, 0:30], par[:, bass.ds(g * 30 + C_CONV, 30)]))
                own.mark(dve.tensor_copy(gpar[:, 30:34], par[:, bass.ds(g * 4 + C_D, 4)]))
                own.settle()
                dve.sem_inc(S["z_used"], 1)
                for q in range(6):
                    dst = tile[:, (4, 5, 0, 1, 2, 3)[q], :]
                    src = acc[(q + 1) % 2]
                    dve.wait_ge(S["conv_first"], g * 6 + q + 1)
                    for tap in (2, 1, 0):
                        lag = 3 - tap
                        ins = dve.scalar_tensor_tensor(out=dst[:, lag:T], in0=src[:, 0:T - lag],
                                                       scalar=gpar[:, 5 * q + tap:5 * q + tap + 1], in1=dst[:, lag:T],
                                                       op0=ALU.mult, op1=ALU.add)
                        if tap:
                            own.mark(ins)
                            own.settle()
                        else:
                            ins.then_inc(S["conv_done"], 1)
                    dve.wait_ge(S["conv_done"], g * 6 + q + 1)
                    dve.sem_inc(acc_free[(q + 1) % 2], 1)
                dve.memset(tile[:, 11, 0:HALF], 0.0).then_inc(S["state_ready"], 1)
                for c in range(NT):
                    cols = slice(c * P, (c + 1) * P)
                    now = bass.ds(g * GH + c * HEADS, GH)
                    byhead = lambda ap: ap.rearrange("p (h x) -> p h x", h=GH)
                    csb = tile[:, 6 + c % 2, :]
                    dve.wait_ge(S["csb_in"], g * 128 + 16 * c + 16)
                    if c:
                        dve.wait_ge(S["y_ready"], g * NT + c)
                    dve.tensor_tensor(byhead(tile[:, 8, :]), byhead(csb), dtm[:, 7, now].unsqueeze(2).to_broadcast([P, GH, P]),
                                      ALU.subtract).then_inc(S["diff_ready"], 1)
                    dve.wait_ge(S["x_turned"], g * NT + c + 1)
                    for n, fac in ((0, 4), (1, 6)):
                        dve.tensor_tensor(byhead(tile[:, 10, n * HALF:(n + 1) * HALF]), byhead(bank[0]),
                                          dtm[:, fac, now].unsqueeze(2).to_broadcast([P, GH, HD]), ALU.mult
                                          ).then_inc(S["xd_ready"], 1)
                    dve.wait_ge(S["btok_ready"], g * NT + c + 1)
                    dve.tensor_tensor(tile[:, 11, HALF + P:HALF + 2 * P], bank[1][:, P:2 * P], tri, ALU.mult
                                      ).then_inc(S["g_masked"], 1)
                    dve.wait_ge(S["e_ready"], g * NT + c + 1)
                    dve.tensor_tensor(byhead(tile[:, 9, :]), byhead(tile[:, 9, :]),
                                      tile[:, 5, cols].unsqueeze(1).to_broadcast([P, GH, P]), ALU.mult
                                      ).then_inc(S["m_ready"], 1)
                    dve.wait_ge(S["l_ready"], g * NT + c + 1)
                    dve.wait_ge(S["g_masked"], g * NT + c + 1)
                    dve.tensor_tensor(byhead(tile[:, 8, :]), byhead(tile[:, 8, :]),
                                      tile[:, 11, HALF + P:HALF + 2 * P].unsqueeze(1).to_broadcast([P, GH, P]), ALU.mult
                                      ).then_inc(S["m_ready"], 1)
                    dve.wait_ge(S["y_ready"], g * NT + c + 1)
                    for j in range(4):
                        dve.scalar_tensor_tensor(out=tile[:, j, cols], in0=tile[:, j, cols], scalar=gpar[:, 30 + j:31 + j],
                                                 in1=bank[3][:, j * P:(j + 1) * P], op0=ALU.mult, op1=ALU.add
                                                 ).then_inc(S["y_taken"], 1)
                    own.mark(dve.tensor_tensor(byhead(tile[:, 11, 0:HALF]), byhead(tile[:, 11, 0:HALF]),
                                               dtm[:, 5, now].unsqueeze(2).to_broadcast([P, GH, HD]), ALU.mult))
                    own.settle()
                    dve.tensor_tensor(tile[:, 11, 0:HALF], tile[:, 11, 0:HALF], bank[2][:, :], ALU.add
                                      ).then_inc(S["state_ready"], 1)
                    dve.wait_ge(S["state_ready"], g * (NT + 1) + c + 2)
                dve.wait_ge(S["y_taken"], g * 32 + 32)
                for j in range(4):
                    dve.wait_ge(S["z_silu"], g * 4 + j + 1)
                    own.mark(dve.tensor_tensor(tile[:, j, :], tile[:, j, :], tile[:, 9, :], ALU.mult))
                    own.settle()
                    dve.sem_inc(S["z_used"], 1)
                    dve.wait_ge(S["y_gated"], g * 4 + j + 1)
                    if j == 0:
                        dve.sem_inc(S["ssm_sq"], 1)
                    else:
                        dve.tensor_tensor(tile[:, 7, :], tile[:, 7, :], tile[:, 8, :], ALU.add).then_inc(S["ssm_sq"], 1)
                        dve.wait_ge(S["ssm_sq"], g * 4 + j + 1)
                factor(S["ssm_ms"], S["ssm_root"], S["ssm_rstd"], g)
                dve.wait_ge(S["ssm_bcast"], g + 1)
                for j in range(5):
                    if j < 4:
                        dve.scalar_tensor_tensor(out=tile[:, j, :], in0=tile[:, j, :],
                                                 scalar=par[:, bass.ds(g * 4 + (C_GSSM + j), 1)], in1=wk[0][:],
                                                 op0=ALU.mult, op1=ALU.mult).then_inc(S["ssm_scaled"], 1)
                    if j:
                        dve.wait_ge(S["ssm_hi"], g * 4 + j)
                        dst = bass.ds(g * 4 + j - 1, 1)
                        dve.tensor_tensor(u_lo[:, dst, :].rearrange("p a t -> p (a t)"), tile[:, j - 1, :],
                                          u_hi[:, dst, :].rearrange("p a t -> p (a t)").bitcast(F32), ALU.subtract
                                          ).then_inc(S["y_split"], 1)
                dve.wait_ge(S["y_split"], g * 4 + 4)
                for _n in range(5):
                    dve.sem_inc(S["z_used"], 1)

            dve.sem_inc(S["z_used"], 1)
            with dve.Fori(0, KT // 2) as t, own.loop(t, 2, KT // 2):
                for s in range(2):
                    m = t * 2 + s
                    dve.wait_ge(S["c_gate"], m + 1)
                    dve.wait_ge(S["block_done"], m * 2 + (N_C + 2))
                    own.mark(dve.tensor_tensor(tile[:, 8 + s, :], tile[:, 8 + s, :], acc[0][:], ALU.mult))
                    own.settle()
                    dve.sem_inc(acc_free[0], 1)
                    dve.wait_ge(merged_s[s], t * 16 + 16)
                    dst = tile[:, bass.ds(m, 1), :].rearrange("p a t -> p (a t)")
                    dve.tensor_tensor(dst, tile[:, 8 + s, :], tile[:, 10 + s, :], ALU.add).then_inc(S["merged_all"], 1)
                    dve.wait_ge(S["merged_all"], m + 1)
                    dve.sem_inc(S["c_free"], 1)
            for k in range(KT):
                dve.wait_ge(S["merged_hi"], k + 1)
                dve.tensor_tensor(u_lo[:, k, :], tile[:, k, :], u_hi[:, k, :].bitcast(F32), ALU.subtract
                                  ).then_inc(S["merged_ready"], 1)

            for k in range(KT):
                b = (N_OUT + k) % 2
                dve.wait_ge(S["block_done"], N_OUT + k + 1)
                dve.wait_ge(S["x2_in"], 16 * KT)
                dve.scalar_tensor_tensor(out=xres[k], in0=acc[b][:], scalar=mod[:, 16 + k:17 + k], in1=xres[k],
                                         op0=ALU.mult, op1=ALU.add).then_inc(S["x1_ready"], 1)
                dve.wait_ge(S["x1_ready"], k + 1)
                dve.sem_inc(acc_free[b], 1)
                dve.wait_ge(S["x1_sq"], k + 1)
                src = tile[:, 10 + 2 * (k % 2), :]
                if k == 0:
                    dve.tensor_copy(tile[:, 11, :], src).then_inc(S["x1_sum"], 1)
                else:
                    dve.wait_ge(S["x1_sum"], k)
                    dve.tensor_tensor(tile[:, 11, :], tile[:, 11, :], src, ALU.add).then_inc(S["x1_sum"], 1)
            factor(S["n2_ms"], S["n2_root"], S["n2_rstd"], 0)
            dve.wait_ge(S["n2_bcast"], 1)
            for k in range(KT + 1):
                if k < KT:
                    if k >= 2:
                        dve.wait_ge(S["n2_ready"], k - 1)
                    dve.scalar_tensor_tensor(out=tile[:, 8 + k % 2, :], in0=xres[k], scalar=a_mlp[:, k:k + 1], in1=wk[0][:],
                                             op0=ALU.mult, op1=ALU.mult).then_inc(S["n2_scaled"], 1)
                if k:
                    dve.wait_ge(S["n2_hi"], k)
                    dve.scalar_tensor_tensor(out=h_lo[:, k - 1, :], in0=tile[:, 8 + (k - 1) % 2, :], scalar=mod[:, 23 + k:24 + k],
                                             in1=h_hi[:, k - 1, :].bitcast(F32), op0=ALU.add, op1=ALU.subtract
                                             ).then_inc(S["n2_ready"], 1)
            dve.wait_ge(S["n2_ready"], KT)

            with dve.Fori(0, QUARTERS) as q4:
                with dve.Fori(0, KT // 2) as t:
                    for s in range(2):
                        m = q4 * 8 + t * 2 + s
                        dve.wait_ge(S["hid_relu"], m + 1)
                        dve.tensor_tensor(tile[:, 10 + s, :], tile[:, 8 + s, :], tile[:, 8 + s, :], ALU.mult
                                          ).then_inc(S["hid_sq"], 1)
                        dve.wait_ge(S["hid_hi"], m + 1)
                        dve.sem_inc(S["relu_free"], 1)
                        dst = bass.ds(t * 2 + s, 1)
                        dve.tensor_tensor(u_lo[:, dst, :].rearrange("p a t -> p (a t)"), tile[:, 10 + s, :],
                                          u_hi[:, dst, :].rearrange("p a t -> p (a t)").bitcast(F32), ALU.subtract
                                          ).then_inc(S["hid_ready"], 1)
                        dve.wait_ge(S["hid_ready"], m + 1)
                with dve.Fori(0, KT // 2) as t:
                    for s in range(2):
                        b = (N_MLP + 8 + s) % 2
                        m = q4 * 8 + t * 2 + s
                        dve.wait_ge(S["block_done"], q4 * 16 + t * 2 + (N_MLP + 8 + s + 1))
                        xk = tile[:, bass.ds(t * 2 + s, 1), :].rearrange("p a t -> p (a t)")
                        dve.scalar_tensor_tensor(out=xk, in0=acc[b][:], scalar=mod[:, bass.ds(t * 2 + (40 + s), 1)], in1=xk,
                                                 op0=ALU.mult, op1=ALU.add).then_inc(S["x2_ready"], 1)
                        dve.wait_ge(S["x2_ready"], m + 1)
                        dve.sem_inc(acc_free[b], 1)

            squares_sum(S["f_sq"], S["f_sum"])
            factor(S["f_ms"], S["f_root"], S["f_rstd"], 0)
            dve.wait_ge(S["f_bcast"], 1)
            for k in range(KT):
                dve.scalar_tensor_tensor(out=xres[k], in0=xres[k], scalar=par[:, C_GFIN + k:C_GFIN + k + 1], in1=wk[0][:],
                                         op0=ALU.mult, op1=ALU.mult).then_inc(S["f_ready"], 1)


def blocks(w):
    k, m = w.shape
    return w.reshape(k // P, P, m // P, P).transpose(2, 1, 0, 3).reshape(m // P, P, (k // P) * P)


def shape_constants():
    n = SW_PAIRS * 2 + DA_HEADS
    slopes = np.exp2(-8.0 * np.arange(1, n + 1) / n).astype(np.float32)
    con = np.zeros((P, K_ALL), np.float32)
    con[:, K_ID:K_ID + P] = np.eye(P, dtype=np.float32)
    con[:, K_TRI:K_TRI + P] = np.triu(np.ones((P, P), np.float32))
    p = np.arange(P)[:, None]
    x = np.arange(256)[None, :]
    ok = (x // 64 >= p // 64 + 1) & (x // 64 <= p // 64 + 2)
    dist = np.abs(P + p - x).astype(np.float32)
    sw = np.zeros((SW_PAIRS, P, 2 * 256), np.float32)
    for j in range(SW_PAIRS):
        for g in range(2):
            sw[j, :, g * 256:(g + 1) * 256] = np.where(ok, -slopes[4 * g + j] / np.float32(SCALE) * dist, np.float32(NEG))
    x = np.arange(T)[None, :] - (T - P)
    ok = x // 64 <= p // 64
    dist = np.abs(p - x).astype(np.float32)
    tab = np.stack([np.where(ok, -slopes[8 + h] / np.float32(SCALE) * dist, np.float32(NEG)) for h in range(DA_HEADS)])
    return con, tab.astype(np.float32), sw


def kernel(**inputs):
    import concourse.bacc as bacc
    from concourse.bass_utils import run_bass_kernel_spmd as run

    a = {k: np.asarray(v) for k, v in inputs.items()}
    cols = lambda v: v.reshape(-1, P).T
    w = a["w_in"][0]
    da_q, da_k, da_v = (w[:, 512 * i:512 * (i + 1)] for i in range(3))
    at = 1536
    sw_q, sw_k, sw_v = w[:, at:at + 512], w[:, at + 512:at + 640], w[:, at + 640:at + 768]
    at += 768
    z, xs = w[:, at:at + 1024], w[:, at + 1024:at + 2048]
    bs, cs = w[:, at + 2048:at + 2304], w[:, at + 2304:at + 2560]
    at += 2560
    dt_cols = w[:, at:at + P]
    gates = [w[:, at + 16 + D * i:at + 16 + D * (i + 1)] for i in range(3)]
    pair = lambda v, ax: np.concatenate([np.take(v, range(64 * h, 64 * h + 64), ax) for j in range(4) for h in (j, j + 4)], ax)
    sw_q = pair(sw_q, 1)
    wb = a["w_branch"][0]
    wab = np.concatenate([wb[0:512], pair(wb[512:1024], 0)], 0)
    stream = []
    dq, dk, dv = (blocks(v) for v in (da_q, da_k, da_v))
    for h in range(DA_HEADS):
        stream += [dv[h], dk[h], dq[h]]
    stream += [blocks(sw_v)[0], blocks(sw_k)[0], *blocks(sw_q)]
    ga, gb, gc = (blocks(v) for v in gates)
    bab, bc = blocks(wab), blocks(wb[1024:2048])
    for m in range(KT):
        stream += [ga[m], gb[m], bab[m]]
    stream += [blocks(dt_cols)[0]]
    bz, bx, bbs, bcs = (blocks(v) for v in (z, xs, bs, cs))
    for g in range(GROUPS):
        stream += [bbs[g], bcs[g], *bx[4 * g:4 * g + 4], *bz[4 * g:4 * g + 4]]
    for m in range(KT):
        stream += [gc[m], bc[m]]
    stream += [*blocks(a["w_out"][0])]
    w1, w2 = blocks(a["w_mlp1"][0]), a["w_mlp2"][0]
    for q in range(QUARTERS):
        stream += [*w1[8 * q:8 * q + 8], *blocks(w2[D * q:D * (q + 1)])]
    stream = np.stack(stream)
    assert len(stream) == N_ALL

    conv = np.concatenate([a["ssm_conv_w"][0], a["ssm_conv_b"]], 0)
    conv = conv.T.reshape(12, P, 5)
    conv = np.concatenate([conv[[8 + g, 10 + g, 4 * g, 4 * g + 1, 4 * g + 2, 4 * g + 3]] for g in range(GROUPS)])
    every = lambda v: np.broadcast_to(v.reshape(1, -1), (P, v.size))
    par = np.ascontiguousarray(np.concatenate([
        cols(a["norm_mix_g"][0]), cols(a["norm_mlp_g"][0]), cols(a["final_norm_g"]), cols(a["ssm_norm_g"][0]),
        cols(a["ada_b"][0]), conv.transpose(1, 0, 2).reshape(P, 60), cols(np.repeat(a["ssm_D"][0], HD)),
        cols(a["da_subln_g"][0]), every(a["ssm_dt_bias"][0]), every(a["ssm_A_log"][0]), every(a["sw_sinks"][0])], 1))
    lam_v = np.ascontiguousarray(np.concatenate([
        every(a["da_lambda_q1"][0]), every(a["da_lambda_k1"][0]), every(a["da_lambda_q2"][0]), every(a["da_lambda_k2"][0]),
    ], 1))
    con, tab, sw = shape_constants()
    arrays = {
        "x_t": np.ascontiguousarray(a["x"][0].T).reshape(KT, P, T),
        "c_t": np.ascontiguousarray(cols(a["c"][0])),
        "ada_blocks": np.ascontiguousarray(blocks(a["ada_w"][0])),
        "w_stream": stream,
        "params": par,
        "constants": con,
        "da_bias": tab,
        "sw_bias": sw,
        "lambda_vectors": lam_v,
    }
    nc = bacc.Bacc("TRN2", target_bir_lowering=False, num_devices=1)
    aps = [nc.dram_tensor(n, v.shape, F32, kind="ExternalInput").ap() for n, v in arrays.items()]
    out = nc.dram_tensor("out_t", [KT, P, T], F32, kind="ExternalOutput").ap()
    build(nc, *aps, out)
    r = run(nc, [arrays], core_ids=[0])
    got = r.results[0]["out_t"]
    return np.ascontiguousarray(got.reshape(D, T).T)[None]
```

```python
from contextlib import ExitStack, contextmanager

import numpy as np
import concourse.bass as bass
from concourse import mybir

F32 = mybir.dt.float32
F32R = mybir.dt.float32r
ALU = mybir.AluOpType
ACT = mybir.ActivationFunctionType

P = 128
T = 1024
D = 1024
KT = D // P
NT = T // P
HALF = 512
EPS = 1e-6
DA_HEADS = 4
SW_PAIRS = 4
GROUPS = 2
GH = 8
HD = 64
HEADS = GROUPS * GH
LAM_INIT = 0.8 - 0.6 * 1.0
DA_OUT = 1.0 - LAM_INIT
SCALE = HD ** -0.5
NEG = -1.0e30

N_DA = 0
N_SW = N_DA + 3 * DA_HEADS
N_DT = N_SW + 2 + SW_PAIRS
N_AB = N_DT + 1
N_SSM = N_AB + 3 * KT
N_C = N_SSM + 10 * GROUPS
N_OUT = N_C + 2 * KT
N_MLP = N_OUT + KT
QUARTERS = 4
N_ALL = N_MLP + 16 * QUARTERS

C_GMIX, C_GMLP, C_GFIN, C_GSSM = 0, 8, 16, 24
C_ADAB = 32
C_CONV = C_ADAB + 48
C_D = C_CONV + 60
C_SUBLN = C_D + 8
C_DTB = C_SUBLN + 1
C_ALOG = C_DTB + HEADS
C_SINK = C_ALOG + HEADS
C_ALL = C_SINK + 8
K_ID, K_TRI, K_ALL = 0, P, 2 * P

PIECES = [(i, half) for i in range(NT) for half in range(1 + i // 4)]
NP_ = len(PIECES)


class Steps:

    def __init__(self, eng, sem):
        self.eng, self.sem, self.base, self.k = eng, sem, 0, 0

    def mark(self, ins):
        ins.then_inc(self.sem, 1)
        self.k += 1

    def settle(self):
        self.eng.wait_ge(self.sem, self.base + self.k)

    @contextmanager
    def loop(self, i, per, trips):
        old, start = self.base, self.k
        self.base = old + i * per
        yield
        assert self.k - start == per, (self.k - start, per)
        self.base, self.k = old, start + per * trips


def flat(ap):
    return ap.rearrange("p a b -> p (a b)")


def build(nc, x_in, c_in, ada_in, w_in, par_in, con_in, da_tab, sw_tab, lam_v, out):
    with ExitStack() as ctx:
        def sb(name, shape, dt=F32):
            return ctx.enter_context(nc.sbuf_tensor(name, shape, dt))

        def sem(name):
            return ctx.enter_context(nc.semaphore(name))

        h_hi = sb("h_hi", [P, KT, T], F32R)
        h_lo = sb("h_lo", [P, KT, T], F32R)
        u_hi = sb("u_hi", [P, KT, T], F32R)
        u_lo = sb("u_lo", [P, KT, T], F32R)
        w_hi = [sb(f"w_hi{i}", [P, KT, P], F32R) for i in range(2)]
        w_lo = [sb(f"w_lo{i}", [P, KT, P], F32R) for i in range(2)]
        raw = sb("raw", [P, 2, KT * P])
        tile = sb("tile", [P, 13, T])
        con = sb("con", [P, K_ALL])
        par = sb("par", [P, C_ALL])
        c_sb = sb("c_sb", [P, KT])
        ones = sb("ones", [P, 1])
        eps = sb("eps", [P, 1])
        mod = sb("mod", [P, 48])
        a_mix = sb("a_mix", [P, KT])
        a_mlp = sb("a_mlp", [P, KT])
        a_da = sb("a_da", [P, 1])
        rms = sb("rms", [P, 6, KT])
        rstd = sb("rstd", [P, KT])
        lam = sb("lam", [P, 8])
        mx = sb("mx", [P, 4])
        mxp = sb("mxp", [P, 4])
        sm = sb("sm", [P, 4])
        rc = sb("rc", [P, 4])
        swm = sb("swm", [P, 16])
        swn = sb("swn", [P, 16])
        sws = sb("sws", [P, 16])
        swe = sb("swe", [P, 16])
        swd = sb("swd", [P, 16])
        swr = sb("swr", [P, 16])
        negsink = sb("negsink", [P, 8])
        exp_a = sb("exp_a", [P, HEADS])
        gpar = sb("gpar", [P, 34])

        dtm = tile[:, 12, :].rearrange("p (n x) -> p n x", n=8)
        id_ = con[:, K_ID:K_ID + P]
        tri = con[:, K_TRI:K_TRI + P]

        acc = [ctx.enter_context(nc.psum_tensor(f"acc{i}", [P, T], F32)) for i in range(2)]
        wk = [ctx.enter_context(nc.psum_tensor(f"wk{i}", [P, T], F32)) for i in range(2)]
        bank = [wk[0][:, 0:HALF], wk[0][:, HALF:T], wk[1][:, 0:HALF], wk[1][:, HALF:T]]

        
        merged_d = nc.dram_tensor("merged_d", [KT, P, T], F32, kind="Internal").ap()
        o_d = nc.dram_tensor("o_d", [DA_HEADS, P, T], F32, kind="Internal").ap()
        cs_d = nc.dram_tensor("cs_d", [P, P], F32, kind="Internal").ap()

        S = {}
        for name in """par_in lam_in con_in c_in w_in0 w_in1 x_in0 x_in1 x_in2 x_in3 ada_in0 ada_in1
            split_hi split_ready block_done acc_free0 acc_free1
            mod_done sq_ready sq_used ms_ready root_ready rstd_ready bcast_ready h_scaled h_hi_ready h_ready
            dve_own gates_free relu_free da_tab_in
            qkv_ready v_turned v_tok scored biased negmax exped weighted turned turned_sb pv_done o_copied
            da_clipped da_sq da_ms da_root da_rstd da_bcast da_scaled da_hi u_ready lam_dots lam_exps
            o_saved o_back sw_split sw_tab_in sw_qkv sw_vt sw_vtok sw_scored sw_biased sw_negmax sw_exped sw_weighted sw_turned sw_turned_sb
            sw_out sw_hi sw_used
            gate_ready ab_free ab_ready merged_out merged_saved
            dt_copied dt_turned dt_abs dt_exp dt_da cs_ready cs_copied cs_saved dt_diff dt_decays
            conv_first conv_done conv_silu csb_in diff_ready relu_ready l_ready e_ready x_turned g_ready btok_ready
            g_masked xd_ready m_ready s_ready y_ready y_taken state_ready
            z_silu z_used y_gated ssm_sq ssm_ms ssm_root ssm_rstd ssm_bcast ssm_scaled ssm_hi y_split
            c_gate c_free merged_in0 merged_in1 merged_all merged_hi merged_ready
            x2_in x1_ready x1_sq x1_sum n2_ms n2_root n2_rstd n2_bcast n2_scaled n2_hi n2_ready
            hid_relu hid_sq hid_hi hid_ready x2_ready f_sq f_sum f_ms f_root f_rstd f_bcast f_ready out_saved
            mod_rest ada_freed""".split():
            S[name] = sem(name)
        w_in_s = [S["w_in0"], S["w_in1"]]
        x_in_s = [S["x_in0"], S["x_in1"], S["x_in2"], S["x_in3"]]
        ada_s = [S["ada_in0"], S["ada_in1"]]
        acc_free = [S["acc_free0"], S["acc_free1"]]
        merged_s = [S["merged_in0"], S["merged_in1"]]

        xres = [tile[:, k, :] for k in range(KT)]
        block = ctx.enter_context(nc.Block())

        @block.sync
        def _(sp):
            sp.dma_start(par[:], par_in).then_inc(S["par_in"], 16)
            sp.dma_start(tile[:, 11, 0:4 * HD], lam_v).then_inc(S["lam_in"], 16)
            sp.dma_start(c_sb[:], c_in).then_inc(S["c_in"], 16)
            for q in range(4):
                sp.dma_start(tile[:, 2 * q:2 * q + 2, :],
                             x_in[2 * q:2 * q + 2].rearrange("k p t -> p k t")).then_inc(x_in_s[q], 16)
                if q == 0:
                    sp.dma_start(con[:], con_in).then_inc(S["con_in"], 16)
            for n in range(2):
                sp.dma_start(raw[:, n], w_in[n]).then_inc(w_in_s[n], 16)
            for b in range(16):
                if b >= 2:
                    sp.wait_ge(S["mod_done"], b - 1)
                sp.dma_start(tile[:, 8 + b % 2, :], ada_in[b]).then_inc(ada_s[b % 2], 16)
            with sp.Fori(0, (N_ALL - 3) // 2) as i:
                for b in range(2):
                    sp.wait_ge(S["split_ready"], i * 2 + b + 1)
                    sp.dma_start(raw[:, b], w_in[bass.ds(i * 2 + 2 + b, 1)].rearrange("a p c -> (a p) c")
                                 ).then_inc(w_in_s[b], 16)
            sp.wait_ge(S["split_ready"], N_ALL - 2)
            sp.dma_start(raw[:, 0], w_in[N_ALL - 1]).then_inc(w_in_s[0], 16)

        @block.gpsimd
        def _(pool):
            def split(b, n, trip, first):
                pool.wait_ge(w_in_s[b], trip * 16 + 16)
                if not first:
                    pool.wait_ge(S["block_done"], n - 1)
                pool.nop(nofuse=True)
                pool.tensor_scalar(flat(w_hi[b][:]), raw[:, b], 1.0, 1.0, ALU.mult, ALU.mult).then_inc(S["split_hi"], 1)
                pool.wait_ge(S["split_hi"], n + 1)
                pool.tensor_tensor(flat(w_lo[b][:]), raw[:, b], flat(w_hi[b][:].bitcast(F32)),
                                   ALU.subtract).then_inc(S["split_ready"], 1)

            split(0, 0, 0, True)
            split(1, 1, 0, True)
            with pool.Fori(0, (N_ALL - 3) // 2) as i:
                for b in range(2):
                    split(b, i * 2 + 2 + b, i + 1, False)
            split(0, N_ALL - 1, (N_ALL - 1) // 2, False)

        @block.tensor
        def _(pe):
            def step(b, pair, k, rhs_hi, rhs_lo, psum=None):
                if k == 0:
                    pe.wait_ge(S["split_ready"], pair * 2 + b + 1)
                    pe.wait_ge(acc_free[b], pair + 1)
                mm = terms(b, k, rhs_hi, rhs_lo, k, acc[b], k == 0, k == KT - 1)
                if k == KT - 1:
                    mm.then_inc(S["block_done"], 1)

            def terms(b, k, rhs_hi, rhs_lo, kr, psum, first, last):
                for t, (w, r) in enumerate(((w_hi, rhs_hi), (w_hi, rhs_lo), (w_lo, rhs_hi))):
                    for half in range(2):
                        cols = slice(half * HALF, (half + 1) * HALF)
                        mm = pe.matmul(psum[:, cols], w[b][:, k, :], r[:, kr, cols],
                                       start=first and t == 0, stop=last and t == 2)
                return mm

            def dense(b, pair, rhs_hi, rhs_lo, moving=None):
                pe.wait_ge(S["split_ready"], pair * 2 + b + 1)
                pe.wait_ge(acc_free[b], pair + 1)
                for k in range(KT):
                    if moving is not None:
                        pe.wait_ge(moving[0], moving[1] + k + 1)
                    mm = terms(b, k, rhs_hi, rhs_lo, k, acc[b], k == 0, k == KT - 1)
                mm.then_inc(S["block_done"], 1)

            def row_means(total, signal, at=0, psum=None):
                for c in range(NT):
                    mm = pe.matmul((psum or bank[3])[:, at + c:at + c + 1], total[:, c * P:(c + 1) * P], ones[:, 0:1],
                                   start=True, stop=True)
                mm.then_inc(signal, 1)

            def broadcast(signal, psum=None):
                for c in range(NT):
                    mm = pe.matmul((psum or wk[0])[:, c * P:(c + 1) * P], rstd[:, c:c + 1].to_broadcast([P, P]), id_,
                                   start=True, stop=True)
                mm.then_inc(signal, 1)

            def modulation(b, slot, trip):
                pe.wait_ge(ada_s[slot], trip * 16 + 16)
                for k in range(KT):
                    mm = pe.matmul(bank[2][:, b:b + 1], tile[:, 8 + slot, k * P:(k + 1) * P], c_sb[:, k:k + 1],
                                   start=k == 0, stop=k == KT - 1)
                mm.then_inc(S["mod_done"], 1)

            pe.wait_ge(S["c_in"], 16)
            for b in range(16):
                modulation(b, b % 2, b // 2)
            pe.wait_ge(S["sq_used"], KT)
            row_means(tile[:, 11, :], S["ms_ready"])
            pe.wait_ge(S["rstd_ready"], 1)
            pe.wait_ge(S["con_in"], 16)
            broadcast(S["bcast_ready"])

            def turn_v(b, triple):
                pe.wait_ge(S["qkv_ready"], triple * 3 + 1)
                for j in range(NT):
                    mm = pe.transpose(acc[b][:, j * P:(j + 1) * P], tile[:, 10, j * P:(j + 1) * P], id_)
                mm.then_inc(S["v_turned"], 1)

            dense(0, 0, h_hi, h_lo, (S["h_ready"], 0))
            dense(1, 0, h_hi, h_lo)
            turn_v(0, 0)
            dense(0, 1, h_hi, h_lo)

            def da_head(t, s):
                head = t * 2 + s
                kt, qt, vt = (0, 11)[s], (1, 2)[s], (3, 12)[s]
                done = [0]

                def steps(count):
                    for _ in range(count):
                        n = 3 * (s + 1) + done[0] // KT
                        step(n % 2, t * 3 + n // 2, done[0] % KT, h_hi, h_lo)
                        done[0] += 1

                def scores(i, m):
                    if i or m:
                        pe.wait_ge(S["biased"], head * 16 + 2 * i + m)
                    rows = slice(m * HD, (m + 1) * HD)
                    for lo in range(0, (i + 1) * P, HALF):
                        hi = min(lo + HALF, (i + 1) * P)
                        mm = pe.matmul(wk[0][:, lo:hi], tile[rows, qt, i * P:(i + 1) * P], tile[rows, kt, lo:hi],
                                       start=True, stop=True)
                    mm.then_inc(S["scored"], 1)

                def turn(i, half):
                    n = PIECES.index((i, half))
                    pe.wait_ge(S["weighted"], head * 8 + i + 1)
                    if n:
                        pe.wait_ge(S["turned_sb"], head * NP_ + n)
                    src = (5, 7)[i % 2]
                    for j in range(4 * half, min(4 * half + 4, i + 1)):
                        mm = pe.transpose(bank[2][:, (j % 4) * P:(j % 4 + 1) * P], tile[:, src, j * P:(j + 1) * P], id_)
                    mm.then_inc(S["turned"], 1)

                def attend(i, half):
                    n = PIECES.index((i, half))
                    pe.wait_ge(S["turned_sb"], head * NP_ + n + 1)
                    if i == 4 and half == 0:
                        pe.wait_ge(S["o_copied"], head * 2 + 1)
                    for j in range(4 * half, min(4 * half + 4, i + 1)):
                        at = (n % 2) * HALF + (j % 4) * P
                        mm = pe.matmul(bank[3][:, (i % 4) * P:(i % 4 + 1) * P], tile[:, vt, j * P:(j + 1) * P],
                                       tile[:, 9, at:at + P], start=j == 0, stop=j == i)
                    mm.then_inc(S["pv_done"], 1)

                pe.wait_ge(S["v_tok"], head + 1)
                pe.wait_ge(S["qkv_ready"], head * 3 + 3)
                for i in range(NT):
                    two = i > 4
                    steps(1)
                    if i == 4:
                        turn_v((3 * (s + 1)) % 2, head + 1)
                    if i > 5:
                        attend(i - 2, 1)
                    scores(i, 0)
                    steps(1)
                    scores(i, 1)
                    if i:
                        turn(i - 1, 0)
                    if i > 2:
                        steps(1)
                    if i:
                        attend(i - 1, 0)
                    if two:
                        turn(i - 1, 1)
                attend(NT - 2, 1)
                steps(1)
                turn(NT - 1, 0)
                steps(1)
                attend(NT - 1, 0)
                turn(NT - 1, 1)
                steps(1)
                assert done[0] == 3 * KT
                attend(NT - 1, 1)

            with pe.Fori(0, DA_HEADS // 2) as t:
                for s in range(2):
                    da_head(t, s)

            def sw_pair(t, s):
                j = t * 2 + s
                qt = (1, 2)[s]
                done = [0]

                def steps(count):
                    for _ in range(count):
                        n = N_SW + 3 + s
                        step(n % 2, t + n // 2, done[0], h_hi, h_lo)
                        done[0] += 1

                def scores(i):
                    pe.wait_ge(S["sw_biased"], j * NT + i + 1)
                    lo = max(i - 1, 0) * P
                    w = (i + 1) * P - lo
                    for g in range(2):
                        rows = slice(g * HD, (g + 1) * HD)
                        mm = pe.matmul(bank[g][:, 256 - w:256], tile[rows, qt, i * P:(i + 1) * P],
                                       tile[rows, 0, lo:lo + w], start=True, stop=True)
                    mm.then_inc(S["sw_scored"], 1)

                def turn(i):
                    pe.wait_ge(S["sw_weighted"], j * NT + i + 1)
                    pe.wait_ge(S["sw_turned_sb"], j * NT + i + 1)
                    for g in range(2):
                        for kb in range(0 if i else 1, 2):
                            at = (g * 2 + kb) * P
                            src = (i % 2) * HALF + g * 256 + kb * P
                            mm = pe.transpose(bank[2][:, at:at + P], tile[:, 5 + (i % 4) // 2, src:src + P], id_)
                    mm.then_inc(S["sw_turned"], 1)

                def attend(i):
                    pe.wait_ge(S["sw_turned_sb"], j * NT + i + 2)
                    if i % 4 == 0:
                        pe.wait_ge(S["sw_split"], j * 2 + i // 4 + 1)
                    for g in range(2):
                        rows = slice(g * HD, (g + 1) * HD)
                        for kb in range(0 if i else 1, 2):
                            jj = i - 1 + kb
                            at = (i % 2) * HALF + (g * 2 + kb) * P
                            mm = pe.matmul(bank[3][rows, (i % 4) * P:(i % 4 + 1) * P],
                                           tile[:, 3, jj * P + g * HD:jj * P + (g + 1) * HD],
                                           tile[:, 9, at:at + P], start=kb == (0 if i else 1), stop=kb == 1)
                    mm.then_inc(S["sw_out"], 1)

                steps(2)
                pe.wait_ge(S["sw_qkv"], j + 1)
                for i in range(NT):
                    scores(i)
                    if i >= 2:
                        turn(i - 2)
                    steps(1 if i < 6 else 0)
                    if i >= 2:
                        attend(i - 2)
                    if i == 4:
                        pe.wait_ge(S["da_sq"], j * 2 + 2)
                        row_means(tile[:, 8, :], S["da_ms"], 0, acc[s])
                        row_means(tile[:, 12, :], S["da_ms"], NT, acc[s])
                turn(NT - 2)
                attend(NT - 2)
                pe.wait_ge(S["da_rstd"], j + 1)
                broadcast(S["da_bcast"], acc[s])
                turn(NT - 1)
                attend(NT - 1)
                pe.wait_ge(S["da_scaled"], j + 1)

            pe.wait_ge(S["v_tok"], DA_HEADS + 1)
            pe.wait_ge(S["o_copied"], 2 * DA_HEADS)
            with pe.Fori(0, SW_PAIRS // 2) as t:
                for s in range(2):
                    sw_pair(t, s)

            pe.wait_ge(S["sw_qkv"], SW_PAIRS + 1)
            pe.wait_ge(S["sw_biased"], SW_PAIRS * NT + 1)
            for c in range(NT):
                mm = pe.transpose(bank[0][:, c * HEADS:(c + 1) * HEADS], tile[0:HEADS, 1, c * P:(c + 1) * P], id_[0:HEADS, 0:HEADS])
            mm.then_inc(S["dt_turned"], 1)
            pe.wait_ge(S["sw_turned_sb"], SW_PAIRS * NT + 1)

            with pe.Fori(0, KT // 2) as t:
                for s in range(2):
                    for q in range(3):
                        n = N_AB + 3 * s + q
                        pair = t * 3 + n // 2
                        if q < 2:
                            dense(n % 2, pair, h_hi, h_lo)
                        else:
                            pe.wait_ge(S["split_ready"], pair * 2 + n % 2 + 1)
                            pe.wait_ge(S["ab_free"], t * 2 + s + 1)
                            for k in range(KT):
                                mm = terms(n % 2, k, u_hi, u_lo, k, wk[0] if k < 4 else acc[n % 2],
                                           k % 4 == 0, k % 4 == 3)
                                if k == 3:
                                    pe.wait_ge(acc_free[n % 2], pair + 1)
                            mm.then_inc(S["block_done"], 1)
                    for q in range(4):
                        pe.wait_ge(ada_s[q % 2], t * 64 + (8 + 2 * s + q // 2) * 16 + 16)
                        for k in range(KT):
                            mm = pe.matmul(bank[2][:, bass.ds(t * 8 + (16 + 4 * s + q), 1)],
                                           tile[:, 8 + q % 2, k * P:(k + 1) * P], c_sb[:, k:k + 1],
                                           start=k == 0, stop=k == KT - 1)
                        mm.then_inc(S["mod_done"], 1)

            pe.wait_ge(S["dt_da"], 1)
            pe.wait_ge(S["ab_free"], KT + 1)
            a_tok = dtm[:, 0, :]
            pe.matmul(bank[1][:, 0:P], a_tok, tri, start=True, stop=True)
            pe.matmul(bank[1][:, P:2 * P], tri, a_tok, start=True, stop=True)
            pe.matmul(bank[1][:, 2 * P:3 * P], ones[:].to_broadcast([P, P]), a_tok, start=True, stop=True
                      ).then_inc(S["cs_ready"], 1)

            def dense_and_norm(b, pair, g):
                for k in range(KT):
                    step(b, pair, k, h_hi, h_lo)
                    if k == 3:
                        pe.wait_ge(S["ssm_sq"], g * 4 + 4)
                        row_means(tile[:, 10, :], S["ssm_ms"])
                pe.wait_ge(S["ssm_rstd"], g + 1)
                broadcast(S["ssm_bcast"])

            for g in range(GROUPS):
                def turn_chunk(c):
                    cols = slice(c * P, (c + 1) * P)
                    if c:
                        pe.wait_ge(S["xd_ready"], g * 16 + 2 * c)
                        pe.wait_ge(S["btok_ready"], g * NT + c)
                        pe.wait_ge(S["g_masked"], g * NT + c)
                    for j in range(4):
                        mm = pe.transpose(bank[0][:, j * P:(j + 1) * P], tile[:, j, cols], id_)
                    mm.then_inc(S["x_turned"], 1)
                    pe.transpose(bank[1][:, 0:P], tile[:, 4, cols], id_)
                    pe.matmul(bank[1][:, P:2 * P], tile[:, 4, cols], tile[:, 5, cols], start=True, stop=True
                              ).then_inc(S["g_ready"], 1)

                def chunk_state(c):
                    pe.wait_ge(S["xd_ready"], g * 16 + 2 * c + 2)
                    pe.wait_ge(S["btok_ready"], g * NT + c + 1)
                    pe.wait_ge(S["state_ready"], g * (NT + 1) + c + 1)
                    pe.matmul(bank[2][:, :], tile[:, 11, HALF:HALF + P], tile[:, 12, 0:HALF], start=True, stop=True
                              ).then_inc(S["s_ready"], 1)

                def chunk_out(c):
                    pe.wait_ge(S["m_ready"], g * 16 + 2 * c + 2)
                    pe.wait_ge(S["state_ready"], g * (NT + 1) + c + 1)
                    if c:
                        pe.wait_ge(S["y_taken"], g * NT * 4 + 4 * c)
                    for r in range(GH):
                        rows = slice((r % 2) * HD, (r % 2 + 1) * HD)
                        o = bank[3][rows, (r // 2) * P:(r // 2 + 1) * P]
                        xd = (c % 2) * HALF + r * HD
                        pe.matmul(o, tile[:, 10, xd:xd + HD], tile[:, 6 + c % 2, r * P:(r + 1) * P],
                                  start=True, stop=False)
                        mm = pe.matmul(o, tile[:, 11, r * HD:(r + 1) * HD], tile[:, 8 + c % 2, r * P:(r + 1) * P],
                                       start=False, stop=True)
                    mm.then_inc(S["y_ready"], 1)

                done = [0]

                def steps(count):
                    for _ in range(count):
                        n = N_SSM + 10 * g + 6 + done[0] // KT
                        step(n % 2, n // 2, done[0] % KT, h_hi, h_lo)
                        done[0] += 1

                n = N_SSM + 10 * g
                if g:
                    dense_and_norm(n % 2, n // 2, g - 1)
                else:
                    dense(n % 2, n // 2, h_hi, h_lo)
                for n in range(n + 1, n + 6):
                    dense(n % 2, n // 2, h_hi, h_lo)
                steps(5)
                if g:
                    pe.wait_ge(S["ssm_scaled"], g * 4)
                else:
                    pe.wait_ge(S["cs_copied"], 2)
                    pe.wait_ge(S["mod_rest"], 1)
                pe.wait_ge(S["conv_silu"], g * 6 + 6)
                turn_chunk(0)
                chunk_state(0)
                for c in range(NT):
                    if c + 1 < NT:
                        turn_chunk(c + 1)
                    chunk_out(c)
                    steps(1)
                    if c + 1 < NT:
                        chunk_state(c + 1)
                    steps(1 if c < 3 else 0)
                assert done[0] == 2 * KT
                for n in range(N_SSM + 10 * g + 8, N_SSM + 10 * g + 10):
                    dense(n % 2, n // 2, h_hi, h_lo)

            def merge_c(m, t, first):
                n = N_C + 2 * m
                if first:
                    dense_and_norm(n % 2, n // 2, GROUPS - 1)
                else:
                    dense(n % 2, t + n // 2, h_hi, h_lo)
                dense((n + 1) % 2, t + (n + 1) // 2, u_hi, u_lo, (S["y_split"], 0) if first else None)

            merge_c(0, 0, True)
            with pe.Fori(0, KT - 1) as t:
                merge_c(1, t, False)

            with pe.Fori(0, KT // 2) as t:
                for s in range(2):
                    n = N_OUT + s
                    dense(n % 2, t + n // 2, u_hi, u_lo, (S["merged_ready"], 0) if s == 0 else None)
            pe.wait_ge(S["x1_sum"], KT)
            row_means(tile[:, 11, :], S["n2_ms"])
            pe.wait_ge(S["n2_rstd"], 1)
            broadcast(S["n2_bcast"])

            with pe.Fori(0, QUARTERS) as q4:
                with pe.Fori(0, KT // 2) as t:
                    for s in range(2):
                        n = N_MLP + s
                        dense(n % 2, q4 * 8 + t + n // 2, h_hi, h_lo, (S["n2_ready"], 0) if s == 0 else None)
                with pe.Fori(0, KT // 2) as t:
                    for s in range(2):
                        n = N_MLP + 8 + s
                        dense(n % 2, q4 * 8 + t + n // 2, u_hi, u_lo, (S["hid_ready"], q4 * 8) if s == 0 else None)
            pe.wait_ge(S["f_sum"], KT)
            row_means(tile[:, 11, :], S["f_ms"])
            pe.wait_ge(S["f_rstd"], 1)
            broadcast(S["f_bcast"])

        @block.scalar
        def _(act):
            act.sem_inc(S["o_saved"], 16)
            act.sem_inc(S["merged_saved"], 16)

            def root(width, signal):
                act.activation(rms[:, 1, 0:NT], rms[:, 0, 0:NT], ACT.Sqrt, bias=eps[:, 0:1], scale=1.0 / width
                               ).then_inc(signal, 1)

            for k in range(KT):
                act.wait_ge(x_in_s[k // 2], 16)
                if k >= 2:
                    act.wait_ge(S["sq_used"], k - 1)
                act.activation(tile[:, 10 + 2 * (k % 2), :], xres[k], ACT.Square).then_inc(S["sq_ready"], 1)
            act.wait_ge(S["lam_dots"], 2)
            act.activation(lam[:, 2:4], lam[:, 0:2], ACT.Exp).then_inc(S["lam_exps"], 1)
            act.wait_ge(S["root_ready"], 1)
            root(D, S["root_ready"])
            for k in range(KT):
                act.wait_ge(S["h_scaled"], k + 1)
                act.activation(h_hi[:, k, :], xres[k], ACT.Identity, bias=mod[:, k:k + 1]).then_inc(S["h_hi_ready"], 1)

            def triple_v(b, triple):
                act.wait_ge(S["block_done"], triple * 3 + 1)
                act.activation(tile[:, 10, :], acc[b][:], ACT.Copy).then_inc(S["qkv_ready"], 1)

            def triple_v_tok(b, dst, triple):
                act.wait_ge(S["v_turned"], triple + 1)
                act.activation(tile[:, dst, :], acc[b][:], ACT.Copy).then_inc(S["v_tok"], 1)
                act.wait_ge(S["v_tok"], triple + 1)
                act.sem_inc(acc_free[b], 1)

            def triple_kq(b, q, dst, triple):
                act.wait_ge(S["block_done"], triple * 3 + q + 1)
                act.activation(tile[:, dst, :], acc[b][:], ACT.Copy).then_inc(S["qkv_ready"], 1)
                act.wait_ge(S["qkv_ready"], triple * 3 + q + 1)
                act.sem_inc(acc_free[b], 1)

            act.dma_start(tile[:, 4, :], da_tab[0]).then_inc(S["da_tab_in"], 16)
            triple_v(0, 0)
            triple_kq(1, 1, 0, 0)
            triple_v_tok(0, 3, 0)
            triple_kq(0, 2, 1, 0)

            def da_head(s, head):
                new = [(3 * (s + 1) + q) % 2 for q in range(3)]

                def exp(i, m):
                    act.wait_ge(S["negmax"], head * 16 + 2 * i + m + 1)
                    col = 2 * (i % 2) + m
                    src = tile[:, (5, 6, 7, 8)[col], 0:(i + 1) * P]
                    act.activation(src, src, ACT.Exp, bias=mx[:, col:col + 1], accum_out=sm[:, col:col + 1]
                                   ).then_inc(S["exped"], 1)

                def piece(i, half):
                    n = PIECES.index((i, half))
                    act.wait_ge(S["turned"], head * NP_ + n + 1)
                    if n >= 2:
                        act.wait_ge(S["pv_done"], head * NP_ + n - 1)
                    w = (min(4 * half + 4, i + 1) - 4 * half) * P
                    act.activation(tile[:, 9, (n % 2) * HALF:(n % 2) * HALF + w], bank[2][:, 0:w], ACT.Copy
                                   ).then_inc(S["turned_sb"], 1)

                def copy_o(half):
                    n = PIECES.index((4 * half + 3, half))
                    act.wait_ge(S["pv_done"], head * NP_ + n + 1)
                    act.activation(tile[:, 10, half * HALF:(half + 1) * HALF], bank[3], ACT.Copy
                                   ).then_inc(S["o_copied"], 1)

                for i in range(NT):
                    if i == 4:
                        act.wait_ge(S["o_saved"], head * 16 + 16)
                        triple_v(new[0], head + 1)
                    exp(i, 0)
                    if i:
                        piece(i - 1, 0)
                    exp(i, 1)
                    if i > 4:
                        piece(i - 1, 1)
                    if i == 4:
                        triple_v_tok(new[0], (12, 3)[s], head + 1)
                        copy_o(0)
                    if i == 6:
                        triple_kq(new[1], 1, (11, 0)[s], head + 1)
                act.dma_start(tile[:, 4, :], da_tab[bass.ds(head + 1, 1)].rearrange("a p x -> (a p) x")
                              ).then_inc(S["da_tab_in"], 16)
                piece(NT - 1, 0)
                piece(NT - 1, 1)
                triple_kq(new[2], 2, (2, 1)[s], head + 1)
                copy_o(1)
                act.wait_ge(S["o_copied"], head * 2 + 2)
                act.dma_start(o_d[bass.ds(head, 1)].rearrange("a p t -> (a p) t"), tile[:, 10, :]).then_inc(S["o_saved"], 16)

            with act.Fori(0, DA_HEADS // 2) as t:
                for s in range(2):
                    da_head(s, t * 2 + s)

            act.sem_inc(S["sw_qkv"], 1)
            act.sem_inc(S["sw_turned_sb"], 1)
            act.wait_ge(S["o_saved"], 16 * DA_HEADS + 16)
            with act.Fori(0, SW_PAIRS // 2) as t:
                for s in range(2):
                    j = t * 2 + s
                    act.dma_start(tile[:, 4, s * HALF:(s + 1) * HALF], sw_tab[bass.ds(j, 1)].rearrange("a p x -> (a p) x")
                                  ).then_inc(S["sw_tab_in"], 16)
                    act.wait_ge(S["da_hi"], j + 1)
                    act.dma_start(tile[:, 10, :], o_d[bass.ds(j, 1)].rearrange("a p t -> (a p) t")
                                  ).then_inc(S["o_back"], 16)

                    def exps(i):
                        act.wait_ge(S["sw_negmax"], j * NT + i + 1)
                        for g in range(2):
                            lo = (i % 2) * HALF + g * 256 + (0 if i else P)
                            src = tile[:, 5 + (i % 4) // 2, lo:(i % 2) * HALF + (g + 1) * 256]
                            col = 2 * (i % 4) + g
                            act.activation(src, src, ACT.Exp, bias=swn[:, col:col + 1], accum_out=sws[:, col:col + 1])
                        cols = slice(2 * (i % 4), 2 * (i % 4) + 2)
                        act.activation(swe[:, cols], swd[:, cols], ACT.Exp).then_inc(S["sw_exped"], 1)

                    def piece(i):
                        act.wait_ge(S["sw_turned"], j * NT + i + 1)
                        if i >= 2:
                            act.wait_ge(S["sw_out"], j * NT + i - 1)
                        for a, z in ((P, 256), (256 + P, HALF)) if i == 0 else ((0, HALF),):
                            last = act.activation(tile[:, 9, (i % 2) * HALF + a:(i % 2) * HALF + z],
                                                  bank[2][:, a:z], ACT.Copy)
                        last.then_inc(S["sw_turned_sb"], 1)

                    def out_hi(half):
                        act.wait_ge(S["sw_out"], j * NT + 4 * half + 4)
                        act.activation(u_hi[:, bass.ds(j + 4, 1), half * HALF:(half + 1) * HALF].rearrange("p a t -> p (a t)"),
                                       bank[3], ACT.Copy).then_inc(S["sw_hi"], 1)

                    for i in range(NT):
                        exps(i)
                        if i >= 2:
                            piece(i - 2)
                        if i == 2:
                            act.wait_ge(S["da_clipped"], j * 2 + 2)
                            act.activation(tile[:, 8, :], tile[:, 8, :], ACT.Square).then_inc(S["da_sq"], 1)
                            act.activation(tile[:, 12, :], tile[:, 10, :], ACT.Square, scale=2.0 ** -30).then_inc(S["da_sq"], 1)
                        if i == 5:
                            out_hi(0)
                    act.wait_ge(S["da_root"], j * 2 + 1)
                    root(P, S["da_root"])
                    n = N_SW + 3 + s
                    act.wait_ge(S["block_done"], j + N_SW + 4)
                    act.activation(tile[:, (2, 1)[s], :], acc[n % 2][:], ACT.Copy).then_inc(S["sw_qkv"], 1)
                    act.wait_ge(S["sw_qkv"], j + 2)
                    act.sem_inc(acc_free[n % 2], 1)
                    piece(NT - 2)
                    piece(NT - 1)
                    out_hi(1)
                    act.wait_ge(S["da_scaled"], j + 1)
                    act.activation(u_hi[:, bass.ds(j, 1), :].rearrange("p a t -> p (a t)"), tile[:, 12, :], ACT.Copy
                                   ).then_inc(S["da_hi"], 1)

            act.wait_ge(S["dt_abs"], 1)
            act.activation(dtm[:, 2, :], dtm[:, 1, :], ACT.Exp, scale=-1.0)
            act.activation(exp_a[:], par[:, C_ALOG:C_ALOG + HEADS], ACT.Exp).then_inc(S["dt_exp"], 1)

            with act.Fori(0, KT // 2) as t:
                for s in range(2):
                    m = t * 2 + s
                    for q in range(4):
                        b = 4 * s + q
                        act.wait_ge(S["mod_done"], t * 8 + (16 + b - 1))
                        act.dma_start(tile[:, 8 + q % 2, :], ada_in[bass.ds(t * 8 + (16 + b), 1)].rearrange("a p c -> (a p) c")
                                      ).then_inc(ada_s[q % 2], 16)
                        if q < 2:
                            n = N_AB + 3 * s + q
                            act.wait_ge(S["block_done"], m * 3 + (N_AB + q + 1))
                            if q == 0:
                                act.wait_ge(S["gates_free"], m + 1)
                            act.activation(tile[:, q, :], acc[n % 2][:], ACT.Sigmoid).then_inc(S["gate_ready"], 1)
                            act.wait_ge(S["gate_ready"], m * 2 + q + 1)
                            act.sem_inc(acc_free[n % 2], 1)
                    act.wait_ge(S["merged_out"], m + 1)
                    act.dma_start(merged_d[bass.ds(m, 1)].rearrange("a p t -> (a p) t"), tile[:, 4 + s, :]
                                  ).then_inc(S["merged_saved"], 16)

            act.wait_ge(S["cs_ready"], 1)
            act.activation(dtm[:, 5, :], bank[1][:, 2 * P:3 * P], ACT.Exp)
            act.activation(dtm[:, 1, :], bank[1][:, 0:P], ACT.Copy).then_inc(S["cs_copied"], 1)
            act.wait_ge(S["cs_copied"], 1)
            act.dma_start(cs_d, dtm[:, 1, :]).then_inc(S["cs_saved"], 16)
            act.wait_ge(S["dt_diff"], 1)
            act.activation(dtm[:, 6, :], dtm[:, 6, :], ACT.Exp).then_inc(S["dt_decays"], 1)
            act.wait_ge(S["cs_saved"], 16)

            with act.Fori(0, GROUPS) as g:
                def load_sums(c):
                    act.dma_start(tile[:, 6 + c % 2, :],
                                  cs_d[bass.ds(g * GH + c * HEADS, GH), :].rearrange("r l -> (r l)").partition_broadcast(P)
                                  ).then_inc(S["csb_in"], 16)

                for q in range(6):
                    dst = tile[:, (4, 5, 0, 1, 2, 3)[q], :]
                    act.wait_ge(S["block_done"], g * 10 + (N_SSM + q + 1))
                    if q == 0:
                        act.wait_ge(S["z_used"], g * 10 + 1)
                    act.activation(dst, acc[(q + 1) % 2][:], ACT.Identity, bias=gpar[:, 5 * q + 4:5 * q + 5],
                                   scale=gpar[:, 5 * q + 3:5 * q + 4]).then_inc(S["conv_first"], 1)
                    act.wait_ge(S["conv_done"], g * 6 + q + 1)
                    act.activation(dst, dst, ACT.Silu).then_inc(S["conv_silu"], 1)
                def prepare(c):
                    csb = tile[:, 6 + c % 2, :]
                    if c >= 2:
                        act.wait_ge(S["y_ready"], g * NT + c - 1)
                    if c:
                        load_sums(c)
                    act.wait_ge(S["csb_in"], g * 128 + 16 * c + 16)
                    act.activation(tile[:, 8 + c % 2, :], csb, ACT.Exp).then_inc(S["e_ready"], 1)
                    act.wait_ge(S["g_ready"], g * NT + c + 1)
                    if c:
                        act.wait_ge(S["s_ready"], g * NT + c)
                    act.activation(tile[:, 11, HALF:HALF + P], bank[1][:, 0:P], ACT.Copy).then_inc(S["btok_ready"], 1)
                    act.wait_ge(S["diff_ready"], g * NT + c + 1)
                    act.activation(csb, csb, ACT.Relu, scale=-1.0).then_inc(S["relu_ready"], 1)
                    act.wait_ge(S["relu_ready"], g * NT + c + 1)
                    act.activation(csb, csb, ACT.Exp, scale=-1.0).then_inc(S["l_ready"], 1)

                load_sums(0)
                for c in range(NT):
                    prepare(c)
                act.wait_ge(S["y_ready"], g * NT + NT - 1)
                for j in range(5):
                    if j < 4:
                        if j == 2:
                            act.wait_ge(S["y_ready"], g * NT + NT)
                        act.wait_ge(S["block_done"], g * 10 + (N_SSM + 6 + j + 1))
                        act.activation(tile[:, (8, 6, 9, 7)[j], :], acc[(j + 1) % 2][:], ACT.Silu).then_inc(S["z_silu"], 1)
                        act.wait_ge(S["z_silu"], g * 4 + j + 1)
                        act.sem_inc(acc_free[(j + 1) % 2], 1)
                    if j:
                        act.wait_ge(S["z_used"], g * 10 + j + 1)
                        if j > 2:
                            act.wait_ge(S["ssm_sq"], g * 4 + j - 1)
                        act.activation(tile[:, 10 if j == 1 else 11, :], tile[:, j - 1, :], ACT.Square).then_inc(S["y_gated"], 1)
                act.wait_ge(S["ssm_root"], g * 2 + 1)
                root(HALF, S["ssm_root"])
                for j in range(4):
                    act.wait_ge(S["ssm_scaled"], g * 4 + j + 1)
                    act.activation(u_hi[:, bass.ds(g * 4 + j, 1), :].rearrange("p a t -> p (a t)"), tile[:, j, :], ACT.Copy
                                   ).then_inc(S["ssm_hi"], 1)

            act.wait_ge(S["merged_saved"], 16 * KT + 16)
            act.wait_ge(S["z_used"], 21)
            with act.Fori(0, KT // 2) as t:
                for s in range(2):
                    m = t * 2 + s
                    act.wait_ge(S["c_free"], m + 1)
                    act.dma_start(tile[:, 10 + s, :], merged_d[bass.ds(m, 1)].rearrange("a p t -> (a p) t")
                                  ).then_inc(merged_s[s], 16)
                    act.wait_ge(S["block_done"], m * 2 + (N_C + 1))
                    act.activation(tile[:, 8 + s, :], acc[1][:], ACT.Sigmoid).then_inc(S["c_gate"], 1)
                    act.wait_ge(S["c_gate"], m + 1)
                    act.sem_inc(acc_free[1], 1)
            for k in range(KT):
                act.wait_ge(S["merged_all"], KT)
                act.activation(u_hi[:, k, :], tile[:, k, :], ACT.Copy).then_inc(S["merged_hi"], 1)
            for k in range(KT):
                act.wait_ge(S["merged_ready"], k + 1)
                act.dma_start(tile[:, k, :], x_in[k]).then_inc(S["x2_in"], 16)
            for k in range(KT):
                act.wait_ge(S["x1_ready"], k + 1)
                if k >= 2:
                    act.wait_ge(S["x1_sum"], k - 1)
                act.activation(tile[:, 10 + 2 * (k % 2), :], xres[k], ACT.Square).then_inc(S["x1_sq"], 1)
            act.wait_ge(S["n2_root"], 1)
            root(D, S["n2_root"])
            for k in range(KT):
                act.wait_ge(S["n2_scaled"], k + 1)
                act.activation(h_hi[:, k, :], tile[:, 8 + k % 2, :], ACT.Identity, bias=mod[:, 24 + k:25 + k]
                               ).then_inc(S["n2_hi"], 1)
            with act.Fori(0, QUARTERS) as q4:
                with act.Fori(0, KT // 2) as t:
                    for s in range(2):
                        b = (N_MLP + s) % 2
                        m = q4 * 8 + t * 2 + s
                        act.wait_ge(S["block_done"], q4 * 16 + t * 2 + (N_MLP + s + 1))
                        act.wait_ge(S["relu_free"], m + 1)
                        act.activation(tile[:, 8 + s, :], acc[b][:], ACT.Relu).then_inc(S["hid_relu"], 1)
                        act.wait_ge(S["hid_relu"], m + 1)
                        act.sem_inc(acc_free[b], 1)
                        act.wait_ge(S["hid_sq"], m + 1)
                        act.activation(u_hi[:, bass.ds(t * 2 + s, 1), :].rearrange("p a t -> p (a t)"), tile[:, 10 + s, :], ACT.Copy
                                       ).then_inc(S["hid_hi"], 1)
            for k in range(KT):
                act.wait_ge(S["x2_ready"], (QUARTERS - 1) * KT + k + 1)
                if k >= 2:
                    act.wait_ge(S["f_sum"], k - 1)
                act.activation(tile[:, 10 + 2 * (k % 2), :], xres[k], ACT.Square).then_inc(S["f_sq"], 1)
            act.wait_ge(S["f_root"], 1)
            root(D, S["f_root"])
            for k in range(KT):
                act.wait_ge(S["f_ready"], k + 1)
                act.dma_start(out[k], xres[k]).then_inc(S["out_saved"], 16)
            act.wait_ge(S["out_saved"], 16 * KT)

        @block.vector
        def _(dve):
            own = Steps(dve, S["dve_own"])
            dve.sem_inc(S["gates_free"], 1)
            dve.sem_inc(S["c_free"], 2)
            dve.sem_inc(S["relu_free"], 2)

            def squares_sum(first_wait, used, base=0):
                for k in range(KT):
                    dve.wait_ge(first_wait, base + k + 1)
                    src = tile[:, 10 + 2 * (k % 2), :]
                    if k == 0:
                        dve.tensor_copy(tile[:, 11, :], src).then_inc(used, 1)
                    else:
                        dve.wait_ge(used, base + k)
                        dve.tensor_tensor(tile[:, 11, :], tile[:, 11, :], src, ALU.add).then_inc(used, 1)

            def factor(ms, root, inverse, n):
                dve.wait_ge(ms, n + 1)
                dve.tensor_copy(rms[:, 0, :], bank[3][:, 0:NT]).then_inc(root, 1)
                dve.wait_ge(root, n * 2 + 2)
                dve.reciprocal(rstd[:], rms[:, 1, :]).then_inc(inverse, 1)

            dve.memset(ones[:], 1.0).then_inc(acc_free[0], 1)
            dve.memset(eps[:], EPS).then_inc(acc_free[1], 1)
            own.mark(dve.memset(sm[:], 0.0))
            dve.wait_ge(S["par_in"], 16)
            dve.wait_ge(S["lam_in"], 16)
            for q in range(2):
                v = tile[:, 11, 2 * q * HD:2 * (q + 1) * HD]
                dve.tensor_tensor_reduce(tile[:, 11, (4 + q) * HD:(5 + q) * HD], v[:, 0:HD], v[:, HD:2 * HD], 1.0, 0.0, ALU.mult, ALU.add,
                                         lam[:, q:q + 1]).then_inc(S["lam_dots"], 1)
            own.mark(dve.tensor_scalar(a_da[:], par[:, C_SUBLN:C_SUBLN + 1], DA_OUT, None, ALU.mult))
            dve.wait_ge(S["lam_dots"], 2)
            squares_sum(S["sq_ready"], S["sq_used"])
            dve.wait_ge(S["lam_exps"], 1)
            own.mark(dve.tensor_tensor(lam[:, 4:5], lam[:, 3:4], lam[:, 2:3], ALU.subtract))
            own.settle()
            own.mark(dve.tensor_scalar(lam[:, 5:6], lam[:, 4:5], -LAM_INIT, None, ALU.add))
            dve.wait_ge(S["mod_done"], 16)
            own.mark(dve.tensor_tensor(mod[:, 0:16], bank[2][:, 0:16], par[:, C_ADAB:C_ADAB + 16], ALU.add))
            own.settle()
            own.mark(dve.scalar_tensor_tensor(out=a_mix[:], in0=mod[:, 8:16], scalar=1.0, in1=par[:, C_GMIX:C_GMIX + 8],
                                              op0=ALU.add, op1=ALU.mult))
            own.settle()

            factor(S["ms_ready"], S["root_ready"], S["rstd_ready"], 0)
            dve.wait_ge(S["bcast_ready"], 1)
            for k in range(KT):
                dve.scalar_tensor_tensor(out=xres[k], in0=xres[k], scalar=a_mix[:, k:k + 1], in1=wk[0][:],
                                         op0=ALU.mult, op1=ALU.mult).then_inc(S["h_scaled"], 1)
                if k:
                    dve.wait_ge(S["h_hi_ready"], k)
                    dve.scalar_tensor_tensor(out=h_lo[:, k - 1, :], in0=xres[k - 1], scalar=mod[:, k - 1:k],
                                             in1=h_hi[:, k - 1, :].bitcast(F32), op0=ALU.add, op1=ALU.subtract
                                             ).then_inc(S["h_ready"], 1)
            dve.wait_ge(S["h_hi_ready"], KT)
            dve.scalar_tensor_tensor(out=h_lo[:, KT - 1, :], in0=xres[KT - 1], scalar=mod[:, KT - 1:KT],
                                     in1=h_hi[:, KT - 1, :].bitcast(F32), op0=ALU.add, op1=ALU.subtract
                                     ).then_inc(S["h_ready"], 1)

            def da_head(head):
                def bias(i, m):
                    col = 2 * (i % 2) + m
                    w = (i + 1) * P
                    if i >= 2 and m == 0:
                        dve.wait_ge(S["turned"], head * NP_ + PIECES.index((i - 2, (i - 2) // 4)) + 1)
                    dve.wait_ge(S["scored"], head * 16 + 2 * i + m + 1)
                    dve.nop(nofuse=True)
                    dve.tensor_tensor_reduce(tile[:, (5, 6, 7, 8)[col], 0:w], wk[0][:, 0:w], tile[:, 4, T - w:T], SCALE, NEG,
                                             ALU.add, ALU.max, mxp[:, col:col + 1]).then_inc(S["biased"], 1)
                    dve.wait_ge(S["biased"], head * 16 + 2 * i + m + 1)
                    dve.tensor_scalar(mx[:, col:col + 1], mxp[:, col:col + 1], -1.0, None, ALU.mult).then_inc(S["negmax"], 1)

                def weigh(i):
                    col = 2 * (i % 2)
                    w = (i + 1) * P
                    p0, p1 = (tile[:, (5, 6, 7, 8)[col + m], 0:w] for m in range(2))
                    dve.wait_ge(S["exped"], head * 16 + 2 * i + 2)
                    own.mark(dve.reciprocal(rc[:, col:col + 2], sm[:, col:col + 2]))
                    own.settle()
                    own.mark(dve.tensor_scalar(p1, p1, rc[:, col + 1:col + 2], lam[:, 5:6], ALU.mult, ALU.mult))
                    own.settle()
                    dve.scalar_tensor_tensor(out=p0, in0=p0, scalar=rc[:, col:col + 1], in1=p1,
                                             op0=ALU.mult, op1=ALU.add).then_inc(S["weighted"], 1)

                dve.wait_ge(S["da_tab_in"], head * 16 + 16)
                for i in range(NT):
                    bias(i, 0)
                    if i:
                        weigh(i - 1)
                    bias(i, 1)
                weigh(NT - 1)
                dve.wait_ge(S["weighted"], head * 8 + 8)
                dve.wait_ge(S["turned"], head * NP_ + NP_)

            with dve.Fori(0, DA_HEADS) as head, own.loop(head, 16, DA_HEADS):
                da_head(head)

            own.mark(dve.tensor_scalar(negsink[:], par[:, C_SINK:C_SINK + 8], -1.0, None, ALU.mult))
            own.settle()
            dve.sem_inc(S["sw_biased"], 1)
            dve.sem_inc(S["sw_split"], 1)
            dve.sem_inc(S["da_hi"], 1)

            def sw_pair(s, j):
                def soften(i):
                    dve.wait_ge(S["sw_scored"], j * NT + i + 1)
                    if i >= 4:
                        dve.wait_ge(S["sw_turned"], j * NT + i - 3)
                    dve.nop(nofuse=True)
                    w = 256 if i else P
                    for g in range(2):
                        col = 2 * (i % 4) + g
                        hi = (i % 2) * HALF + (g + 1) * 256
                        last = dve.tensor_tensor_reduce(
                            tile[:, 5 + (i % 4) // 2, hi - w:hi], bank[g][:, 256 - w:256],
                            tile[:, 4, s * HALF + (g + 1) * 256 - w:s * HALF + (g + 1) * 256], SCALE, NEG, ALU.add, ALU.max,
                            swm[:, col:col + 1])
                    last.then_inc(S["sw_biased"], 1)
                    cols = slice(2 * (i % 4), 2 * (i % 4) + 2)
                    dve.wait_ge(S["sw_biased"], j * NT + i + 2)
                    own.mark(dve.scalar_tensor_tensor(out=swn[:, cols], in0=swm[:, cols], scalar=-1.0,
                                                      in1=negsink[:, bass.ds(j * 2, 2)], op0=ALU.mult, op1=ALU.min))
                    own.settle()
                    dve.tensor_tensor(swd[:, cols], swn[:, cols], negsink[:, bass.ds(j * 2, 2)], ALU.subtract
                                      ).then_inc(S["sw_negmax"], 1)

                def weigh(i):
                    cols = slice(2 * (i % 4), 2 * (i % 4) + 2)
                    dve.wait_ge(S["sw_exped"], j * NT + i + 1)
                    own.mark(dve.tensor_tensor(swr[:, cols], sws[:, cols], swe[:, cols], ALU.add))
                    own.settle()
                    own.mark(dve.reciprocal(swr[:, cols], swr[:, cols]))
                    own.settle()
                    for g in range(2):
                        lo = (i % 2) * HALF + g * 256 + (0 if i else P)
                        p = tile[:, 5 + (i % 4) // 2, lo:(i % 2) * HALF + (g + 1) * 256]
                        last = dve.tensor_scalar(p, p, swr[:, 2 * (i % 4) + g:2 * (i % 4) + g + 1], None, ALU.mult)
                    last.then_inc(S["sw_weighted"], 1)

                def out_lo(half):
                    dve.wait_ge(S["sw_hi"], j * 2 + half + 1)
                    at = (slice(None), bass.ds(j + 4, 1), slice(half * HALF, (half + 1) * HALF))
                    dve.tensor_tensor(u_lo[at].rearrange("p a t -> p (a t)"), bank[3],
                                      u_hi[at].rearrange("p a t -> p (a t)").bitcast(F32), ALU.subtract
                                      ).then_inc(S["sw_split"], 1)

                dve.wait_ge(S["sw_tab_in"], j * 16 + 16)
                for i in range(NT):
                    soften(i)
                    if i:
                        weigh(i - 1)
                    if i == 0:
                        clip(j)
                    if i == 4:
                        factor_da(j)
                    if i == 6:
                        out_lo(0)
                weigh(NT - 1)
                dve.wait_ge(S["da_root"], j * 2 + 2)
                own.mark(dve.reciprocal(rms[:, 2, :], rms[:, 1, :]))
                own.settle()
                dve.tensor_tensor(rstd[:], rms[:, 2, :], rms[:, 4, :], ALU.mult).then_inc(S["da_rstd"], 1)
                dve.wait_ge(S["da_bcast"], j + 1)
                dve.scalar_tensor_tensor(out=tile[:, 12, :], in0=tile[:, 10, :], scalar=a_da[:, 0:1], in1=acc[s][:],
                                         op0=ALU.mult, op1=ALU.mult).then_inc(S["da_scaled"], 1)
                out_lo(1)
                dve.wait_ge(S["da_hi"], j + 2)
                dst = bass.ds(j, 1)
                dve.tensor_tensor(u_lo[:, dst, :].rearrange("p a t -> p (a t)"), tile[:, 12, :],
                                  u_hi[:, dst, :].rearrange("p a t -> p (a t)").bitcast(F32), ALU.subtract
                                  ).then_inc(S["u_ready"], 1)
                dve.wait_ge(S["u_ready"], j + 1)

            def clip(j):
                dve.wait_ge(S["o_back"], j * 16 + 16)
                dve.tensor_scalar(tile[:, 8, :], tile[:, 10, :], 2.0 ** 60, -2.0 ** 60, ALU.min, ALU.max
                                  ).then_inc(S["da_clipped"], 1)
                dve.tensor_scalar(tile[:, 10, :], tile[:, 10, :], 2.0 ** 70, -2.0 ** 70, ALU.min, ALU.max
                                  ).then_inc(S["da_clipped"], 1)

            def factor_da(j):
                dve.wait_ge(S["da_ms"], j * 2 + 2)
                s1, s2 = rms[:, 0, :], rms[:, 1, :]
                big, low, fac = rms[:, 2, :], rms[:, 3, :], rms[:, 4, :]
                own.mark(dve.tensor_copy(rms[:, 0:2, :], acc_means(j)))
                own.settle()
                own.mark(dve.tensor_scalar(big, s2, 2.0 ** 52, None, ALU.is_gt))
                own.mark(dve.tensor_scalar(rms[:, 5, :], s2, 2.0 ** 68, None, ALU.is_lt))
                own.settle()
                own.mark(dve.tensor_scalar(low, big, -1.0, 1.0, ALU.mult, ALU.add))
                own.mark(dve.tensor_tensor(s2, s2, big, ALU.mult))
                own.settle()
                own.mark(dve.scalar_tensor_tensor(out=fac, in0=big, scalar=2.0 ** -30, in1=low, op0=ALU.mult, op1=ALU.add))
                own.settle()
                own.mark(dve.tensor_tensor(low, s1, low, ALU.mult))
                own.mark(dve.tensor_tensor(fac, fac, rms[:, 5, :], ALU.mult))
                own.settle()
                dve.tensor_tensor(rms[:, 0, :], low, s2, ALU.add).then_inc(S["da_root"], 1)

            which = [None]

            def acc_means(j):
                return acc[which[0]][:, 0:2 * NT].rearrange("p (a b) -> p a b", a=2)

            with dve.Fori(0, SW_PAIRS // 2) as t, own.loop(t, 2 * (3 * NT + 9), SW_PAIRS // 2):
                for s in range(2):
                    which[0] = s
                    sw_pair(s, t * 2 + s)

            heads = lambda ap: ap.rearrange("p (c h) -> p c h", h=HEADS)
            dve.wait_ge(S["dt_turned"], 1)
            own.mark(dve.tensor_tensor(heads(dtm[:, 3, :]), heads(bank[0][:, 0:P]),
                                       par[:, C_DTB:C_DTB + HEADS].unsqueeze(1).to_broadcast([P, NT, HEADS]), ALU.add))
            own.settle()
            dve.scalar_tensor_tensor(out=dtm[:, 1, :], in0=dtm[:, 3, :], scalar=-1.0, in1=dtm[:, 3, :], op0=ALU.mult,
                                     op1=ALU.max).then_inc(S["dt_abs"], 1)
            dve.wait_ge(S["dt_exp"], 1)
            e_, s_, s2, q_ = (dtm[:, n, :] for n in (2, 4, 6, 7))
            own.mark(dve.tensor_scalar(q_, e_, 2.0, None, ALU.add))
            own.settle()
            own.mark(dve.reciprocal(s2, q_))
            own.settle()
            own.mark(dve.tensor_tensor(s_, e_, s2, ALU.mult))
            own.settle()
            own.mark(dve.tensor_tensor(s2, s_, s_, ALU.mult))
            own.settle()
            own.mark(dve.tensor_scalar(q_, s2, 1.0 / 15, None, ALU.mult))
            for odd in (13, 11, 9, 7, 5, 3):
                own.settle()
                own.mark(dve.scalar_tensor_tensor(out=q_, in0=q_, scalar=1.0 / odd, in1=s2, op0=ALU.add, op1=ALU.mult))
            own.settle()
            own.mark(dve.scalar_tensor_tensor(out=q_, in0=q_, scalar=1.0, in1=s_, op0=ALU.add, op1=ALU.mult))
            own.mark(dve.tensor_scalar(dtm[:, 3, :], dtm[:, 3, :], 0.0, None, ALU.max))
            own.settle()
            dt_ = dtm[:, 4, :]
            own.mark(dve.scalar_tensor_tensor(out=dt_, in0=q_, scalar=2.0, in1=dtm[:, 3, :], op0=ALU.mult, op1=ALU.add))
            own.settle()
            dve.scalar_tensor_tensor(out=heads(dtm[:, 0, :]), in0=heads(dt_), scalar=-1.0,
                                     in1=exp_a[:].unsqueeze(1).to_broadcast([P, NT, HEADS]),
                                     op0=ALU.mult, op1=ALU.mult).then_inc(S["dt_da"], 1)
            dve.sem_inc(S["ab_free"], 1)
            with dve.Fori(0, KT // 2) as t, own.loop(t, 4, KT // 2):
                for s in range(2):
                    m = t * 2 + s
                    b = (N_AB + 3 * s + 2) % 2
                    dve.wait_ge(S["gate_ready"], m * 2 + 2)
                    dve.wait_ge(S["block_done"], m * 3 + (N_AB + 3))
                    own.mark(dve.tensor_tensor(tile[:, 2, :], tile[:, 0, :], wk[0][:], ALU.mult))
                    own.mark(dve.tensor_tensor(tile[:, 3, :], tile[:, 1, :], acc[b][:], ALU.mult))
                    own.settle()
                    dve.sem_inc(acc_free[b], 1)
                    dve.sem_inc(S["ab_free"], 1)
                    dve.sem_inc(S["gates_free"], 1)
                    dve.wait_ge(S["merged_saved"], t * 32 + 16)
                    dve.tensor_tensor(tile[:, 4 + s, :], tile[:, 2, :], tile[:, 3, :], ALU.add).then_inc(S["merged_out"], 1)
                    dve.wait_ge(S["merged_out"], m + 1)
            dve.wait_ge(S["mod_done"], 48)
            dve.tensor_tensor(mod[:, 16:48], bank[2][:, 16:48], par[:, C_ADAB + 16:C_ADAB + 48], ALU.add
                              ).then_inc(S["mod_rest"], 1)
            dve.wait_ge(S["mod_rest"], 1)
            own.mark(dve.scalar_tensor_tensor(out=a_mlp[:], in0=mod[:, 32:40], scalar=1.0,
                                              in1=par[:, C_GMLP:C_GMLP + 8], op0=ALU.add, op1=ALU.mult))

            dve.wait_ge(S["cs_copied"], 1)
            own.mark(dve.tensor_copy(dtm[:, 7, :], bank[1][:, P:2 * P]))
            own.settle()
            dve.tensor_tensor(dtm[:, 6, :], bank[1][:, 2 * P:3 * P], dtm[:, 7, :], ALU.subtract).then_inc(S["dt_diff"], 1)
            dve.wait_ge(S["dt_decays"], 1)
            own.mark(dve.tensor_tensor(dtm[:, 6, :], dtm[:, 6, :], dt_, ALU.mult))
            own.settle()
            dve.sem_inc(S["cs_copied"], 1)

            with dve.Fori(0, GROUPS) as g, own.loop(g, 14 + NT + 4, GROUPS):
                own.mark(dve.tensor_copy(gpar[:, 0:30], par[:, bass.ds(g * 30 + C_CONV, 30)]))
                own.mark(dve.tensor_copy(gpar[:, 30:34], par[:, bass.ds(g * 4 + C_D, 4)]))
                own.settle()
                dve.sem_inc(S["z_used"], 1)
                for q in range(6):
                    dst = tile[:, (4, 5, 0, 1, 2, 3)[q], :]
                    src = acc[(q + 1) % 2]
                    dve.wait_ge(S["conv_first"], g * 6 + q + 1)
                    for tap in (2, 1, 0):
                        lag = 3 - tap
                        ins = dve.scalar_tensor_tensor(out=dst[:, lag:T], in0=src[:, 0:T - lag],
                                                       scalar=gpar[:, 5 * q + tap:5 * q + tap + 1], in1=dst[:, lag:T],
                                                       op0=ALU.mult, op1=ALU.add)
                        if tap:
                            own.mark(ins)
                            own.settle()
                        else:
                            ins.then_inc(S["conv_done"], 1)
                    dve.wait_ge(S["conv_done"], g * 6 + q + 1)
                    dve.sem_inc(acc_free[(q + 1) % 2], 1)
                dve.memset(tile[:, 11, 0:HALF], 0.0).then_inc(S["state_ready"], 1)
                byhead = lambda ap: ap.rearrange("p (h x) -> p h x", h=GH)

                def prepare(c):
                    now = bass.ds(g * GH + c * HEADS, GH)
                    csb = tile[:, 6 + c % 2, :]
                    dve.wait_ge(S["x_turned"], g * NT + c + 1)
                    if c:
                        dve.wait_ge(S["s_ready"], g * NT + c)
                    if c >= 2:
                        dve.wait_ge(S["y_ready"], g * NT + c - 1)
                    for dst, fac in ((tile[:, 10, (c % 2) * HALF:(c % 2 + 1) * HALF], 4), (tile[:, 12, 0:HALF], 6)):
                        dve.tensor_tensor(byhead(dst), byhead(bank[0]),
                                          dtm[:, fac, now].unsqueeze(2).to_broadcast([P, GH, HD]), ALU.mult
                                          ).then_inc(S["xd_ready"], 1)
                    dve.wait_ge(S["btok_ready"], g * NT + c + 1)
                    if c:
                        dve.wait_ge(S["m_ready"], g * 16 + 2 * c)
                    dve.tensor_tensor(tile[:, 11, HALF + P:HALF + 2 * P], bank[1][:, P:2 * P], tri, ALU.mult
                                      ).then_inc(S["g_masked"], 1)
                    dve.wait_ge(S["e_ready"], g * NT + c + 1)
                    dve.tensor_tensor(byhead(csb), byhead(csb), dtm[:, 7, now].unsqueeze(2).to_broadcast([P, GH, P]),
                                      ALU.subtract).then_inc(S["diff_ready"], 1)

                def finish(c):
                    csb, e_row = tile[:, 6 + c % 2, :], tile[:, 8 + c % 2, :]
                    dve.tensor_tensor(byhead(e_row), byhead(e_row),
                                      tile[:, 5, c * P:(c + 1) * P].unsqueeze(1).to_broadcast([P, GH, P]), ALU.mult
                                      ).then_inc(S["m_ready"], 1)
                    dve.wait_ge(S["l_ready"], g * NT + c + 1)
                    dve.wait_ge(S["g_masked"], g * NT + c + 1)
                    dve.tensor_tensor(byhead(csb), byhead(csb),
                                      tile[:, 11, HALF + P:HALF + 2 * P].unsqueeze(1).to_broadcast([P, GH, P]), ALU.mult
                                      ).then_inc(S["m_ready"], 1)

                prepare(0)
                finish(0)
                for c in range(NT):
                    cols = slice(c * P, (c + 1) * P)
                    now = bass.ds(g * GH + c * HEADS, GH)
                    if c + 1 < NT:
                        prepare(c + 1)
                    dve.wait_ge(S["y_ready"], g * NT + c + 1)
                    for j in range(4):
                        dve.scalar_tensor_tensor(out=tile[:, j, cols], in0=tile[:, j, cols], scalar=gpar[:, 30 + j:31 + j],
                                                 in1=bank[3][:, j * P:(j + 1) * P], op0=ALU.mult, op1=ALU.add
                                                 ).then_inc(S["y_taken"], 1)
                    own.mark(dve.tensor_tensor(byhead(tile[:, 11, 0:HALF]), byhead(tile[:, 11, 0:HALF]),
                                               dtm[:, 5, now].unsqueeze(2).to_broadcast([P, GH, HD]), ALU.mult))
                    own.settle()
                    dve.tensor_tensor(tile[:, 11, 0:HALF], tile[:, 11, 0:HALF], bank[2][:, :], ALU.add
                                      ).then_inc(S["state_ready"], 1)
                    dve.wait_ge(S["state_ready"], g * (NT + 1) + c + 2)
                    if c + 1 < NT:
                        finish(c + 1)
                dve.wait_ge(S["y_taken"], g * 32 + 32)
                for j in range(4):
                    dve.wait_ge(S["z_silu"], g * 4 + j + 1)
                    own.mark(dve.tensor_tensor(tile[:, j, :], tile[:, j, :], tile[:, (8, 6, 9, 7)[j], :], ALU.mult))
                    own.settle()
                    dve.sem_inc(S["z_used"], 1)
                    dve.wait_ge(S["y_gated"], g * 4 + j + 1)
                    if j == 0:
                        dve.sem_inc(S["ssm_sq"], 1)
                    else:
                        dve.tensor_tensor(tile[:, 10, :], tile[:, 10, :], tile[:, 11, :], ALU.add).then_inc(S["ssm_sq"], 1)
                        dve.wait_ge(S["ssm_sq"], g * 4 + j + 1)
                factor(S["ssm_ms"], S["ssm_root"], S["ssm_rstd"], g)
                dve.wait_ge(S["ssm_bcast"], g + 1)
                for j in range(5):
                    if j < 4:
                        dve.scalar_tensor_tensor(out=tile[:, j, :], in0=tile[:, j, :],
                                                 scalar=par[:, bass.ds(g * 4 + (C_GSSM + j), 1)], in1=wk[0][:],
                                                 op0=ALU.mult, op1=ALU.mult).then_inc(S["ssm_scaled"], 1)
                    if j:
                        dve.wait_ge(S["ssm_hi"], g * 4 + j)
                        dst = bass.ds(g * 4 + j - 1, 1)
                        dve.tensor_tensor(u_lo[:, dst, :].rearrange("p a t -> p (a t)"), tile[:, j - 1, :],
                                          u_hi[:, dst, :].rearrange("p a t -> p (a t)").bitcast(F32), ALU.subtract
                                          ).then_inc(S["y_split"], 1)
                dve.wait_ge(S["y_split"], g * 4 + 4)
                for _n in range(5):
                    dve.sem_inc(S["z_used"], 1)

            dve.sem_inc(S["z_used"], 1)
            with dve.Fori(0, KT // 2) as t, own.loop(t, 2, KT // 2):
                for s in range(2):
                    m = t * 2 + s
                    dve.wait_ge(S["c_gate"], m + 1)
                    dve.wait_ge(S["block_done"], m * 2 + (N_C + 2))
                    own.mark(dve.tensor_tensor(tile[:, 8 + s, :], tile[:, 8 + s, :], acc[0][:], ALU.mult))
                    own.settle()
                    dve.sem_inc(acc_free[0], 1)
                    dve.wait_ge(merged_s[s], t * 16 + 16)
                    dst = tile[:, bass.ds(m, 1), :].rearrange("p a t -> p (a t)")
                    dve.tensor_tensor(dst, tile[:, 8 + s, :], tile[:, 10 + s, :], ALU.add).then_inc(S["merged_all"], 1)
                    dve.wait_ge(S["merged_all"], m + 1)
                    dve.sem_inc(S["c_free"], 1)
            for k in range(KT):
                dve.wait_ge(S["merged_hi"], k + 1)
                dve.tensor_tensor(u_lo[:, k, :], tile[:, k, :], u_hi[:, k, :].bitcast(F32), ALU.subtract
                                  ).then_inc(S["merged_ready"], 1)

            for k in range(KT):
                b = (N_OUT + k) % 2
                dve.wait_ge(S["block_done"], N_OUT + k + 1)
                dve.wait_ge(S["x2_in"], 16 * KT)
                dve.scalar_tensor_tensor(out=xres[k], in0=acc[b][:], scalar=mod[:, 16 + k:17 + k], in1=xres[k],
                                         op0=ALU.mult, op1=ALU.add).then_inc(S["x1_ready"], 1)
                dve.wait_ge(S["x1_ready"], k + 1)
                dve.sem_inc(acc_free[b], 1)
                dve.wait_ge(S["x1_sq"], k + 1)
                src = tile[:, 10 + 2 * (k % 2), :]
                if k == 0:
                    dve.tensor_copy(tile[:, 11, :], src).then_inc(S["x1_sum"], 1)
                else:
                    dve.wait_ge(S["x1_sum"], k)
                    dve.tensor_tensor(tile[:, 11, :], tile[:, 11, :], src, ALU.add).then_inc(S["x1_sum"], 1)
            factor(S["n2_ms"], S["n2_root"], S["n2_rstd"], 0)
            dve.wait_ge(S["n2_bcast"], 1)
            for k in range(KT + 1):
                if k < KT:
                    if k >= 2:
                        dve.wait_ge(S["n2_ready"], k - 1)
                    dve.scalar_tensor_tensor(out=tile[:, 8 + k % 2, :], in0=xres[k], scalar=a_mlp[:, k:k + 1], in1=wk[0][:],
                                             op0=ALU.mult, op1=ALU.mult).then_inc(S["n2_scaled"], 1)
                if k:
                    dve.wait_ge(S["n2_hi"], k)
                    dve.scalar_tensor_tensor(out=h_lo[:, k - 1, :], in0=tile[:, 8 + (k - 1) % 2, :], scalar=mod[:, 23 + k:24 + k],
                                             in1=h_hi[:, k - 1, :].bitcast(F32), op0=ALU.add, op1=ALU.subtract
                                             ).then_inc(S["n2_ready"], 1)
            dve.wait_ge(S["n2_ready"], KT)

            with dve.Fori(0, QUARTERS) as q4:
                with dve.Fori(0, KT // 2) as t:
                    for s in range(2):
                        m = q4 * 8 + t * 2 + s
                        dve.wait_ge(S["hid_relu"], m + 1)
                        dve.tensor_tensor(tile[:, 10 + s, :], tile[:, 8 + s, :], tile[:, 8 + s, :], ALU.mult
                                          ).then_inc(S["hid_sq"], 1)
                        dve.wait_ge(S["hid_hi"], m + 1)
                        dve.sem_inc(S["relu_free"], 1)
                        dst = bass.ds(t * 2 + s, 1)
                        dve.tensor_tensor(u_lo[:, dst, :].rearrange("p a t -> p (a t)"), tile[:, 10 + s, :],
                                          u_hi[:, dst, :].rearrange("p a t -> p (a t)").bitcast(F32), ALU.subtract
                                          ).then_inc(S["hid_ready"], 1)
                        dve.wait_ge(S["hid_ready"], m + 1)
                with dve.Fori(0, KT // 2) as t:
                    for s in range(2):
                        b = (N_MLP + 8 + s) % 2
                        m = q4 * 8 + t * 2 + s
                        dve.wait_ge(S["block_done"], q4 * 16 + t * 2 + (N_MLP + 8 + s + 1))
                        xk = tile[:, bass.ds(t * 2 + s, 1), :].rearrange("p a t -> p (a t)")
                        dve.scalar_tensor_tensor(out=xk, in0=acc[b][:], scalar=mod[:, bass.ds(t * 2 + (40 + s), 1)], in1=xk,
                                                 op0=ALU.mult, op1=ALU.add).then_inc(S["x2_ready"], 1)
                        dve.wait_ge(S["x2_ready"], m + 1)
                        dve.sem_inc(acc_free[b], 1)

            squares_sum(S["f_sq"], S["f_sum"])
            factor(S["f_ms"], S["f_root"], S["f_rstd"], 0)
            dve.wait_ge(S["f_bcast"], 1)
            for k in range(KT):
                dve.scalar_tensor_tensor(out=xres[k], in0=xres[k], scalar=par[:, C_GFIN + k:C_GFIN + k + 1], in1=wk[0][:],
                                         op0=ALU.mult, op1=ALU.mult).then_inc(S["f_ready"], 1)


def blocks(w):
    k, m = w.shape
    return w.reshape(k // P, P, m // P, P).transpose(2, 1, 0, 3).reshape(m // P, P, (k // P) * P)


def shape_constants():
    n = SW_PAIRS * 2 + DA_HEADS
    slopes = np.exp2(-8.0 * np.arange(1, n + 1) / n).astype(np.float32)
    con = np.zeros((P, K_ALL), np.float32)
    con[:, K_ID:K_ID + P] = np.eye(P, dtype=np.float32)
    con[:, K_TRI:K_TRI + P] = np.triu(np.ones((P, P), np.float32))
    p = np.arange(P)[:, None]
    x = np.arange(256)[None, :]
    ok = (x // 64 >= p // 64 + 1) & (x // 64 <= p // 64 + 2)
    dist = np.abs(P + p - x).astype(np.float32)
    sw = np.zeros((SW_PAIRS, P, 2 * 256), np.float32)
    for j in range(SW_PAIRS):
        for g in range(2):
            sw[j, :, g * 256:(g + 1) * 256] = np.where(ok, -slopes[4 * g + j] / np.float32(SCALE) * dist, np.float32(NEG))
    x = np.arange(T)[None, :] - (T - P)
    ok = x // 64 <= p // 64
    dist = np.abs(p - x).astype(np.float32)
    tab = np.stack([np.where(ok, -slopes[8 + h] / np.float32(SCALE) * dist, np.float32(NEG)) for h in range(DA_HEADS)])
    tab = np.concatenate([tab.astype(np.float32), np.concatenate([sw[0], sw[1]], 1)[None]])
    return con, tab, sw


def kernel(**inputs):
    import concourse.bacc as bacc
    from concourse.bass_utils import run_bass_kernel_spmd as run

    a = {k: np.asarray(v) for k, v in inputs.items()}
    cols = lambda v: v.reshape(-1, P).T
    w = a["w_in"][0]
    da_q, da_k, da_v = (w[:, 512 * i:512 * (i + 1)] for i in range(3))
    at = 1536
    sw_q, sw_k, sw_v = w[:, at:at + 512], w[:, at + 512:at + 640], w[:, at + 640:at + 768]
    at += 768
    z, xs = w[:, at:at + 1024], w[:, at + 1024:at + 2048]
    bs, cs = w[:, at + 2048:at + 2304], w[:, at + 2304:at + 2560]
    at += 2560
    dt_cols = w[:, at:at + P]
    gates = [w[:, at + 16 + D * i:at + 16 + D * (i + 1)] for i in range(3)]
    pair = lambda v, ax: np.concatenate([np.take(v, range(64 * h, 64 * h + 64), ax) for j in range(4) for h in (j, j + 4)], ax)
    sw_q = pair(sw_q, 1)
    wb = a["w_branch"][0]
    wab = np.concatenate([wb[0:512], pair(wb[512:1024], 0)], 0)
    stream = []
    dq, dk, dv = (blocks(v) for v in (da_q, da_k, da_v))
    for h in range(DA_HEADS):
        stream += [dv[h], dk[h], dq[h]]
    stream += [blocks(sw_v)[0], blocks(sw_k)[0], *blocks(sw_q)]
    ga, gb, gc = (blocks(v) for v in gates)
    bab, bc = blocks(wab), blocks(wb[1024:2048])
    stream += [blocks(dt_cols)[0]]
    for m in range(KT):
        stream += [ga[m], gb[m], bab[m]]
    bz, bx, bbs, bcs = (blocks(v) for v in (z, xs, bs, cs))
    for g in range(GROUPS):
        stream += [bbs[g], bcs[g], *bx[4 * g:4 * g + 4], *bz[4 * g:4 * g + 4]]
    for m in range(KT):
        stream += [gc[m], bc[m]]
    stream += [*blocks(a["w_out"][0])]
    w1, w2 = blocks(a["w_mlp1"][0]), a["w_mlp2"][0]
    for q in range(QUARTERS):
        stream += [*w1[8 * q:8 * q + 8], *blocks(w2[D * q:D * (q + 1)])]
    stream = np.stack(stream)
    assert len(stream) == N_ALL

    conv = np.concatenate([a["ssm_conv_w"][0], a["ssm_conv_b"]], 0)
    conv = conv.T.reshape(12, P, 5)
    conv = np.concatenate([conv[[8 + g, 10 + g, 4 * g, 4 * g + 1, 4 * g + 2, 4 * g + 3]] for g in range(GROUPS)])
    every = lambda v: np.broadcast_to(v.reshape(1, -1), (P, v.size))
    par = np.ascontiguousarray(np.concatenate([
        cols(a["norm_mix_g"][0]), cols(a["norm_mlp_g"][0]), cols(a["final_norm_g"]), cols(a["ssm_norm_g"][0]),
        cols(a["ada_b"][0]), conv.transpose(1, 0, 2).reshape(P, 60), cols(np.repeat(a["ssm_D"][0], HD)),
        cols(a["da_subln_g"][0]), every(a["ssm_dt_bias"][0]), every(a["ssm_A_log"][0]), every(a["sw_sinks"][0].reshape(2, 4).T)], 1))
    lam_v = np.ascontiguousarray(np.concatenate([
        every(a["da_lambda_q1"][0]), every(a["da_lambda_k1"][0]), every(a["da_lambda_q2"][0]), every(a["da_lambda_k2"][0]),
    ], 1))
    con, tab, sw = shape_constants()
    arrays = {
        "x_t": np.ascontiguousarray(a["x"][0].T).reshape(KT, P, T),
        "c_t": np.ascontiguousarray(cols(a["c"][0])),
        "ada_blocks": np.ascontiguousarray(blocks(a["ada_w"][0])),
        "w_stream": stream,
        "params": par,
        "constants": con,
        "da_bias": tab,
        "sw_bias": sw,
        "lambda_vectors": lam_v,
    }
    nc = bacc.Bacc("TRN2", target_bir_lowering=False, num_devices=1)
    aps = [nc.dram_tensor(n, v.shape, F32, kind="ExternalInput").ap() for n, v in arrays.items()]
    out = nc.dram_tensor("out_t", [KT, P, T], F32, kind="ExternalOutput").ap()
    build(nc, *aps, out)
    r = run(nc, [arrays], core_ids=[0])
    got = r.results[0]["out_t"]
    return np.ascontiguousarray(got.reshape(D, T).T)[None]
```

```python
from contextlib import ExitStack, contextmanager

import numpy as np
import concourse.bass as bass
from concourse import mybir

F32 = mybir.dt.float32
F32R = mybir.dt.float32r
ALU = mybir.AluOpType
ACT = mybir.ActivationFunctionType

P = 128
T = 1024
D = 1024
KT = D // P
NT = T // P
HALF = 512
EPS = 1e-6
DA_HEADS = 4
SW_PAIRS = 4
GROUPS = 2
GH = 8
HD = 64
HEADS = GROUPS * GH
LAM_INIT = 0.8 - 0.6 * 1.0
DA_OUT = 1.0 - LAM_INIT
SCALE = HD ** -0.5
NEG = -1.0e30

N_DA = 0
N_SW = N_DA + 3 * DA_HEADS
N_DT = N_SW + 2 + SW_PAIRS
N_AB = N_DT + 1
N_SSM = N_AB + 3 * KT
N_C = N_SSM + 10 * GROUPS
N_OUT = N_C + 2 * KT
N_MLP = N_OUT + KT
QUARTERS = 4
N_ALL = N_MLP + 16 * QUARTERS

C_GMIX, C_GMLP, C_GFIN, C_GSSM = 0, 8, 16, 24
C_ADAB = 32
C_CONV = C_ADAB + 48
C_D = C_CONV + 60
C_SUBLN = C_D + 8
C_DTB = C_SUBLN + 1
C_ALOG = C_DTB + HEADS
C_SINK = C_ALOG + HEADS
C_ALL = C_SINK + 8
K_ID, K_TRI, K_ALL = 0, P, 2 * P

PIECES = [(i, half) for i in range(NT) for half in range(1 + i // 4)]
NP_ = len(PIECES)


class Steps:

    def __init__(self, eng, sem):
        self.eng, self.sem, self.base, self.k = eng, sem, 0, 0

    def mark(self, ins):
        ins.then_inc(self.sem, 1)
        self.k += 1

    def settle(self):
        self.eng.wait_ge(self.sem, self.base + self.k)

    @contextmanager
    def loop(self, i, per, trips):
        old, start = self.base, self.k
        self.base = old + i * per
        yield
        assert self.k - start == per, (self.k - start, per)
        self.base, self.k = old, start + per * trips


def flat(ap):
    return ap.rearrange("p a b -> p (a b)")


def build(nc, x_in, c_in, ada_in, w_in, par_in, con_in, da_tab, sw_tab, lam_v, out):
    with ExitStack() as ctx:
        def sb(name, shape, dt=F32):
            return ctx.enter_context(nc.sbuf_tensor(name, shape, dt))

        def sem(name):
            return ctx.enter_context(nc.semaphore(name))

        h_hi = sb("h_hi", [P, KT, T], F32R)
        h_lo = sb("h_lo", [P, KT, T], F32R)
        u_hi = sb("u_hi", [P, KT, T], F32R)
        u_lo = sb("u_lo", [P, KT, T], F32R)
        w_hi = [sb(f"w_hi{i}", [P, KT, P], F32R) for i in range(2)]
        w_lo = [sb(f"w_lo{i}", [P, KT, P], F32R) for i in range(2)]
        raw = sb("raw", [P, 2, KT * P])
        tile = sb("tile", [P, 13, T])
        con = sb("con", [P, K_ALL])
        par = sb("par", [P, C_ALL])
        c_sb = sb("c_sb", [P, KT])
        ones = sb("ones", [P, 1])
        eps = sb("eps", [P, 1])
        mod = sb("mod", [P, 48])
        a_mix = sb("a_mix", [P, KT])
        a_mlp = sb("a_mlp", [P, KT])
        a_da = sb("a_da", [P, 1])
        rms = sb("rms", [P, 6, KT])
        rstd = sb("rstd", [P, KT])
        lam = sb("lam", [P, 8])
        mx = sb("mx", [P, 4])
        mxp = sb("mxp", [P, 4])
        sm = sb("sm", [P, 4])
        rc = sb("rc", [P, 4])
        swm = sb("swm", [P, 16])
        swn = sb("swn", [P, 16])
        sws = sb("sws", [P, 16])
        swe = sb("swe", [P, 16])
        swd = sb("swd", [P, 16])
        swr = sb("swr", [P, 16])
        negsink = sb("negsink", [P, 8])
        exp_a = sb("exp_a", [P, HEADS])
        gpar = sb("gpar", [P, 34])

        dtm = tile[:, 12, :].rearrange("p (n x) -> p n x", n=8)
        id_ = con[:, K_ID:K_ID + P]
        tri = con[:, K_TRI:K_TRI + P]

        acc = [ctx.enter_context(nc.psum_tensor(f"acc{i}", [P, T], F32)) for i in range(2)]
        wk = [ctx.enter_context(nc.psum_tensor(f"wk{i}", [P, T], F32)) for i in range(2)]
        bank = [wk[0][:, 0:HALF], wk[0][:, HALF:T], wk[1][:, 0:HALF], wk[1][:, HALF:T]]

        merged_d = nc.dram_tensor("merged_d", [KT, P, T], F32, kind="Internal").ap()
        o_d = nc.dram_tensor("o_d", [DA_HEADS, P, T], F32, kind="Internal").ap()
        cs_d = nc.dram_tensor("cs_d", [P, P], F32, kind="Internal").ap()

        S = {}
        for name in """par_in lam_in con_in c_in w_in0 w_in1 x_in0 x_in1 x_in2 x_in3 ada_in0 ada_in1 ada_in2 ada_in3
            split_hi split_ready block_done acc_free0 acc_free1
            mod_done sq_ready sq_used ms_ready root_ready rstd_ready bcast_ready h_scaled h_hi_ready h_ready
            dve_own gates_free relu_free da_tab_in
            qkv_ready v_turned v_tok scored biased negmax exped weighted turned turned_sb pv_done o_copied
            da_clipped da_sq da_ms da_root da_rstd da_bcast da_scaled da_hi u_ready lam_dots lam_exps
            o_saved o_back sw_split sw_tab_in sw_qkv sw_scored sw_biased sw_negmax sw_exped sw_weighted sw_turned sw_turned_sb
            sw_out sw_hi
            gate_ready ab_free merged_out merged_saved
            dt_turned dt_abs dt_exp dt_da cs_ready cs_copied cs_saved dt_diff dt_decays
            conv_first conv_done conv_silu csb_in diff_ready relu_ready l_ready e_ready x_turned g_ready btok_ready
            g_masked xd_ready c_decayed m_ready s_ready y_ready y_taken state_ready
            z_silu z_used y_gated ssm_sq ssm_ms ssm_root ssm_rstd ssm_bcast ssm_scaled ssm_hi y_split
            c_gate c_free merged_in0 merged_in1 merged_all merged_hi merged_ready
            x2_in x1_ready x1_sq x1_sum n2_ms n2_root n2_rstd n2_bcast n2_scaled n2_hi n2_ready n2_full n2_odd_ready
            hid_relu hid_sq hid_hi hid_ready x2_ready f_sq f_sum f_ms f_root f_rstd f_bcast f_ready out_saved
            mix_shifted mix_weighed mix_reduced pool_own mix_mod_done ada_used mod_rest""".split():
            S[name] = sem(name)
        w_in_s = [S["w_in0"], S["w_in1"]]
        x_in_s = [S["x_in0"], S["x_in1"], S["x_in2"], S["x_in3"]]
        ada_s = [S[f"ada_in{n}"] for n in range(4)]
        acc_free = [S["acc_free0"], S["acc_free1"]]
        merged_s = [S["merged_in0"], S["merged_in1"]]

        xres = [tile[:, k, :] for k in range(KT)]
        mix_banks = [bank[2], acc[1][:, 0:HALF], acc[1][:, HALF:T], bank[3]]
        block = ctx.enter_context(nc.Block())

        @block.sync
        def _(sp):
            sp.dma_start(par[:], par_in).then_inc(S["par_in"], 16)
            sp.dma_start(tile[:, 11, 0:4 * HD], lam_v).then_inc(S["lam_in"], 16)
            sp.dma_start(c_sb[:], c_in).then_inc(S["c_in"], 16)
            for q in range(4):
                sp.dma_start(tile[:, 2 * q:2 * q + 2, :],
                             x_in[2 * q:2 * q + 2].rearrange("k p t -> p k t")).then_inc(x_in_s[q], 16)
                if q == 0:
                    sp.dma_start(con[:], con_in).then_inc(S["con_in"], 16)
            for k in range(KT):
                if k == 1:
                    sp.wait_ge(S["sq_used"], KT)
                if k >= 2:
                    sp.wait_ge(S["mix_mod_done"], k - 1)
                sp.dma_start(tile[:, (8, 10)[k % 2], :], ada_in[k]).then_inc(ada_s[k % 2], 16)
                if k >= 2:
                    sp.wait_ge(S["mix_reduced"], k - 1)
                sp.dma_start(tile[:, (9, 12)[k % 2], :], ada_in[KT + k]).then_inc(ada_s[2 + k % 2], 16)
                if k < 2:
                    sp.dma_start(raw[:, k], w_in[k]).then_inc(w_in_s[k], 16)
            with sp.Fori(0, (N_ALL - 3) // 2) as i:
                for b in range(2):
                    sp.wait_ge(S["split_ready"], i * 2 + b + 1)
                    sp.dma_start(raw[:, b], w_in[bass.ds(i * 2 + 2 + b, 1)].rearrange("a p c -> (a p) c")
                                 ).then_inc(w_in_s[b], 16)
            sp.wait_ge(S["split_ready"], N_ALL - 2)
            sp.dma_start(raw[:, 0], w_in[N_ALL - 1]).then_inc(w_in_s[0], 16)

        @block.gpsimd
        def _(pool):
            def split(b, n, trip, first):
                pool.wait_ge(w_in_s[b], trip * 16 + 16)
                if not first:
                    pool.wait_ge(S["block_done"], n - 1)
                pool.nop(nofuse=True)
                pool.tensor_scalar(flat(w_hi[b][:]), raw[:, b], 1.0, 1.0, ALU.mult, ALU.mult).then_inc(S["split_hi"], 1)
                pool.wait_ge(S["split_hi"], n + 1)
                pool.tensor_tensor(flat(w_lo[b][:]), raw[:, b], flat(w_hi[b][:].bitcast(F32)),
                                   ALU.subtract).then_inc(S["split_ready"], 1)

            own = Steps(pool, S["pool_own"])
            pool.wait_ge(S["c_in"], 16)
            for k in range(KT):
                block_k = tile[:, (8, 10)[k % 2], :]
                rows = block_k.rearrange("p (k c) -> p k c", k=KT)
                pool.wait_ge(ada_s[k % 2], 16 * (k // 2) + 16)
                own.mark(pool.tensor_tensor(rows, rows, c_sb[:].unsqueeze(2).to_broadcast([P, KT, P]), ALU.mult))
                for w in (4 * P, 2 * P, P):
                    own.settle()
                    half = pool.tensor_tensor(block_k[:, 0:w], block_k[:, 0:w], block_k[:, w:2 * w], ALU.add)
                    if w > P:
                        own.mark(half)
                half.then_inc(S["mix_shifted"], 1)
                if k < 2:
                    split(k, k, 0, True)
            pool.sem_inc(S["y_split"], 1)
            first = N_SSM + 8
            with pool.Fori(0, (first - 3) // 2) as i:
                for b in range(2):
                    split(b, i * 2 + 2 + b, i + 1, False)
            split((first - 1) % 2, first - 1, (first - 1) // 2, False)
            with pool.Fori(0, GROUPS) as g:
                def split_of(n):
                    split(n % 2, g * 10 + n, g * 5 + n // 2, False)

                def decay_c(c):
                    pool.wait_ge(S["e_ready"], g * NT + c + 1)
                    decays = tile[:, 8 + c % 2, :].rearrange("p (h x) -> p h x", h=GH)
                    pool.tensor_tensor(decays, decays, tile[:, 5, c * P:(c + 1) * P].unsqueeze(1).to_broadcast([P, GH, P]),
                                       ALU.mult).then_inc(S["c_decayed"], 1)

                for c in range(3):
                    decay_c(c)
                split_of(first)
                for c in range(3, NT):
                    decay_c(c)
                for n in range(first + 1, first + 5):
                    split_of(n)
                for j in range(4):
                    pool.wait_ge(S["ssm_hi"], g * 4 + j + 1)
                    dst = bass.ds(g * 4 + j, 1)
                    pool.tensor_tensor(u_lo[:, dst, :].rearrange("p a t -> p (a t)"), tile[:, j, :],
                                       u_hi[:, dst, :].rearrange("p a t -> p (a t)").bitcast(F32), ALU.subtract
                                       ).then_inc(S["y_split"], 1)
                for n in range(first + 5, first + 10):
                    split_of(n)
            rest = first + 10 * GROUPS

            def splits_between(start, stop):
                with pool.Fori(0, (stop - start) // 2) as i:
                    for n in (start, start + 1):
                        split(n % 2, i * 2 + n, i + n // 2, False)

            splits_between(rest, N_MLP + 2)
            for k in range(1, KT, 2):
                pool.wait_ge(S["n2_full"], k // 2 + 1)
                pool.tensor_tensor(h_lo[:, k, :], tile[:, 10, :] if k % 4 == 1 else tile[:, 12, :],
                                   h_hi[:, k, :].bitcast(F32), ALU.subtract).then_inc(S["n2_odd_ready"], 1)
            splits_between(N_MLP + 2, N_ALL)

        @block.tensor
        def _(pe):
            def step(b, pair, k, rhs_hi, rhs_lo):
                if k == 0:
                    pe.wait_ge(S["split_ready"], pair * 2 + b + 1)
                    pe.wait_ge(acc_free[b], pair + 1)
                mm = terms(b, k, rhs_hi, rhs_lo, acc[b], k == 0, k == KT - 1)
                if k == KT - 1:
                    mm.then_inc(S["block_done"], 1)

            def terms(b, k, rhs_hi, rhs_lo, psum, first, last):
                for t, (w, r) in enumerate(((w_hi, rhs_hi), (w_hi, rhs_lo), (w_lo, rhs_hi))):
                    for half in range(2):
                        cols = slice(half * HALF, (half + 1) * HALF)
                        mm = pe.matmul(psum[:, cols], w[b][:, k, :], r[:, k, cols],
                                       start=first and t == 0, stop=last and t == 2)
                return mm

            def dense(b, pair, rhs_hi, rhs_lo, moving=None):
                pe.wait_ge(S["split_ready"], pair * 2 + b + 1)
                pe.wait_ge(acc_free[b], pair + 1)
                for k in range(KT):
                    if moving is not None:
                        moving(k)
                    mm = terms(b, k, rhs_hi, rhs_lo, acc[b], k == 0, k == KT - 1)
                mm.then_inc(S["block_done"], 1)

            def counted(ready, base):
                return lambda k: pe.wait_ge(ready, base + k + 1)

            def n2_tile(k):
                pe.wait_ge(S["n2_odd_ready"] if k % 2 else S["n2_ready"], k // 2 + 1)

            def row_means(total, signal, at=0, psum=None):
                for c in range(NT):
                    mm = pe.matmul((psum or bank[3])[:, at + c:at + c + 1], total[:, c * P:(c + 1) * P], ones[:, 0:1],
                                   start=True, stop=True)
                mm.then_inc(signal, 1)

            def broadcast(signal, psum=None):
                for c in range(NT):
                    mm = pe.matmul((psum or wk[0])[:, c * P:(c + 1) * P], rstd[:, c:c + 1].to_broadcast([P, P]), id_,
                                   start=True, stop=True)
                mm.then_inc(signal, 1)

            def mix_modulation(k):
                pe.wait_ge(S["mix_shifted"], k + 1)
                pe.matmul(mix_banks[k % 4][:, 0:1], tile[:, (8, 10)[k % 2], 0:P], ones[:, 0:1], start=True, stop=True)
                pe.wait_ge(S["mix_reduced"], k + 1)
                pe.matmul(mix_banks[k % 4][:, 1:2], tile[:, 11, (k % 2) * P:(k % 2 + 1) * P], ones[:, 0:1],
                          start=True, stop=True).then_inc(S["mix_mod_done"], 1)

            pe.wait_ge(S["sq_used"], KT)
            row_means(tile[:, 11, :], S["ms_ready"])
            pe.wait_ge(S["rstd_ready"], 1)
            pe.wait_ge(S["con_in"], 16)
            broadcast(S["bcast_ready"])
            mix_modulation(0)
            for k in range(KT):
                if k + 1 < KT:
                    mix_modulation(k + 1)
                pe.wait_ge(S["h_ready"], k + 1)
                step(0, 0, k, h_hi, h_lo)

            def turn_v(b, triple):
                pe.wait_ge(S["qkv_ready"], triple * 3 + 1)
                for j in range(NT):
                    mm = pe.transpose(acc[b][:, j * P:(j + 1) * P], tile[:, 10, j * P:(j + 1) * P], id_)
                mm.then_inc(S["v_turned"], 1)

            dense(1, 0, h_hi, h_lo)
            turn_v(0, 0)
            dense(0, 1, h_hi, h_lo)

            def da_head(t, s):
                head = t * 2 + s
                kt, qt, vt = (0, 11)[s], (1, 2)[s], (3, 12)[s]
                done = [0]

                def steps(count):
                    for _ in range(count):
                        n = 3 * (s + 1) + done[0] // KT
                        step(n % 2, t * 3 + n // 2, done[0] % KT, h_hi, h_lo)
                        done[0] += 1

                def scores(i, m):
                    if i or m:
                        pe.wait_ge(S["biased"], head * 16 + 2 * i + m)
                    rows = slice(m * HD, (m + 1) * HD)
                    for lo in range(0, (i + 1) * P, HALF):
                        hi = min(lo + HALF, (i + 1) * P)
                        mm = pe.matmul(wk[0][:, lo:hi], tile[rows, qt, i * P:(i + 1) * P], tile[rows, kt, lo:hi],
                                       start=True, stop=True)
                    mm.then_inc(S["scored"], 1)

                def turn(i, half):
                    n = PIECES.index((i, half))
                    pe.wait_ge(S["weighted"], head * 8 + i + 1)
                    if n:
                        pe.wait_ge(S["turned_sb"], head * NP_ + n)
                    src = (5, 7)[i % 2]
                    for j in range(4 * half, min(4 * half + 4, i + 1)):
                        mm = pe.transpose(bank[2][:, (j % 4) * P:(j % 4 + 1) * P], tile[:, src, j * P:(j + 1) * P], id_)
                    mm.then_inc(S["turned"], 1)

                def attend(i, half):
                    n = PIECES.index((i, half))
                    pe.wait_ge(S["turned_sb"], head * NP_ + n + 1)
                    if i == 4 and half == 0:
                        pe.wait_ge(S["o_copied"], head * 2 + 1)
                    for j in range(4 * half, min(4 * half + 4, i + 1)):
                        at = (n % 2) * HALF + (j % 4) * P
                        mm = pe.matmul(bank[3][:, (i % 4) * P:(i % 4 + 1) * P], tile[:, vt, j * P:(j + 1) * P],
                                       tile[:, 9, at:at + P], start=j == 0, stop=j == i)
                    mm.then_inc(S["pv_done"], 1)

                pe.wait_ge(S["v_tok"], head + 1)
                pe.wait_ge(S["qkv_ready"], head * 3 + 3)
                for i in range(NT):
                    two = i > 4
                    steps(1)
                    if i == 4:
                        turn_v((3 * (s + 1)) % 2, head + 1)
                    if i > 5:
                        attend(i - 2, 1)
                    scores(i, 0)
                    steps(1)
                    scores(i, 1)
                    if i:
                        turn(i - 1, 0)
                    if i > 2:
                        steps(1)
                    if i:
                        attend(i - 1, 0)
                    if two:
                        turn(i - 1, 1)
                attend(NT - 2, 1)
                steps(1)
                turn(NT - 1, 0)
                steps(1)
                attend(NT - 1, 0)
                turn(NT - 1, 1)
                steps(1)
                assert done[0] == 3 * KT
                attend(NT - 1, 1)

            with pe.Fori(0, DA_HEADS // 2) as t:
                for s in range(2):
                    da_head(t, s)

            def sw_pair(t, s):
                j = t * 2 + s
                qt = (1, 2)[s]
                done = [0]

                def steps(count):
                    for _ in range(count):
                        n = N_SW + 3 + s
                        step(n % 2, t + n // 2, done[0], h_hi, h_lo)
                        done[0] += 1

                def scores(i):
                    pe.wait_ge(S["sw_biased"], j * NT + i + 1)
                    lo = max(i - 1, 0) * P
                    w = (i + 1) * P - lo
                    for g in range(2):
                        rows = slice(g * HD, (g + 1) * HD)
                        mm = pe.matmul(bank[g][:, 256 - w:256], tile[rows, qt, i * P:(i + 1) * P],
                                       tile[rows, 0, lo:lo + w], start=True, stop=True)
                    mm.then_inc(S["sw_scored"], 1)

                def turn(i):
                    pe.wait_ge(S["sw_weighted"], j * NT + i + 1)
                    pe.wait_ge(S["sw_turned_sb"], j * NT + i + 1)
                    for g in range(2):
                        for kb in range(0 if i else 1, 2):
                            at = (g * 2 + kb) * P
                            src = (i % 2) * HALF + g * 256 + kb * P
                            mm = pe.transpose(bank[2][:, at:at + P], tile[:, 5 + (i % 4) // 2, src:src + P], id_)
                    mm.then_inc(S["sw_turned"], 1)

                def attend(i):
                    pe.wait_ge(S["sw_turned_sb"], j * NT + i + 2)
                    if i % 4 == 0:
                        pe.wait_ge(S["sw_split"], j * 2 + i // 4 + 1)
                    for g in range(2):
                        rows = slice(g * HD, (g + 1) * HD)
                        for kb in range(0 if i else 1, 2):
                            jj = i - 1 + kb
                            at = (i % 2) * HALF + (g * 2 + kb) * P
                            mm = pe.matmul(bank[3][rows, (i % 4) * P:(i % 4 + 1) * P],
                                           tile[:, 3, jj * P + g * HD:jj * P + (g + 1) * HD],
                                           tile[:, 9, at:at + P], start=kb == (0 if i else 1), stop=kb == 1)
                    mm.then_inc(S["sw_out"], 1)

                steps(1)
                pe.wait_ge(S["sw_qkv"], j + 1)
                for i in range(NT):
                    scores(i)
                    if i >= 2:
                        turn(i - 2)
                    if i == 3:
                        pe.wait_ge(S["da_sq"], j * 2 + 1)
                        row_means(tile[:, 8, :], S["da_ms"], 0, acc[s])
                    elif i == 4:
                        pe.wait_ge(S["da_sq"], j * 2 + 2)
                        row_means(tile[:, 12, :], S["da_ms"], NT, acc[s])
                    else:
                        steps(1)
                    if i >= 2:
                        attend(i - 2)
                turn(NT - 2)
                pe.wait_ge(S["da_rstd"], j + 1)
                broadcast(S["da_bcast"], acc[s])
                attend(NT - 2)
                turn(NT - 1)
                steps(1)
                attend(NT - 1)
                pe.wait_ge(S["da_scaled"], j + 1)

            pe.wait_ge(S["v_tok"], DA_HEADS + 1)
            pe.wait_ge(S["o_copied"], 2 * DA_HEADS)
            with pe.Fori(0, SW_PAIRS // 2) as t:
                for s in range(2):
                    sw_pair(t, s)

            pe.wait_ge(S["sw_qkv"], SW_PAIRS + 1)
            pe.wait_ge(S["sw_biased"], SW_PAIRS * NT + 1)
            for c in range(NT):
                mm = pe.transpose(bank[0][:, c * HEADS:(c + 1) * HEADS], tile[0:HEADS, 1, c * P:(c + 1) * P], id_[0:HEADS, 0:HEADS])
            mm.then_inc(S["dt_turned"], 1)
            pe.wait_ge(S["sw_turned_sb"], SW_PAIRS * NT + 1)

            pe.sem_inc(S["mod_done"], 8)
            with pe.Fori(0, KT // 2) as t:
                for s in range(2):
                    for q in range(3):
                        n = N_AB + 3 * s + q
                        pair = t * 3 + n // 2
                        if q < 2:
                            dense(n % 2, pair, h_hi, h_lo)
                        else:
                            pe.wait_ge(S["split_ready"], pair * 2 + n % 2 + 1)
                            pe.wait_ge(S["ab_free"], t * 2 + s + 1)
                            for k in range(KT):
                                mm = terms(n % 2, k, u_hi, u_lo, wk[0] if k < 4 else acc[n % 2],
                                           k % 4 == 0, k % 4 == 3)
                                if k == 3:
                                    pe.wait_ge(acc_free[n % 2], pair + 1)
                            mm.then_inc(S["block_done"], 1)
                    for q in range(4):
                        pe.wait_ge(S["ada_used"], t * 8 + (4 * s + q + 5))
                        at = (4 * s + q) * P
                        pe.matmul(bank[2][:, bass.ds(t * 8 + (16 + 4 * s + q), 1)], tile[:, 7, at:at + P], ones[:, 0:1],
                                  start=True, stop=True).then_inc(S["mod_done"], 1)

            pe.wait_ge(S["dt_da"], 1)
            pe.wait_ge(S["ab_free"], KT + 1)
            a_tok = dtm[:, 0, :]
            pe.matmul(bank[1][:, 0:P], a_tok, tri, start=True, stop=True)
            pe.matmul(bank[1][:, P:2 * P], tri, a_tok, start=True, stop=True)
            pe.matmul(bank[1][:, 2 * P:3 * P], ones[:].to_broadcast([P, P]), a_tok, start=True, stop=True
                      ).then_inc(S["cs_ready"], 1)

            def dense_and_norm(b, pair, g):
                for k in range(KT):
                    step(b, pair, k, h_hi, h_lo)
                    if k == 4:
                        pe.wait_ge(S["ssm_sq"], g * 4 + 4)
                        row_means(tile[:, 10, :], S["ssm_ms"])
                    if k == 6:
                        pe.wait_ge(S["ssm_rstd"], g + 1)
                        broadcast(S["ssm_bcast"])

            for g in range(GROUPS):
                def turn_chunk(c):
                    cols = slice(c * P, (c + 1) * P)
                    if c:
                        pe.wait_ge(S["xd_ready"], g * 16 + 2 * c)
                        pe.wait_ge(S["btok_ready"], g * NT + c)
                        pe.wait_ge(S["g_masked"], g * NT + c)
                    for j in range(4):
                        mm = pe.transpose(bank[0][:, j * P:(j + 1) * P], tile[:, j, cols], id_)
                    mm.then_inc(S["x_turned"], 1)
                    pe.transpose(bank[1][:, 0:P], tile[:, 4, cols], id_)
                    pe.matmul(bank[1][:, P:2 * P], tile[:, 4, cols], tile[:, 5, cols], start=True, stop=True
                              ).then_inc(S["g_ready"], 1)

                def chunk_state(c):
                    pe.wait_ge(S["xd_ready"], g * 16 + 2 * c + 2)
                    pe.wait_ge(S["btok_ready"], g * NT + c + 1)
                    pe.wait_ge(S["state_ready"], g * (NT + 1) + c + 1)
                    pe.matmul(bank[2][:, :], tile[:, 11, HALF:HALF + P], tile[:, 12, 0:HALF], start=True, stop=True
                              ).then_inc(S["s_ready"], 1)

                def chunk_out(c):
                    pe.wait_ge(S["m_ready"], g * NT + c + 1)
                    pe.wait_ge(S["c_decayed"], g * NT + c + 1)
                    pe.wait_ge(S["state_ready"], g * (NT + 1) + c + 1)
                    if c:
                        pe.wait_ge(S["y_taken"], g * NT * 4 + 4 * c)
                    for r in range(GH):
                        rows = slice((r % 2) * HD, (r % 2 + 1) * HD)
                        o = bank[3][rows, (r // 2) * P:(r // 2 + 1) * P]
                        xd = (c % 2) * HALF + r * HD
                        pe.matmul(o, tile[:, 10, xd:xd + HD], tile[:, 6 + c % 2, r * P:(r + 1) * P],
                                  start=True, stop=False)
                        mm = pe.matmul(o, tile[:, 11, r * HD:(r + 1) * HD], tile[:, 8 + c % 2, r * P:(r + 1) * P],
                                       start=False, stop=True)
                    mm.then_inc(S["y_ready"], 1)

                done = [0]

                def steps(count):
                    for _ in range(count):
                        n = N_SSM + 10 * g + 6 + done[0] // KT
                        step(n % 2, n // 2, done[0] % KT, h_hi, h_lo)
                        done[0] += 1

                n = N_SSM + 10 * g
                if g:
                    dense_and_norm(n % 2, n // 2, g - 1)
                else:
                    dense(n % 2, n // 2, h_hi, h_lo)
                for n in range(n + 1, n + 6):
                    dense(n % 2, n // 2, h_hi, h_lo)
                steps(5)
                if g:
                    pe.wait_ge(S["ssm_scaled"], g * 4)
                else:
                    pe.wait_ge(S["cs_copied"], 2)
                    pe.wait_ge(S["mod_rest"], 1)
                pe.wait_ge(S["conv_silu"], g * 6 + 6)
                turn_chunk(0)
                steps(1)
                chunk_state(0)
                for c in range(NT):
                    if c + 1 < NT:
                        turn_chunk(c + 1)
                    steps(0 if c else 1)
                    chunk_out(c)
                    steps(1)
                    if c + 1 < NT:
                        chunk_state(c + 1)
                    steps(0 if c else 1)
                assert done[0] == 2 * KT
                for n in range(N_SSM + 10 * g + 8, N_SSM + 10 * g + 10):
                    dense(n % 2, n // 2, h_hi, h_lo)

            def merge_c(m, t, first):
                n = N_C + 2 * m
                if first:
                    dense_and_norm(n % 2, n // 2, GROUPS - 1)
                else:
                    dense(n % 2, t + n // 2, h_hi, h_lo)
                dense((n + 1) % 2, t + (n + 1) // 2, u_hi, u_lo, counted(S["y_split"], 1) if first else None)

            merge_c(0, 0, True)
            with pe.Fori(0, KT - 1) as t:
                merge_c(1, t, False)

            with pe.Fori(0, KT // 2) as t:
                for s in range(2):
                    n = N_OUT + s
                    dense(n % 2, t + n // 2, h_hi, h_lo, counted(S["merged_ready"], 0) if s == 0 else None)
            pe.wait_ge(S["x1_sum"], KT)
            row_means(tile[:, 11, :], S["n2_ms"])
            pe.wait_ge(S["n2_rstd"], 1)
            broadcast(S["n2_bcast"])

            with pe.Fori(0, QUARTERS) as q4:
                with pe.Fori(0, KT // 2) as t:
                    for s in range(2):
                        n = N_MLP + s
                        dense(n % 2, q4 * 8 + t + n // 2, h_hi, h_lo, n2_tile if s == 0 else None)
                with pe.Fori(0, KT // 2) as t:
                    for s in range(2):
                        n = N_MLP + 8 + s
                        dense(n % 2, q4 * 8 + t + n // 2, u_hi, u_lo, counted(S["hid_ready"], q4 * 8) if s == 0 else None)
            pe.wait_ge(S["f_sum"], KT)
            row_means(tile[:, 11, :], S["f_ms"])
            pe.wait_ge(S["f_rstd"], 1)
            broadcast(S["f_bcast"])

        @block.scalar
        def _(act):
            act.sem_inc(S["o_saved"], 16)
            act.sem_inc(S["merged_saved"], 16)

            def root(width, signal):
                act.activation(rms[:, 1, 0:NT], rms[:, 0, 0:NT], ACT.Sqrt, bias=eps[:, 0:1], scale=1.0 / width
                               ).then_inc(signal, 1)

            for k in range(KT):
                act.wait_ge(x_in_s[k // 2], 16)
                if k >= 2:
                    act.wait_ge(S["sq_used"], k - 1)
                act.activation(tile[:, 10 + 2 * (k % 2), :], xres[k], ACT.Square).then_inc(S["sq_ready"], 1)
            act.wait_ge(S["lam_dots"], 2)
            act.activation(lam[:, 2:4], lam[:, 0:2], ACT.Exp).then_inc(S["lam_exps"], 1)

            def scale_rows(k):
                act.wait_ge(ada_s[2 + k % 2], 16 * (k // 2) + 16)
                for n in range(KT):
                    rows = tile[:, (9, 12)[k % 2], n * P:(n + 1) * P]
                    last = act.activation(rows, rows, ACT.Identity, scale=c_sb[:, n:n + 1])
                last.then_inc(S["mix_weighed"], 1)

            act.wait_ge(S["c_in"], 16)
            scale_rows(0)
            act.wait_ge(S["root_ready"], 1)
            root(D, S["root_ready"])
            for k in range(KT):
                if k + 1 < KT:
                    scale_rows(k + 1)
                act.wait_ge(S["h_scaled"], k + 1)
                act.activation(h_hi[:, k, :], xres[k], ACT.Identity, bias=mod[:, k:k + 1]).then_inc(S["h_hi_ready"], 1)

            def triple_v(b, triple):
                act.wait_ge(S["block_done"], triple * 3 + 1)
                act.activation(tile[:, 10, :], acc[b][:], ACT.Copy).then_inc(S["qkv_ready"], 1)

            def triple_v_tok(b, dst, triple):
                act.wait_ge(S["v_turned"], triple + 1)
                act.activation(tile[:, dst, :], acc[b][:], ACT.Copy).then_inc(S["v_tok"], 1)
                act.wait_ge(S["v_tok"], triple + 1)
                act.sem_inc(acc_free[b], 1)

            def triple_kq(b, q, dst, triple):
                act.wait_ge(S["block_done"], triple * 3 + q + 1)
                act.activation(tile[:, dst, :], acc[b][:], ACT.Copy).then_inc(S["qkv_ready"], 1)
                act.wait_ge(S["qkv_ready"], triple * 3 + q + 1)
                act.sem_inc(acc_free[b], 1)

            act.dma_start(tile[:, 4, :], da_tab[0]).then_inc(S["da_tab_in"], 16)
            triple_v(0, 0)
            triple_kq(1, 1, 0, 0)
            triple_v_tok(0, 3, 0)
            triple_kq(0, 2, 1, 0)

            def da_head(s, head):
                new = [(3 * (s + 1) + q) % 2 for q in range(3)]

                def exp(i, m):
                    act.wait_ge(S["negmax"], head * 16 + 2 * i + m + 1)
                    col = 2 * (i % 2) + m
                    src = tile[:, (5, 6, 7, 8)[col], 0:(i + 1) * P]
                    act.activation(src, src, ACT.Exp, bias=mx[:, col:col + 1], accum_out=sm[:, col:col + 1]
                                   ).then_inc(S["exped"], 1)

                def piece(i, half):
                    n = PIECES.index((i, half))
                    act.wait_ge(S["turned"], head * NP_ + n + 1)
                    if n >= 2:
                        act.wait_ge(S["pv_done"], head * NP_ + n - 1)
                    w = (min(4 * half + 4, i + 1) - 4 * half) * P
                    act.activation(tile[:, 9, (n % 2) * HALF:(n % 2) * HALF + w], bank[2][:, 0:w], ACT.Copy
                                   ).then_inc(S["turned_sb"], 1)

                def copy_o(half):
                    n = PIECES.index((4 * half + 3, half))
                    act.wait_ge(S["pv_done"], head * NP_ + n + 1)
                    act.activation(tile[:, 10, half * HALF:(half + 1) * HALF], bank[3], ACT.Copy
                                   ).then_inc(S["o_copied"], 1)

                for i in range(NT):
                    if i == 4:
                        act.wait_ge(S["o_saved"], head * 16 + 16)
                        triple_v(new[0], head + 1)
                    exp(i, 0)
                    if i:
                        piece(i - 1, 0)
                    exp(i, 1)
                    if i > 4:
                        piece(i - 1, 1)
                    if i == 4:
                        triple_v_tok(new[0], (12, 3)[s], head + 1)
                        copy_o(0)
                    if i == 6:
                        triple_kq(new[1], 1, (11, 0)[s], head + 1)
                act.dma_start(tile[:, 4, :], da_tab[bass.ds(head + 1, 1)].rearrange("a p x -> (a p) x")
                              ).then_inc(S["da_tab_in"], 16)
                piece(NT - 1, 0)
                piece(NT - 1, 1)
                triple_kq(new[2], 2, (2, 1)[s], head + 1)
                copy_o(1)
                act.wait_ge(S["o_copied"], head * 2 + 2)
                act.dma_start(o_d[bass.ds(head, 1)].rearrange("a p t -> (a p) t"), tile[:, 10, :]).then_inc(S["o_saved"], 16)

            with act.Fori(0, DA_HEADS // 2) as t:
                for s in range(2):
                    da_head(s, t * 2 + s)

            act.sem_inc(S["sw_qkv"], 1)
            act.sem_inc(S["sw_turned_sb"], 1)
            act.wait_ge(S["o_saved"], 16 * DA_HEADS + 16)
            with act.Fori(0, SW_PAIRS // 2) as t:
                for s in range(2):
                    j = t * 2 + s
                    act.dma_start(tile[:, 4, s * HALF:(s + 1) * HALF], sw_tab[bass.ds(j, 1)].rearrange("a p x -> (a p) x")
                                  ).then_inc(S["sw_tab_in"], 16)
                    act.wait_ge(S["da_hi"], j + 1)
                    act.dma_start(tile[:, 10, :], o_d[bass.ds(j, 1)].rearrange("a p t -> (a p) t")
                                  ).then_inc(S["o_back"], 16)

                    def exps(i):
                        act.wait_ge(S["sw_negmax"], j * NT + i + 1)
                        for g in range(2):
                            lo = (i % 2) * HALF + g * 256 + (0 if i else P)
                            src = tile[:, 5 + (i % 4) // 2, lo:(i % 2) * HALF + (g + 1) * 256]
                            col = 2 * (i % 4) + g
                            act.activation(src, src, ACT.Exp, bias=swn[:, col:col + 1], accum_out=sws[:, col:col + 1])
                        cols = slice(2 * (i % 4), 2 * (i % 4) + 2)
                        act.activation(swe[:, cols], swd[:, cols], ACT.Exp).then_inc(S["sw_exped"], 1)

                    def piece(i):
                        act.wait_ge(S["sw_turned"], j * NT + i + 1)
                        if i >= 2:
                            act.wait_ge(S["sw_out"], j * NT + i - 1)
                        for a, z in ((P, 256), (256 + P, HALF)) if i == 0 else ((0, HALF),):
                            last = act.activation(tile[:, 9, (i % 2) * HALF + a:(i % 2) * HALF + z],
                                                  bank[2][:, a:z], ACT.Copy)
                        last.then_inc(S["sw_turned_sb"], 1)

                    def out_hi(half):
                        act.wait_ge(S["sw_out"], j * NT + 4 * half + 4)
                        act.activation(u_hi[:, bass.ds(j + 4, 1), half * HALF:(half + 1) * HALF].rearrange("p a t -> p (a t)"),
                                       bank[3], ACT.Copy).then_inc(S["sw_hi"], 1)

                    for i in range(NT):
                        if i >= 2:
                            piece(i - 2)
                        exps(i)
                        if i == 2:
                            act.wait_ge(S["da_clipped"], j * 2 + 1)
                            act.activation(tile[:, 8, :], tile[:, 8, :], ACT.Square).then_inc(S["da_sq"], 1)
                        if i == 3:
                            act.wait_ge(S["da_clipped"], j * 2 + 2)
                            act.activation(tile[:, 12, :], tile[:, 10, :], ACT.Square, scale=2.0 ** -30).then_inc(S["da_sq"], 1)
                        if i == 5:
                            out_hi(0)
                        if i == 6:
                            act.wait_ge(S["da_root"], j * 2 + 1)
                            root(P, S["da_root"])
                    piece(NT - 2)
                    piece(NT - 1)
                    n = N_SW + 3 + s
                    act.wait_ge(S["block_done"], j + N_SW + 4)
                    act.activation(tile[:, (2, 1)[s], :], acc[n % 2][:], ACT.Copy).then_inc(S["sw_qkv"], 1)
                    act.wait_ge(S["sw_qkv"], j + 2)
                    act.sem_inc(acc_free[n % 2], 1)
                    out_hi(1)
                    act.wait_ge(S["da_scaled"], j + 1)
                    act.activation(u_hi[:, bass.ds(j, 1), :].rearrange("p a t -> p (a t)"), tile[:, 12, :], ACT.Copy
                                   ).then_inc(S["da_hi"], 1)

            act.wait_ge(S["dt_abs"], 1)
            act.activation(dtm[:, 2, :], dtm[:, 1, :], ACT.Exp, scale=-1.0)
            act.activation(exp_a[:], par[:, C_ALOG:C_ALOG + HEADS], ACT.Exp).then_inc(S["dt_exp"], 1)

            with act.Fori(0, KT // 2) as t:
                for s in range(2):
                    m = t * 2 + s
                    for q in range(4):
                        b = 4 * s + q
                        act.wait_ge(S["ada_used"], t * 8 + (b + 1))
                        act.dma_start(tile[:, 8 + q, :], ada_in[bass.ds(t * 8 + (16 + b), 1)].rearrange("a p c -> (a p) c")
                                      ).then_inc(ada_s[q], 16)
                    for q in range(2):
                        n = N_AB + 3 * s + q
                        act.wait_ge(S["block_done"], m * 3 + (N_AB + q + 1))
                        if q == 0:
                            act.wait_ge(S["gates_free"], m + 1)
                        act.activation(tile[:, q, :], acc[n % 2][:], ACT.Sigmoid).then_inc(S["gate_ready"], 1)
                        act.wait_ge(S["gate_ready"], m * 2 + q + 1)
                        act.sem_inc(acc_free[n % 2], 1)
                    act.wait_ge(S["merged_out"], m + 1)
                    act.dma_start(merged_d[bass.ds(m, 1)].rearrange("a p t -> (a p) t"), tile[:, 4 + s, :]
                                  ).then_inc(S["merged_saved"], 16)

            act.wait_ge(S["cs_ready"], 1)
            act.activation(dtm[:, 5, :], bank[1][:, 2 * P:3 * P], ACT.Exp)
            act.activation(dtm[:, 1, :], bank[1][:, 0:P], ACT.Copy).then_inc(S["cs_copied"], 1)
            act.wait_ge(S["cs_copied"], 1)
            act.dma_start(cs_d, dtm[:, 1, :]).then_inc(S["cs_saved"], 16)
            act.wait_ge(S["dt_diff"], 1)
            act.activation(dtm[:, 6, :], dtm[:, 6, :], ACT.Exp).then_inc(S["dt_decays"], 1)
            act.wait_ge(S["cs_saved"], 16)

            with act.Fori(0, GROUPS) as g:
                def load_sums(c):
                    act.dma_start(tile[:, 6 + c % 2, :],
                                  cs_d[bass.ds(g * GH + c * HEADS, GH), :].rearrange("r l -> (r l)").partition_broadcast(P)
                                  ).then_inc(S["csb_in"], 16)

                for q in range(6):
                    dst = tile[:, (4, 5, 0, 1, 2, 3)[q], :]
                    act.wait_ge(S["block_done"], g * 10 + (N_SSM + q + 1))
                    if q == 0:
                        act.wait_ge(S["z_used"], g * 10 + 1)
                    if q == 2:
                        act.wait_ge(S["y_split"], g * 4 + 1)
                    act.activation(dst, acc[(q + 1) % 2][:], ACT.Identity, bias=gpar[:, 5 * q + 4:5 * q + 5],
                                   scale=gpar[:, 5 * q + 3:5 * q + 4]).then_inc(S["conv_first"], 1)
                    act.wait_ge(S["conv_done"], g * 6 + q + 1)
                    act.activation(dst, dst, ACT.Silu).then_inc(S["conv_silu"], 1)

                def prepare(c):
                    csb = tile[:, 6 + c % 2, :]
                    act.wait_ge(S["csb_in"], g * 128 + 16 * c + 16)
                    act.activation(tile[:, 8 + c % 2, :], csb, ACT.Exp).then_inc(S["e_ready"], 1)
                    act.wait_ge(S["g_ready"], g * NT + c + 1)
                    if c:
                        act.wait_ge(S["s_ready"], g * NT + c)
                    act.activation(tile[:, 11, HALF:HALF + P], bank[1][:, 0:P], ACT.Copy).then_inc(S["btok_ready"], 1)
                    act.wait_ge(S["diff_ready"], g * NT + c + 1)
                    act.activation(csb, csb, ACT.Relu, scale=-1.0).then_inc(S["relu_ready"], 1)
                    if c + 1 < NT:
                        if c:
                            act.wait_ge(S["y_ready"], g * NT + c)
                        load_sums(c + 1)
                    act.wait_ge(S["relu_ready"], g * NT + c + 1)
                    act.activation(csb, csb, ACT.Exp, scale=-1.0).then_inc(S["l_ready"], 1)

                load_sums(0)
                for c in range(NT):
                    prepare(c)
                act.wait_ge(S["y_ready"], g * NT + NT - 1)
                for j in range(5):
                    if j < 4:
                        if j == 2:
                            act.wait_ge(S["y_ready"], g * NT + NT)
                        act.wait_ge(S["block_done"], g * 10 + (N_SSM + 6 + j + 1))
                        act.activation(tile[:, (8, 6, 9, 7)[j], :], acc[(j + 1) % 2][:], ACT.Silu).then_inc(S["z_silu"], 1)
                        act.wait_ge(S["z_silu"], g * 4 + j + 1)
                        act.sem_inc(acc_free[(j + 1) % 2], 1)
                    if j:
                        act.wait_ge(S["z_used"], g * 10 + j + 1)
                        if j > 2:
                            act.wait_ge(S["ssm_sq"], g * 4 + j - 1)
                        act.activation(tile[:, 10 if j == 1 else 11, :], tile[:, j - 1, :], ACT.Square).then_inc(S["y_gated"], 1)
                act.wait_ge(S["ssm_root"], g * 2 + 1)
                root(HALF, S["ssm_root"])
                for j in range(4):
                    act.wait_ge(S["ssm_scaled"], g * 4 + j + 1)
                    act.activation(u_hi[:, bass.ds(g * 4 + j, 1), :].rearrange("p a t -> p (a t)"), tile[:, j, :], ACT.Copy
                                   ).then_inc(S["ssm_hi"], 1)

            act.wait_ge(S["merged_saved"], 16 * KT + 16)
            act.wait_ge(S["z_used"], 21)
            with act.Fori(0, KT // 2) as t:
                for s in range(2):
                    m = t * 2 + s
                    act.wait_ge(S["c_free"], m + 1)
                    act.dma_start(tile[:, 10 + s, :], merged_d[bass.ds(m, 1)].rearrange("a p t -> (a p) t")
                                  ).then_inc(merged_s[s], 16)
                    act.wait_ge(S["block_done"], m * 2 + (N_C + 1))
                    act.activation(tile[:, 8 + s, :], acc[1][:], ACT.Sigmoid).then_inc(S["c_gate"], 1)
                    act.wait_ge(S["c_gate"], m + 1)
                    act.sem_inc(acc_free[1], 1)
            for part in (range(KT - 1), range(KT - 1, KT)):
                for k in part:
                    act.wait_ge(S["merged_all"], k + 1)
                    act.activation(h_hi[:, k, :], tile[:, k, :], ACT.Copy).then_inc(S["merged_hi"], 1)
                for k in part:
                    act.wait_ge(S["merged_ready"], k + 1)
                    act.dma_start(tile[:, k, :], x_in[k]).then_inc(S["x2_in"], 16)
            for k in range(KT):
                act.wait_ge(S["x1_ready"], k + 1)
                if k >= 2:
                    act.wait_ge(S["x1_sum"], k - 1)
                act.activation(tile[:, 10 + 2 * (k % 2), :], xres[k], ACT.Square).then_inc(S["x1_sq"], 1)
            act.wait_ge(S["n2_root"], 1)
            root(D, S["n2_root"])
            for k in range(KT):
                act.wait_ge(S["n2_scaled"], k + 1)
                act.activation(h_hi[:, k, :], tile[:, 8 + k % 2, :], ACT.Identity, bias=mod[:, 24 + k:25 + k]
                               ).then_inc(S["n2_hi"], 1)
                if k % 2:
                    if k >= 4:
                        act.wait_ge(S["n2_odd_ready"], k // 2 - 1)
                    act.activation(tile[:, 10, :] if k % 4 == 1 else tile[:, 12, :], tile[:, 9, :], ACT.Identity,
                                   bias=mod[:, 24 + k:25 + k]).then_inc(S["n2_full"], 1)
            with act.Fori(0, QUARTERS) as q4:
                with act.Fori(0, KT // 2) as t:
                    for s in range(2):
                        b = (N_MLP + s) % 2
                        m = q4 * 8 + t * 2 + s
                        act.wait_ge(S["block_done"], q4 * 16 + t * 2 + (N_MLP + s + 1))
                        act.wait_ge(S["relu_free"], m + 1)
                        act.activation(tile[:, 8 + s, :], acc[b][:], ACT.Relu).then_inc(S["hid_relu"], 1)
                        act.wait_ge(S["hid_relu"], m + 1)
                        act.sem_inc(acc_free[b], 1)
                        act.wait_ge(S["hid_sq"], m + 1)
                        act.activation(u_hi[:, bass.ds(t * 2 + s, 1), :].rearrange("p a t -> p (a t)"), tile[:, 10 + s, :], ACT.Copy
                                       ).then_inc(S["hid_hi"], 1)
            for k in range(KT):
                act.wait_ge(S["x2_ready"], (QUARTERS - 1) * KT + k + 1)
                if k >= 2:
                    act.wait_ge(S["f_sum"], k - 1)
                act.activation(tile[:, 10 + 2 * (k % 2), :], xres[k], ACT.Square).then_inc(S["f_sq"], 1)
            act.wait_ge(S["f_root"], 1)
            root(D, S["f_root"])
            for k in range(KT):
                act.wait_ge(S["f_ready"], k + 1)
                act.dma_start(out[k], xres[k]).then_inc(S["out_saved"], 16)
            act.wait_ge(S["out_saved"], 16 * KT)

        @block.vector
        def _(dve):
            own = Steps(dve, S["dve_own"])
            dve.sem_inc(S["gates_free"], 1)
            dve.sem_inc(S["c_free"], 2)
            dve.sem_inc(S["relu_free"], 2)

            def squares_sum(first_wait, used, base=0):
                for k in range(KT):
                    dve.wait_ge(first_wait, base + k + 1)
                    src = tile[:, 10 + 2 * (k % 2), :]
                    if k == 0:
                        dve.tensor_copy(tile[:, 11, :], src).then_inc(used, 1)
                    else:
                        dve.wait_ge(used, base + k)
                        dve.tensor_tensor(tile[:, 11, :], tile[:, 11, :], src, ALU.add).then_inc(used, 1)

            def factor(ms, root, inverse, n):
                dve.wait_ge(ms, n + 1)
                dve.tensor_copy(rms[:, 0, :], bank[3][:, 0:NT]).then_inc(root, 1)
                dve.wait_ge(root, n * 2 + 2)
                dve.reciprocal(rstd[:], rms[:, 1, :]).then_inc(inverse, 1)

            def weigh_rows(src):
                rows = src.rearrange("p (k c) -> p k c", k=KT)
                own.mark(dve.tensor_tensor(rows, rows, c_sb[:].unsqueeze(2).to_broadcast([P, KT, P]), ALU.mult))
                own.settle()

            def sum_rows(src, dst, signal):
                dve.tensor_reduce(dst, src.rearrange("p (k c) -> p c k", k=KT), mybir.AxisListType.X, ALU.add
                                  ).then_inc(signal, 1)

            dve.memset(ones[:], 1.0).then_inc(acc_free[0], 1)
            dve.memset(eps[:], EPS).then_inc(acc_free[1], 1)
            own.mark(dve.memset(sm[:], 0.0))
            dve.wait_ge(S["par_in"], 16)
            dve.wait_ge(S["lam_in"], 16)
            for q in range(2):
                v = tile[:, 11, 2 * q * HD:2 * (q + 1) * HD]
                dve.tensor_tensor_reduce(tile[:, 11, (4 + q) * HD:(5 + q) * HD], v[:, 0:HD], v[:, HD:2 * HD], 1.0, 0.0, ALU.mult, ALU.add,
                                         lam[:, q:q + 1]).then_inc(S["lam_dots"], 1)
            own.mark(dve.tensor_scalar(a_da[:], par[:, C_SUBLN:C_SUBLN + 1], DA_OUT, None, ALU.mult))
            dve.wait_ge(S["lam_dots"], 2)
            squares_sum(S["sq_ready"], S["sq_used"])
            dve.wait_ge(S["lam_exps"], 1)
            own.mark(dve.tensor_tensor(lam[:, 4:5], lam[:, 3:4], lam[:, 2:3], ALU.subtract))
            own.settle()
            own.mark(dve.tensor_scalar(lam[:, 5:6], lam[:, 4:5], -LAM_INIT, None, ALU.add))
            factor(S["ms_ready"], S["root_ready"], S["rstd_ready"], 0)
            pair_of = lambda ap, k: ap.rearrange("p (a b) -> p a b", a=2)[:, :, k]

            def h_low(k):
                dve.wait_ge(S["h_hi_ready"], k + 1)
                dve.scalar_tensor_tensor(out=h_lo[:, k, :], in0=xres[k], scalar=mod[:, k:k + 1],
                                         in1=h_hi[:, k, :].bitcast(F32), op0=ALU.add, op1=ALU.subtract
                                         ).then_inc(S["h_ready"], 1)

            def scale_rows(k):
                dve.wait_ge(S["mix_weighed"], k + 1)
                if k >= 2:
                    dve.wait_ge(S["mix_mod_done"], k - 1)
                sum_rows(tile[:, (9, 12)[k % 2], :], tile[:, 11, (k % 2) * P:(k % 2 + 1) * P], S["mix_reduced"])

            scale_rows(0)
            dve.wait_ge(S["bcast_ready"], 1)
            for k in range(KT):
                dve.wait_ge(S["mix_mod_done"], k + 1)
                own.mark(dve.tensor_tensor(pair_of(mod[:, 0:16], k), mix_banks[k % 4][:, 0:2],
                                           pair_of(par[:, C_ADAB:C_ADAB + 16], k), ALU.add))
                own.settle()
                own.mark(dve.scalar_tensor_tensor(out=a_mix[:, k:k + 1], in0=mod[:, 8 + k:9 + k], scalar=1.0,
                                                  in1=par[:, C_GMIX + k:C_GMIX + k + 1], op0=ALU.add, op1=ALU.mult))
                own.settle()
                dve.scalar_tensor_tensor(out=xres[k], in0=xres[k], scalar=a_mix[:, k:k + 1], in1=wk[0][:],
                                         op0=ALU.mult, op1=ALU.mult).then_inc(S["h_scaled"], 1)
                if k + 1 < KT:
                    scale_rows(k + 1)
                h_low(k)

            def da_head(head):
                def bias(i, m):
                    col = 2 * (i % 2) + m
                    w = (i + 1) * P
                    if i >= 2 and m == 0:
                        dve.wait_ge(S["turned"], head * NP_ + PIECES.index((i - 2, (i - 2) // 4)) + 1)
                    dve.wait_ge(S["scored"], head * 16 + 2 * i + m + 1)
                    dve.nop(nofuse=True)
                    dve.tensor_tensor_reduce(tile[:, (5, 6, 7, 8)[col], 0:w], wk[0][:, 0:w], tile[:, 4, T - w:T], SCALE, NEG,
                                             ALU.add, ALU.max, mxp[:, col:col + 1]).then_inc(S["biased"], 1)
                    dve.wait_ge(S["biased"], head * 16 + 2 * i + m + 1)
                    dve.tensor_scalar(mx[:, col:col + 1], mxp[:, col:col + 1], -1.0, None, ALU.mult).then_inc(S["negmax"], 1)

                def weigh(i):
                    col = 2 * (i % 2)
                    w = (i + 1) * P
                    p0, p1 = (tile[:, (5, 6, 7, 8)[col + m], 0:w] for m in range(2))
                    dve.wait_ge(S["exped"], head * 16 + 2 * i + 2)
                    own.mark(dve.reciprocal(rc[:, col:col + 2], sm[:, col:col + 2]))
                    own.settle()
                    own.mark(dve.tensor_scalar(p1, p1, rc[:, col + 1:col + 2], lam[:, 5:6], ALU.mult, ALU.mult))
                    own.settle()
                    dve.scalar_tensor_tensor(out=p0, in0=p0, scalar=rc[:, col:col + 1], in1=p1,
                                             op0=ALU.mult, op1=ALU.add).then_inc(S["weighted"], 1)

                dve.wait_ge(S["da_tab_in"], head * 16 + 16)
                for i in range(NT):
                    bias(i, 0)
                    if i:
                        weigh(i - 1)
                    bias(i, 1)
                weigh(NT - 1)
                dve.wait_ge(S["weighted"], head * 8 + 8)
                dve.wait_ge(S["turned"], head * NP_ + NP_)

            with dve.Fori(0, DA_HEADS) as head, own.loop(head, 16, DA_HEADS):
                da_head(head)

            own.mark(dve.tensor_scalar(negsink[:], par[:, C_SINK:C_SINK + 8], -1.0, None, ALU.mult))
            own.settle()
            dve.sem_inc(S["sw_biased"], 1)
            dve.sem_inc(S["sw_split"], 1)
            dve.sem_inc(S["da_hi"], 1)

            def sw_pair(s, j):
                def soften(i):
                    dve.wait_ge(S["sw_scored"], j * NT + i + 1)
                    if i >= 4:
                        dve.wait_ge(S["sw_turned"], j * NT + i - 3)
                    dve.nop(nofuse=True)
                    w = 256 if i else P
                    for g in range(2):
                        col = 2 * (i % 4) + g
                        hi = (i % 2) * HALF + (g + 1) * 256
                        last = dve.tensor_tensor_reduce(
                            tile[:, 5 + (i % 4) // 2, hi - w:hi], bank[g][:, 256 - w:256],
                            tile[:, 4, s * HALF + (g + 1) * 256 - w:s * HALF + (g + 1) * 256], SCALE, NEG, ALU.add, ALU.max,
                            swm[:, col:col + 1])
                    last.then_inc(S["sw_biased"], 1)
                    cols = slice(2 * (i % 4), 2 * (i % 4) + 2)
                    dve.wait_ge(S["sw_biased"], j * NT + i + 2)
                    own.mark(dve.scalar_tensor_tensor(out=swn[:, cols], in0=swm[:, cols], scalar=-1.0,
                                                      in1=negsink[:, bass.ds(j * 2, 2)], op0=ALU.mult, op1=ALU.min))
                    own.settle()
                    dve.tensor_tensor(swd[:, cols], swn[:, cols], negsink[:, bass.ds(j * 2, 2)], ALU.subtract
                                      ).then_inc(S["sw_negmax"], 1)

                def weigh(i):
                    cols = slice(2 * (i % 4), 2 * (i % 4) + 2)
                    dve.wait_ge(S["sw_exped"], j * NT + i + 1)
                    own.mark(dve.tensor_tensor(swr[:, cols], sws[:, cols], swe[:, cols], ALU.add))
                    own.settle()
                    own.mark(dve.reciprocal(swr[:, cols], swr[:, cols]))
                    own.settle()
                    for g in range(2):
                        lo = (i % 2) * HALF + g * 256 + (0 if i else P)
                        p = tile[:, 5 + (i % 4) // 2, lo:(i % 2) * HALF + (g + 1) * 256]
                        last = dve.tensor_scalar(p, p, swr[:, 2 * (i % 4) + g:2 * (i % 4) + g + 1], None, ALU.mult)
                    last.then_inc(S["sw_weighted"], 1)

                def out_lo(half):
                    dve.wait_ge(S["sw_hi"], j * 2 + half + 1)
                    at = (slice(None), bass.ds(j + 4, 1), slice(half * HALF, (half + 1) * HALF))
                    dve.tensor_tensor(u_lo[at].rearrange("p a t -> p (a t)"), bank[3],
                                      u_hi[at].rearrange("p a t -> p (a t)").bitcast(F32), ALU.subtract
                                      ).then_inc(S["sw_split"], 1)

                dve.wait_ge(S["sw_tab_in"], j * 16 + 16)
                for i in range(NT):
                    soften(i)
                    if i:
                        weigh(i - 1)
                    if i == 1:
                        clip_tight(j)
                    if i == 2:
                        clip_wide(j)
                    if i == 5:
                        out_lo(0)
                        factor_da(j)
                    if i == 7:
                        dve.wait_ge(S["da_root"], j * 2 + 2)
                        own.mark(dve.reciprocal(rms[:, 2, :], rms[:, 1, :]))
                        own.settle()
                        dve.tensor_tensor(rstd[:], rms[:, 2, :], rms[:, 4, :], ALU.mult).then_inc(S["da_rstd"], 1)
                weigh(NT - 1)
                dve.wait_ge(S["da_bcast"], j + 1)
                dve.scalar_tensor_tensor(out=tile[:, 12, :], in0=tile[:, 10, :], scalar=a_da[:, 0:1], in1=acc[s][:],
                                         op0=ALU.mult, op1=ALU.mult).then_inc(S["da_scaled"], 1)
                out_lo(1)
                dve.wait_ge(S["da_hi"], j + 2)
                dst = bass.ds(j, 1)
                dve.tensor_tensor(u_lo[:, dst, :].rearrange("p a t -> p (a t)"), tile[:, 12, :],
                                  u_hi[:, dst, :].rearrange("p a t -> p (a t)").bitcast(F32), ALU.subtract
                                  ).then_inc(S["u_ready"], 1)
                dve.wait_ge(S["u_ready"], j + 1)

            def clip_tight(j):
                dve.wait_ge(S["o_back"], j * 16 + 16)
                dve.tensor_scalar(tile[:, 8, :], tile[:, 10, :], 2.0 ** 60, -2.0 ** 60, ALU.min, ALU.max
                                  ).then_inc(S["da_clipped"], 1)

            def clip_wide(j):
                dve.tensor_scalar(tile[:, 10, :], tile[:, 10, :], 2.0 ** 70, -2.0 ** 70, ALU.min, ALU.max
                                  ).then_inc(S["da_clipped"], 1)

            def factor_da(j):
                dve.wait_ge(S["da_ms"], j * 2 + 2)
                s1, s2 = rms[:, 0, :], rms[:, 1, :]
                big, low, fac = rms[:, 2, :], rms[:, 3, :], rms[:, 4, :]
                own.mark(dve.tensor_copy(rms[:, 0:2, :], acc_means(j)))
                own.settle()
                own.mark(dve.tensor_scalar(big, s2, 2.0 ** 52, None, ALU.is_gt))
                own.mark(dve.tensor_scalar(rms[:, 5, :], s2, 2.0 ** 68, None, ALU.is_lt))
                own.settle()
                own.mark(dve.tensor_scalar(low, big, -1.0, 1.0, ALU.mult, ALU.add))
                own.mark(dve.tensor_tensor(s2, s2, big, ALU.mult))
                own.settle()
                own.mark(dve.scalar_tensor_tensor(out=fac, in0=big, scalar=2.0 ** -30, in1=low, op0=ALU.mult, op1=ALU.add))
                own.settle()
                own.mark(dve.tensor_tensor(low, s1, low, ALU.mult))
                own.mark(dve.tensor_tensor(fac, fac, rms[:, 5, :], ALU.mult))
                own.settle()
                dve.tensor_tensor(rms[:, 0, :], low, s2, ALU.add).then_inc(S["da_root"], 1)

            which = [None]

            def acc_means(j):
                return acc[which[0]][:, 0:2 * NT].rearrange("p (a b) -> p a b", a=2)

            with dve.Fori(0, SW_PAIRS // 2) as t, own.loop(t, 2 * (3 * NT + 9), SW_PAIRS // 2):
                for s in range(2):
                    which[0] = s
                    sw_pair(s, t * 2 + s)

            dve.sem_inc(S["ada_used"], 4)
            heads = lambda ap: ap.rearrange("p (c h) -> p c h", h=HEADS)
            dve.wait_ge(S["dt_turned"], 1)
            own.mark(dve.tensor_tensor(heads(dtm[:, 3, :]), heads(bank[0][:, 0:P]),
                                       par[:, C_DTB:C_DTB + HEADS].unsqueeze(1).to_broadcast([P, NT, HEADS]), ALU.add))
            own.settle()
            dve.scalar_tensor_tensor(out=dtm[:, 1, :], in0=dtm[:, 3, :], scalar=-1.0, in1=dtm[:, 3, :], op0=ALU.mult,
                                     op1=ALU.max).then_inc(S["dt_abs"], 1)
            dve.wait_ge(S["dt_exp"], 1)
            e_, s_, s2, q_ = (dtm[:, n, :] for n in (2, 4, 6, 7))
            own.mark(dve.tensor_scalar(q_, e_, 2.0, None, ALU.add))
            own.settle()
            own.mark(dve.reciprocal(s2, q_))
            own.settle()
            own.mark(dve.tensor_tensor(s_, e_, s2, ALU.mult))
            own.settle()
            own.mark(dve.tensor_tensor(s2, s_, s_, ALU.mult))
            own.settle()
            own.mark(dve.tensor_scalar(q_, s2, 1.0 / 15, None, ALU.mult))
            for odd in (13, 11, 9, 7, 5, 3):
                own.settle()
                own.mark(dve.scalar_tensor_tensor(out=q_, in0=q_, scalar=1.0 / odd, in1=s2, op0=ALU.add, op1=ALU.mult))
            own.settle()
            own.mark(dve.scalar_tensor_tensor(out=q_, in0=q_, scalar=1.0, in1=s_, op0=ALU.add, op1=ALU.mult))
            own.mark(dve.tensor_scalar(dtm[:, 3, :], dtm[:, 3, :], 0.0, None, ALU.max))
            own.settle()
            dt_ = dtm[:, 4, :]
            own.mark(dve.scalar_tensor_tensor(out=dt_, in0=q_, scalar=2.0, in1=dtm[:, 3, :], op0=ALU.mult, op1=ALU.add))
            own.settle()
            dve.scalar_tensor_tensor(out=heads(dtm[:, 0, :]), in0=heads(dt_), scalar=-1.0,
                                     in1=exp_a[:].unsqueeze(1).to_broadcast([P, NT, HEADS]),
                                     op0=ALU.mult, op1=ALU.mult).then_inc(S["dt_da"], 1)
            dve.sem_inc(S["ab_free"], 1)
            dve.wait_ge(S["c_in"], 16)
            with dve.Fori(0, KT // 2) as t, own.loop(t, 12, KT // 2):
                for s in range(2):
                    m = t * 2 + s
                    b = (N_AB + 3 * s + 2) % 2
                    for q in range(4):
                        at = 4 * s + q
                        dve.wait_ge(ada_s[q], t * 32 + (5 + s) * 16)
                        dve.wait_ge(S["mod_done"], t * 8 + (at + 1))
                        weigh_rows(tile[:, 8 + q, :])
                        sum_rows(tile[:, 8 + q, :], tile[:, 7, at * P:(at + 1) * P], S["ada_used"])
                    dve.wait_ge(S["gate_ready"], m * 2 + 2)
                    dve.wait_ge(S["block_done"], m * 3 + (N_AB + 3))
                    own.mark(dve.tensor_tensor(tile[:, 2, :], tile[:, 0, :], wk[0][:], ALU.mult))
                    own.mark(dve.tensor_tensor(tile[:, 3, :], tile[:, 1, :], acc[b][:], ALU.mult))
                    own.settle()
                    dve.sem_inc(acc_free[b], 1)
                    dve.sem_inc(S["ab_free"], 1)
                    dve.sem_inc(S["gates_free"], 1)
                    dve.wait_ge(S["merged_saved"], t * 32 + 16)
                    dve.tensor_tensor(tile[:, 4 + s, :], tile[:, 2, :], tile[:, 3, :], ALU.add).then_inc(S["merged_out"], 1)
                    dve.wait_ge(S["merged_out"], m + 1)
            dve.wait_ge(S["mod_done"], 8 + 32)
            dve.tensor_tensor(mod[:, 16:48], bank[2][:, 16:48], par[:, C_ADAB + 16:C_ADAB + 48], ALU.add
                              ).then_inc(S["mod_rest"], 1)
            dve.wait_ge(S["mod_rest"], 1)
            own.mark(dve.scalar_tensor_tensor(out=a_mlp[:], in0=mod[:, 32:40], scalar=1.0,
                                              in1=par[:, C_GMLP:C_GMLP + 8], op0=ALU.add, op1=ALU.mult))

            dve.wait_ge(S["cs_copied"], 1)
            own.mark(dve.tensor_copy(dtm[:, 7, :], bank[1][:, P:2 * P]))
            own.settle()
            dve.tensor_tensor(dtm[:, 6, :], bank[1][:, 2 * P:3 * P], dtm[:, 7, :], ALU.subtract).then_inc(S["dt_diff"], 1)
            dve.wait_ge(S["dt_decays"], 1)
            own.mark(dve.tensor_tensor(dtm[:, 6, :], dtm[:, 6, :], dt_, ALU.mult))
            own.settle()
            dve.sem_inc(S["cs_copied"], 1)

            with dve.Fori(0, GROUPS) as g, own.loop(g, 14 + NT + 4, GROUPS):
                own.mark(dve.tensor_copy(gpar[:, 0:30], par[:, bass.ds(g * 30 + C_CONV, 30)]))
                own.mark(dve.tensor_copy(gpar[:, 30:34], par[:, bass.ds(g * 4 + C_D, 4)]))
                own.settle()
                dve.sem_inc(S["z_used"], 1)
                for q in range(6):
                    dst = tile[:, (4, 5, 0, 1, 2, 3)[q], :]
                    src = acc[(q + 1) % 2]
                    dve.wait_ge(S["conv_first"], g * 6 + q + 1)
                    for tap in (2, 1, 0):
                        lag = 3 - tap
                        ins = dve.scalar_tensor_tensor(out=dst[:, lag:T], in0=src[:, 0:T - lag],
                                                       scalar=gpar[:, 5 * q + tap:5 * q + tap + 1], in1=dst[:, lag:T],
                                                       op0=ALU.mult, op1=ALU.add)
                        if tap:
                            own.mark(ins)
                            own.settle()
                        else:
                            ins.then_inc(S["conv_done"], 1)
                    dve.wait_ge(S["conv_done"], g * 6 + q + 1)
                    dve.sem_inc(acc_free[(q + 1) % 2], 1)
                dve.memset(tile[:, 11, 0:HALF], 0.0).then_inc(S["state_ready"], 1)
                byhead = lambda ap: ap.rearrange("p (h x) -> p h x", h=GH)

                def prepare(c):
                    now = bass.ds(g * GH + c * HEADS, GH)
                    csb = tile[:, 6 + c % 2, :]
                    dve.wait_ge(S["x_turned"], g * NT + c + 1)
                    if c:
                        dve.wait_ge(S["s_ready"], g * NT + c)
                    if c >= 2:
                        dve.wait_ge(S["y_ready"], g * NT + c - 1)
                    for dst, fac in ((tile[:, 10, (c % 2) * HALF:(c % 2 + 1) * HALF], 4), (tile[:, 12, 0:HALF], 6)):
                        dve.tensor_tensor(byhead(dst), byhead(bank[0]),
                                          dtm[:, fac, now].unsqueeze(2).to_broadcast([P, GH, HD]), ALU.mult
                                          ).then_inc(S["xd_ready"], 1)
                    dve.wait_ge(S["btok_ready"], g * NT + c + 1)
                    if c:
                        dve.wait_ge(S["m_ready"], g * NT + c)
                    dve.tensor_tensor(tile[:, 11, HALF + P:HALF + 2 * P], bank[1][:, P:2 * P], tri, ALU.mult
                                      ).then_inc(S["g_masked"], 1)
                    dve.wait_ge(S["e_ready"], g * NT + c + 1)
                    dve.tensor_tensor(byhead(csb), byhead(csb), dtm[:, 7, now].unsqueeze(2).to_broadcast([P, GH, P]),
                                      ALU.subtract).then_inc(S["diff_ready"], 1)

                def finish(c):
                    csb = tile[:, 6 + c % 2, :]
                    dve.wait_ge(S["l_ready"], g * NT + c + 1)
                    dve.wait_ge(S["g_masked"], g * NT + c + 1)
                    dve.tensor_tensor(byhead(csb), byhead(csb),
                                      tile[:, 11, HALF + P:HALF + 2 * P].unsqueeze(1).to_broadcast([P, GH, P]), ALU.mult
                                      ).then_inc(S["m_ready"], 1)

                prepare(0)
                finish(0)
                for c in range(NT):
                    cols = slice(c * P, (c + 1) * P)
                    now = bass.ds(g * GH + c * HEADS, GH)
                    if c + 1 < NT:
                        prepare(c + 1)
                    dve.wait_ge(S["y_ready"], g * NT + c + 1)
                    own.mark(dve.tensor_tensor(byhead(tile[:, 11, 0:HALF]), byhead(tile[:, 11, 0:HALF]),
                                               dtm[:, 5, now].unsqueeze(2).to_broadcast([P, GH, HD]), ALU.mult))
                    own.settle()
                    dve.tensor_tensor(tile[:, 11, 0:HALF], tile[:, 11, 0:HALF], bank[2][:, :], ALU.add
                                      ).then_inc(S["state_ready"], 1)
                    dve.wait_ge(S["state_ready"], g * (NT + 1) + c + 2)
                    for j in range(4):
                        dve.scalar_tensor_tensor(out=tile[:, j, cols], in0=tile[:, j, cols], scalar=gpar[:, 30 + j:31 + j],
                                                 in1=bank[3][:, j * P:(j + 1) * P], op0=ALU.mult, op1=ALU.add
                                                 ).then_inc(S["y_taken"], 1)
                    if c + 1 < NT:
                        finish(c + 1)
                dve.wait_ge(S["y_taken"], g * 32 + 32)
                for j in range(4):
                    dve.wait_ge(S["z_silu"], g * 4 + j + 1)
                    own.mark(dve.tensor_tensor(tile[:, j, :], tile[:, j, :], tile[:, (8, 6, 9, 7)[j], :], ALU.mult))
                    own.settle()
                    dve.sem_inc(S["z_used"], 1)
                    dve.wait_ge(S["y_gated"], g * 4 + j + 1)
                    if j == 0:
                        dve.sem_inc(S["ssm_sq"], 1)
                    else:
                        dve.tensor_tensor(tile[:, 10, :], tile[:, 10, :], tile[:, 11, :], ALU.add).then_inc(S["ssm_sq"], 1)
                        dve.wait_ge(S["ssm_sq"], g * 4 + j + 1)
                factor(S["ssm_ms"], S["ssm_root"], S["ssm_rstd"], g)
                dve.wait_ge(S["ssm_bcast"], g + 1)
                for j in range(4):
                    dve.scalar_tensor_tensor(out=tile[:, j, :], in0=tile[:, j, :],
                                             scalar=par[:, bass.ds(g * 4 + (C_GSSM + j), 1)], in1=wk[0][:],
                                             op0=ALU.mult, op1=ALU.mult).then_inc(S["ssm_scaled"], 1)
                dve.wait_ge(S["ssm_scaled"], g * 4 + 4)
                for _n in range(5):
                    dve.sem_inc(S["z_used"], 1)

            dve.sem_inc(S["z_used"], 1)
            def merge_c(m, t, s):
                dve.wait_ge(S["c_gate"], m + 1)
                dve.wait_ge(S["block_done"], m * 2 + (N_C + 2))
                own.mark(dve.tensor_tensor(tile[:, 8 + s, :], tile[:, 8 + s, :], acc[0][:], ALU.mult))
                own.settle()
                dve.sem_inc(acc_free[0], 1)
                dve.wait_ge(merged_s[s], t * 16 + 16)
                dst = tile[:, bass.ds(m, 1), :].rearrange("p a t -> p (a t)")
                dve.tensor_tensor(dst, tile[:, 8 + s, :], tile[:, 10 + s, :], ALU.add).then_inc(S["merged_all"], 1)
                dve.wait_ge(S["merged_all"], m + 1)
                dve.sem_inc(S["c_free"], 1)

            def merged_low(k):
                dve.wait_ge(S["merged_hi"], k + 1)
                dve.tensor_tensor(h_lo[:, k, :], tile[:, k, :], h_hi[:, k, :].bitcast(F32), ALU.subtract
                                  ).then_inc(S["merged_ready"], 1)

            with dve.Fori(0, KT // 2 - 1) as t, own.loop(t, 2, KT // 2 - 1):
                for s in range(2):
                    merge_c(t * 2 + s, t, s)
            merge_c(KT - 2, KT // 2 - 1, 0)
            for k in range(KT - 1):
                merged_low(k)
            merge_c(KT - 1, KT // 2 - 1, 1)
            merged_low(KT - 1)

            for k in range(KT):
                b = (N_OUT + k) % 2
                dve.wait_ge(S["block_done"], N_OUT + k + 1)
                dve.wait_ge(S["x2_in"], 16 * KT)
                dve.scalar_tensor_tensor(out=xres[k], in0=acc[b][:], scalar=mod[:, 16 + k:17 + k], in1=xres[k],
                                         op0=ALU.mult, op1=ALU.add).then_inc(S["x1_ready"], 1)
                dve.wait_ge(S["x1_ready"], k + 1)
                dve.sem_inc(acc_free[b], 1)
                dve.wait_ge(S["x1_sq"], k + 1)
                src = tile[:, 10 + 2 * (k % 2), :]
                if k == 0:
                    dve.tensor_copy(tile[:, 11, :], src).then_inc(S["x1_sum"], 1)
                else:
                    dve.wait_ge(S["x1_sum"], k)
                    dve.tensor_tensor(tile[:, 11, :], tile[:, 11, :], src, ALU.add).then_inc(S["x1_sum"], 1)
            factor(S["n2_ms"], S["n2_root"], S["n2_rstd"], 0)
            dve.wait_ge(S["n2_bcast"], 1)
            for k in range(KT):
                if k >= 2:
                    dve.wait_ge(S["n2_full"] if k % 2 else S["n2_ready"], k // 2)
                dve.scalar_tensor_tensor(out=tile[:, 8 + k % 2, :], in0=xres[k], scalar=a_mlp[:, k:k + 1], in1=wk[0][:],
                                         op0=ALU.mult, op1=ALU.mult).then_inc(S["n2_scaled"], 1)
                if k % 2:
                    dve.wait_ge(S["n2_hi"], k)
                    dve.scalar_tensor_tensor(out=h_lo[:, k - 1, :], in0=tile[:, 8, :], scalar=mod[:, 23 + k:24 + k],
                                             in1=h_hi[:, k - 1, :].bitcast(F32), op0=ALU.add, op1=ALU.subtract
                                             ).then_inc(S["n2_ready"], 1)
            dve.wait_ge(S["n2_ready"], KT // 2)
            dve.wait_ge(S["n2_odd_ready"], KT // 2)

            def hidden(q4):
                with dve.Fori(0, KT // 2) as t:
                    for s in range(2):
                        m = q4 * 8 + t * 2 + s
                        dve.wait_ge(S["hid_relu"], m + 1)
                        dve.tensor_tensor(tile[:, 10 + s, :], tile[:, 8 + s, :], tile[:, 8 + s, :], ALU.mult
                                          ).then_inc(S["hid_sq"], 1)
                        dve.wait_ge(S["hid_hi"], m + 1)
                        dve.sem_inc(S["relu_free"], 1)
                        dst = bass.ds(t * 2 + s, 1)
                        dve.tensor_tensor(u_lo[:, dst, :].rearrange("p a t -> p (a t)"), tile[:, 10 + s, :],
                                          u_hi[:, dst, :].rearrange("p a t -> p (a t)").bitcast(F32), ALU.subtract
                                          ).then_inc(S["hid_ready"], 1)
                        dve.wait_ge(S["hid_ready"], m + 1)

            with dve.Fori(0, QUARTERS - 1) as q4:
                hidden(q4)
                with dve.Fori(0, KT // 2) as t:
                    for s in range(2):
                        b = (N_MLP + 8 + s) % 2
                        m = q4 * 8 + t * 2 + s
                        dve.wait_ge(S["block_done"], q4 * 16 + t * 2 + (N_MLP + 8 + s + 1))
                        xk = tile[:, bass.ds(t * 2 + s, 1), :].rearrange("p a t -> p (a t)")
                        dve.scalar_tensor_tensor(out=xk, in0=acc[b][:], scalar=mod[:, bass.ds(t * 2 + (40 + s), 1)], in1=xk,
                                                 op0=ALU.mult, op1=ALU.add).then_inc(S["x2_ready"], 1)
                        dve.wait_ge(S["x2_ready"], m + 1)
                        dve.sem_inc(acc_free[b], 1)

            hidden(QUARTERS - 1)
            for k in range(KT):
                n = N_MLP + 16 * (QUARTERS - 1) + 8 + k
                dve.wait_ge(S["block_done"], n + 1)
                dve.scalar_tensor_tensor(out=xres[k], in0=acc[n % 2][:], scalar=mod[:, 40 + k:41 + k], in1=xres[k],
                                         op0=ALU.mult, op1=ALU.add).then_inc(S["x2_ready"], 1)
                dve.wait_ge(S["x2_ready"], (QUARTERS - 1) * KT + k + 1)
                dve.sem_inc(acc_free[n % 2], 1)
                dve.wait_ge(S["f_sq"], k + 1)
                src = tile[:, 10 + 2 * (k % 2), :]
                if k == 0:
                    dve.tensor_copy(tile[:, 11, :], src).then_inc(S["f_sum"], 1)
                else:
                    dve.wait_ge(S["f_sum"], k)
                    dve.tensor_tensor(tile[:, 11, :], tile[:, 11, :], src, ALU.add).then_inc(S["f_sum"], 1)
            factor(S["f_ms"], S["f_root"], S["f_rstd"], 0)
            dve.wait_ge(S["f_bcast"], 1)
            for k in range(KT):
                dve.scalar_tensor_tensor(out=xres[k], in0=xres[k], scalar=par[:, C_GFIN + k:C_GFIN + k + 1], in1=wk[0][:],
                                         op0=ALU.mult, op1=ALU.mult).then_inc(S["f_ready"], 1)


def blocks(w):
    k, m = w.shape
    return w.reshape(k // P, P, m // P, P).transpose(2, 1, 0, 3).reshape(m // P, P, (k // P) * P)


def shape_constants():
    n = SW_PAIRS * 2 + DA_HEADS
    slopes = np.exp2(-8.0 * np.arange(1, n + 1) / n).astype(np.float32)
    con = np.zeros((P, K_ALL), np.float32)
    con[:, K_ID:K_ID + P] = np.eye(P, dtype=np.float32)
    con[:, K_TRI:K_TRI + P] = np.triu(np.ones((P, P), np.float32))
    p = np.arange(P)[:, None]
    x = np.arange(256)[None, :]
    ok = (x // 64 >= p // 64 + 1) & (x // 64 <= p // 64 + 2)
    dist = np.abs(P + p - x).astype(np.float32)
    sw = np.zeros((SW_PAIRS, P, 2 * 256), np.float32)
    for j in range(SW_PAIRS):
        for g in range(2):
            sw[j, :, g * 256:(g + 1) * 256] = np.where(ok, -slopes[4 * g + j] / np.float32(SCALE) * dist, np.float32(NEG))
    x = np.arange(T)[None, :] - (T - P)
    ok = x // 64 <= p // 64
    dist = np.abs(p - x).astype(np.float32)
    tab = np.stack([np.where(ok, -slopes[8 + h] / np.float32(SCALE) * dist, np.float32(NEG)) for h in range(DA_HEADS)])
    tab = np.concatenate([tab.astype(np.float32), np.concatenate([sw[0], sw[1]], 1)[None]])
    return con, tab, sw


def kernel(**inputs):
    import concourse.bacc as bacc
    from concourse.bass_utils import run_bass_kernel_spmd as run

    a = {k: np.asarray(v) for k, v in inputs.items()}
    cols = lambda v: v.reshape(-1, P).T
    w = a["w_in"][0]
    da_q, da_k, da_v = (w[:, 512 * i:512 * (i + 1)] for i in range(3))
    at = 1536
    sw_q, sw_k, sw_v = w[:, at:at + 512], w[:, at + 512:at + 640], w[:, at + 640:at + 768]
    at += 768
    z, xs = w[:, at:at + 1024], w[:, at + 1024:at + 2048]
    bs, cs = w[:, at + 2048:at + 2304], w[:, at + 2304:at + 2560]
    at += 2560
    dt_cols = w[:, at:at + P]
    gates = [w[:, at + 16 + D * i:at + 16 + D * (i + 1)] for i in range(3)]
    pair = lambda v, ax: np.concatenate([np.take(v, range(64 * h, 64 * h + 64), ax) for j in range(4) for h in (j, j + 4)], ax)
    sw_q = pair(sw_q, 1)
    wb = a["w_branch"][0]
    wab = np.concatenate([wb[0:512], pair(wb[512:1024], 0)], 0)
    stream = []
    dq, dk, dv = (blocks(v) for v in (da_q, da_k, da_v))
    for h in range(DA_HEADS):
        stream += [dv[h], dk[h], dq[h]]
    stream += [blocks(sw_v)[0], blocks(sw_k)[0], *blocks(sw_q)]
    ga, gb, gc = (blocks(v) for v in gates)
    bab, bc = blocks(wab), blocks(wb[1024:2048])
    stream += [blocks(dt_cols)[0]]
    for m in range(KT):
        stream += [ga[m], gb[m], bab[m]]
    bz, bx, bbs, bcs = (blocks(v) for v in (z, xs, bs, cs))
    for g in range(GROUPS):
        stream += [bbs[g], bcs[g], *bx[4 * g:4 * g + 4], *bz[4 * g:4 * g + 4]]
    for m in range(KT):
        stream += [gc[m], bc[m]]
    stream += [*blocks(a["w_out"][0])]
    w1, w2 = blocks(a["w_mlp1"][0]), a["w_mlp2"][0]
    for q in range(QUARTERS):
        stream += [*w1[8 * q:8 * q + 8], *blocks(w2[D * q:D * (q + 1)])]
    stream = np.stack(stream)
    assert len(stream) == N_ALL

    conv = np.concatenate([a["ssm_conv_w"][0], a["ssm_conv_b"]], 0)
    conv = conv.T.reshape(12, P, 5)
    conv = np.concatenate([conv[[8 + g, 10 + g, 4 * g, 4 * g + 1, 4 * g + 2, 4 * g + 3]] for g in range(GROUPS)])
    every = lambda v: np.broadcast_to(v.reshape(1, -1), (P, v.size))
    par = np.ascontiguousarray(np.concatenate([
        cols(a["norm_mix_g"][0]), cols(a["norm_mlp_g"][0]), cols(a["final_norm_g"]), cols(a["ssm_norm_g"][0]),
        cols(a["ada_b"][0]), conv.transpose(1, 0, 2).reshape(P, 60), cols(np.repeat(a["ssm_D"][0], HD)),
        cols(a["da_subln_g"][0]), every(a["ssm_dt_bias"][0]), every(a["ssm_A_log"][0]), every(a["sw_sinks"][0].reshape(2, 4).T)], 1))
    lam_v = np.ascontiguousarray(np.concatenate([
        every(a["da_lambda_q1"][0]), every(a["da_lambda_k1"][0]), every(a["da_lambda_q2"][0]), every(a["da_lambda_k2"][0]),
    ], 1))
    con, tab, sw = shape_constants()
    arrays = {
        "x_t": np.ascontiguousarray(a["x"][0].T).reshape(KT, P, T),
        "c_t": np.ascontiguousarray(cols(a["c"][0])),
        "ada_blocks": np.ascontiguousarray(blocks(a["ada_w"][0])),
        "w_stream": stream,
        "params": par,
        "constants": con,
        "da_bias": tab,
        "sw_bias": sw,
        "lambda_vectors": lam_v,
    }
    nc = bacc.Bacc("TRN2", target_bir_lowering=False, num_devices=1)
    aps = [nc.dram_tensor(n, v.shape, F32, kind="ExternalInput").ap() for n, v in arrays.items()]
    out = nc.dram_tensor("out_t", [KT, P, T], F32, kind="ExternalOutput").ap()
    build(nc, *aps, out)
    r = run(nc, [arrays], core_ids=[0])
    got = r.results[0]["out_t"]
    return np.ascontiguousarray(got.reshape(D, T).T)[None]
```
